# Optimizing a Trainium2 kernel written in Bass

```python
import math
import jax, jax.numpy as jnp
from jax import lax
import numpy as np

D_MODEL = 1024
BATCH = 1
SEQ = 256
DEPTH = 2

MEM_LEN = 256
HEAD_DIM = 64
SELF_WIDTH = 3 * D_MODEL // 4
N_MOBA_HEADS = SELF_WIDTH // HEAD_DIM
N_DIFF_HEADS = SELF_WIDTH // (2 * HEAD_DIM)
N_MEM_HEADS = 4
MEM_WIDTH = N_MEM_HEADS * HEAD_DIM
A_IN = 3 * SELF_WIDTH + MEM_WIDTH
B_IN = SELF_WIDTH + MEM_WIDTH
D_FF = 4 * D_MODEL
MOBA_BLOCK = 256
MOBA_TOPK = 3
Q_BLOCK = 128
MOBA_Q_CHUNK = 32
ROPE_THETA = 10000.0
EPS = 1e-6
NEG = -1e30
N_A_LAYERS = DEPTH // 2
N_B_LAYERS = DEPTH - N_A_LAYERS


def _rmsnorm(x, g):
    xf = x.astype(jnp.float32)
    y = xf * lax.rsqrt(jnp.mean(xf * xf, axis=-1, keepdims=True) + EPS)
    return (y * g.astype(jnp.float32)).astype(x.dtype)

def _rope_tables(n):
    half = HEAD_DIM // 2
    inv = 1.0 / (ROPE_THETA ** (jnp.arange(half, dtype=jnp.float32) / half))
    ang = jnp.arange(n, dtype=jnp.float32)[:, None] * inv[None, :]
    return jnp.cos(ang), jnp.sin(ang)

def _apply_rope(x, cos, sin):
    half = HEAD_DIM // 2
    shp = (x.shape[1],) + (1,) * (x.ndim - 3) + (half,)
    c = cos.reshape(shp)
    s = sin.reshape(shp)
    xf = x.astype(jnp.float32)
    x1, x2 = xf[..., :half], xf[..., half:]
    return jnp.concatenate([x1 * c - x2 * s, x2 * c + x1 * s], axis=-1).astype(x.dtype)

def _sq_relu_mlp(h, w_up, w_down):
    u = jax.nn.relu(h @ w_up)
    return (u * u) @ w_down

def _memory_attention(qm, mem, mem_norm, w_mem_kv):
    B, S = qm.shape[:2]
    M = mem.shape[1]
    kv = _rmsnorm(mem, mem_norm) @ w_mem_kv
    mk = kv[..., :MEM_WIDTH].reshape(B, M, N_MEM_HEADS, HEAD_DIM).astype(jnp.float32)
    mv = kv[..., MEM_WIDTH:].reshape(B, M, N_MEM_HEADS, HEAD_DIM).astype(jnp.float32)
    s = jnp.einsum('bshd,bmhd->bhsm', qm.astype(jnp.float32), mk) * (HEAD_DIM ** -0.5)
    p = jax.nn.softmax(s, axis=-1)
    o = jnp.einsum('bhsm,bmhd->bshd', p, mv)
    return o.reshape(B, S, MEM_WIDTH).astype(qm.dtype)

def _diff_attention(q, k, v, lam, lam_init, subln):
    B, S, H, _, d = q.shape
    nq = S // Q_BLOCK
    kf = k.astype(jnp.float32)
    vf = v.astype(jnp.float32)
    qb = q.astype(jnp.float32).reshape(B, nq, Q_BLOCK, H, 2, d).transpose(1, 0, 2, 3, 4, 5)
    kpos = jnp.arange(S)
    scale = d ** -0.5

    def block(args):
        qi, i = args
        s = jnp.einsum('bqhcd,bkhcd->bhcqk', qi, kf) * scale
        qpos = i * Q_BLOCK + jnp.arange(Q_BLOCK)
        s = jnp.where(kpos[None, :] <= qpos[:, None], s, NEG)
        p = jax.nn.softmax(s, axis=-1)
        w = p[:, :, 0] - lam * p[:, :, 1]
        return jnp.einsum('bhqk,bkhe->bqhe', w, vf)

    o = lax.map(block, (qb, jnp.arange(nq)))
    o = o.transpose(1, 0, 2, 3, 4).reshape(B, S, H, 2 * d)
    o = _rmsnorm(o, subln) * (1.0 - lam_init)
    return o.reshape(B, S, H * 2 * d).astype(v.dtype)

def _moba_attention(q, kbh, vbh, kmean):
    B, S, H, d = q.shape
    NB = kbh.shape[2]
    ksel = min(MOBA_TOPK, NB)
    C = MOBA_Q_CHUNK
    nc = S // C
    qc = q.astype(jnp.float32).transpose(0, 2, 1, 3).reshape(B, H, nc, C, d).transpose(2, 0, 1, 3, 4)
    b_ix = jnp.arange(B)[:, None, None, None]
    h_ix = jnp.arange(H)[None, :, None, None]
    scale = d ** -0.5

    def chunk(args):
        qi, i = args
        qpos = i * C + jnp.arange(C)
        cur = (i * C) // MOBA_BLOCK
        gate = jnp.einsum('bhqd,bhnd->bhqn', qi, kmean)
        gate = jnp.where(jnp.arange(NB) < cur, gate, NEG)
        _, idx = lax.top_k(gate, ksel)
        valid = idx < cur
        k_sel = kbh[b_ix, h_ix, idx]
        v_sel = vbh[b_ix, h_ix, idx]
        s_sel = jnp.einsum('bhqd,bhqnkd->bhqnk', qi, k_sel) * scale
        s_sel = jnp.where(valid[..., None], s_sel, NEG).reshape(B, H, C, ksel * MOBA_BLOCK)
        k_own = lax.dynamic_index_in_dim(kbh, cur, axis=2, keepdims=False)
        v_own = lax.dynamic_index_in_dim(vbh, cur, axis=2, keepdims=False)
        s_own = jnp.einsum('bhqd,bhkd->bhqk', qi, k_own) * scale
        kpos = cur * MOBA_BLOCK + jnp.arange(MOBA_BLOCK)
        s_own = jnp.where(kpos[None, :] <= qpos[:, None], s_own, NEG)
        p = jax.nn.softmax(jnp.concatenate([s_sel, s_own], axis=-1), axis=-1)
        p_sel = p[..., :ksel * MOBA_BLOCK].reshape(B, H, C, ksel, MOBA_BLOCK)
        p_own = p[..., ksel * MOBA_BLOCK:]
        return (jnp.einsum('bhqnk,bhqnkd->bhqd', p_sel, v_sel)
                + jnp.einsum('bhqk,bhkd->bhqd', p_own, v_own))

    o = lax.map(chunk, (qc, jnp.arange(nc)))
    return o.transpose(1, 0, 3, 2, 4).reshape(B, S, H * d).astype(q.dtype)

def first_inputs(seed: int = 0) -> dict:
    key = jax.random.key(seed)
    ks = iter(jax.random.split(key, 40))

    def nrm(shape, scale):
        return jax.random.normal(next(ks), shape, jnp.float32) * scale

    def gain(shape):
        return 1.0 + nrm(shape, 0.02)

    NA, NBL, D = N_A_LAYERS, N_B_LAYERS, D_MODEL
    return {
        "x": nrm((BATCH, SEQ, D), 1.0),
        "mem": nrm((BATCH, MEM_LEN, D), 1.0),
        "a_norm_attn": gain((NA, D)),
        "a_w_in": nrm((NA, D, A_IN), D ** -0.5),
        "a_lambda": nrm((NA, 4, HEAD_DIM), 0.1),
        "a_subln": gain((NA, 2 * HEAD_DIM)),
        "a_mem_norm": gain((NA, D)),
        "a_w_mem_kv": nrm((NA, D, 2 * MEM_WIDTH), D ** -0.5),
        "a_w_out": nrm((NA, D, D), D ** -0.5),
        "a_norm_mlp": gain((NA, D)),
        "a_w_up": nrm((NA, D, D_FF), D ** -0.5),
        "a_w_down": nrm((NA, D_FF, D), D_FF ** -0.5),
        "kv_norm": gain((D,)),
        "w_kv": nrm((D, 2 * SELF_WIDTH), D ** -0.5),
        "b_norm_attn": gain((NBL, D)),
        "b_w_in": nrm((NBL, D, B_IN), D ** -0.5),
        "b_mem_norm": gain((NBL, D)),
        "b_w_mem_kv": nrm((NBL, D, 2 * MEM_WIDTH), D ** -0.5),
        "b_w_out": nrm((NBL, D, D), D ** -0.5),
        "b_norm_mlp": gain((NBL, D)),
        "b_w_up": nrm((NBL, D, D_FF), D ** -0.5),
        "b_w_down": nrm((NBL, D_FF, D), D_FF ** -0.5),
        "final_norm": gain((D,)),
    }

def first_block(x, mem, a_norm_attn, a_w_in, a_lambda, a_subln, a_mem_norm, a_w_mem_kv,
              a_w_out, a_norm_mlp, a_w_up, a_w_down, kv_norm, w_kv, b_norm_attn, b_w_in,
              b_mem_norm, b_w_mem_kv, b_w_out, b_norm_mlp, b_w_up, b_w_down, final_norm):
    B, S, _ = x.shape
    cos, sin = _rope_tables(S)
    kbh = vbh = kmean = None
    for layer in range(DEPTH):
        if layer < N_A_LAYERS:
            i = layer
            h = _rmsnorm(x, a_norm_attn[i])
            z = h @ a_w_in[i]
            w = SELF_WIDTH
            q = z[..., :w].reshape(B, S, N_DIFF_HEADS, 2, HEAD_DIM)
            k = z[..., w:2 * w].reshape(B, S, N_DIFF_HEADS, 2, HEAD_DIM)
            v = z[..., 2 * w:3 * w].reshape(B, S, N_DIFF_HEADS, 2 * HEAD_DIM)
            qm = z[..., 3 * w:].reshape(B, S, N_MEM_HEADS, HEAD_DIM)
            q = _apply_rope(q, cos, sin)
            k = _apply_rope(k, cos, sin)
            lam_init = 0.8 - 0.6 * math.exp(-0.3 * layer)
            lp = a_lambda[i].astype(jnp.float32)
            lam = jnp.exp(jnp.sum(lp[0] * lp[1])) - jnp.exp(jnp.sum(lp[2] * lp[3])) + lam_init
            o_self = _diff_attention(q, k, v, lam, lam_init, a_subln[i])
            o_mem = _memory_attention(qm, mem, a_mem_norm[i], a_w_mem_kv[i])
            x = x + jnp.concatenate([o_self, o_mem], axis=-1) @ a_w_out[i]
            x = x + _sq_relu_mlp(_rmsnorm(x, a_norm_mlp[i]), a_w_up[i], a_w_down[i])
        else:
            j = layer - N_A_LAYERS
            if j == 0:
                hk = _rmsnorm(x, kv_norm)
                kv = hk @ w_kv
                ks_ = _apply_rope(kv[..., :SELF_WIDTH].reshape(B, S, N_MOBA_HEADS, HEAD_DIM), cos, sin)
                vs_ = kv[..., SELF_WIDTH:].reshape(B, S, N_MOBA_HEADS, HEAD_DIM)
                n_blk = -(-S // MOBA_BLOCK)
                pad = n_blk * MOBA_BLOCK - S
                padw = ((0, 0), (0, pad), (0, 0), (0, 0))
                kbh = jnp.pad(ks_.astype(jnp.float32), padw).reshape(
                    B, n_blk, MOBA_BLOCK, N_MOBA_HEADS, HEAD_DIM).transpose(0, 3, 1, 2, 4)
                vbh = jnp.pad(vs_.astype(jnp.float32), padw).reshape(
                    B, n_blk, MOBA_BLOCK, N_MOBA_HEADS, HEAD_DIM).transpose(0, 3, 1, 2, 4)
                kmean = jnp.mean(kbh, axis=3)
            h = _rmsnorm(x, b_norm_attn[j])
            z = h @ b_w_in[j]
            q = _apply_rope(z[..., :SELF_WIDTH].reshape(B, S, N_MOBA_HEADS, HEAD_DIM), cos, sin)
            qm = z[..., SELF_WIDTH:].reshape(B, S, N_MEM_HEADS, HEAD_DIM)
            o_self = _moba_attention(q, kbh, vbh, kmean).astype(x.dtype)
            o_mem = _memory_attention(qm, mem, b_mem_norm[j], b_w_mem_kv[j])
            x = x + jnp.concatenate([o_self, o_mem], axis=-1) @ b_w_out[j]
            x = x + _sq_relu_mlp(_rmsnorm(x, b_norm_mlp[j]), b_w_up[j], b_w_down[j])
    return _rmsnorm(x, final_norm)


DEPTH_2 = 1

CHUNK = 64
MIX_WIDTH = D_MODEL
A_WIDTH = MIX_WIDTH // 2
B_WIDTH = MIX_WIDTH - A_WIDTH
A_HEADS = A_WIDTH // HEAD_DIM
B_HEADS = B_WIDTH // HEAD_DIM
KV_LATENT = 128
IDX_HEADS = 4
IDX_DIM = 32
TOPK_MAX = 256
NUM_BUCKETS = 32
MAX_DISTANCE = 128
ROPE_BASE = 10000.0
RMS_EPS = 1e-6
GN_EPS = 1e-5
FFN_HIDDEN = ((-(-(8 * D_MODEL) // 3) + 255) // 256) * 256

IN_SIZES = [A_WIDTH, KV_LATENT, IDX_HEADS * IDX_DIM, IDX_DIM, IDX_HEADS,
            B_WIDTH, B_WIDTH, B_WIDTH, B_WIDTH]
IN_WIDTH = sum(IN_SIZES)
IN_OFFSETS = [int(o) for o in np.cumsum(IN_SIZES)[:-1]]


def rmsnorm(x, w):
    xf = x.astype(jnp.float32)
    y = xf * lax.rsqrt(jnp.mean(xf * xf, axis=-1, keepdims=True) + RMS_EPS)
    return (y * w.astype(jnp.float32)).astype(x.dtype)

def t5_bucket(rel):
    half = NUM_BUCKETS // 2
    max_exact = half // 2
    ret = jnp.where(rel > 0, half, 0)
    n = jnp.abs(rel)
    nf = jnp.maximum(n, 1).astype(jnp.float32)
    large = max_exact + (jnp.log(nf / max_exact) / math.log(MAX_DISTANCE / max_exact)
                         * (half - max_exact)).astype(jnp.int32)
    large = jnp.minimum(large, half - 1)
    return ret + jnp.where(n < max_exact, n, large)

def rotary(x, pos):
    half = x.shape[-1] // 2
    inv = ROPE_BASE ** (-jnp.arange(half, dtype=jnp.float32) / half)
    ang = pos.astype(jnp.float32)[:, None] * inv[None, :]
    cos = jnp.cos(ang)[:, None, :]
    sin = jnp.sin(ang)[:, None, :]
    x1, x2 = x[..., :half], x[..., half:]
    return jnp.concatenate([x1 * cos - x2 * sin, x1 * sin + x2 * cos], axis=-1)

def indexed_sparse_attention(q, k, v, iq, ik, iw, rel_bias):
    b, s, h, dh = q.shape
    topk = min(TOPK_MAX, s // 4)
    n_blocks = s // Q_BLOCK
    key_pos = jnp.arange(s)
    idx_scale = IDX_DIM ** -0.5
    w_scale = IDX_HEADS ** -0.5

    def block(i):
        t0 = i * Q_BLOCK
        qb = lax.dynamic_slice_in_dim(q, t0, Q_BLOCK, axis=1)
        iqb = lax.dynamic_slice_in_dim(iq, t0, Q_BLOCK, axis=1)
        iwb = lax.dynamic_slice_in_dim(iw, t0, Q_BLOCK, axis=1)
        qpos = t0 + jnp.arange(Q_BLOCK)
        limit = (qpos // CHUNK + 1) * CHUNK
        admissible = key_pos[None, :] < limit[:, None]
        dots = jnp.einsum('bthd,bsd->bths', iqb, ik).astype(jnp.float32) * idx_scale
        score = jnp.einsum('bth,bths->bts', iwb.astype(jnp.float32) * w_scale,
                           jax.nn.relu(dots))
        score = jnp.where(admissible[None], score, -jnp.inf)
        _, idx = lax.top_k(score, topk)
        valid = idx < limit[None, :, None]
        kg = jax.vmap(lambda kb, ib: kb[ib])(k, idx)
        vg = jax.vmap(lambda vb, ib: vb[ib])(v, idx)
        logits = jnp.einsum('bthd,btkd->bhtk', qb, kg).astype(jnp.float32) * dh ** -0.5
        bias = rel_bias[t5_bucket(idx - qpos[None, :, None])]
        logits = logits + jnp.transpose(bias, (0, 3, 1, 2)).astype(jnp.float32)
        logits = jnp.where(valid[:, None], logits, -jnp.inf)
        p = jax.nn.softmax(logits, axis=-1)
        return jnp.einsum('bhtk,btkd->bthd', p.astype(v.dtype), vg)

    outs = lax.map(block, jnp.arange(n_blocks))
    return jnp.moveaxis(outs, 0, 1).reshape(b, s, h * dh)

def chunkwise_retention(q, k, v):
    b, s, h, dh = q.shape
    nc = s // CHUNK
    log_g = jnp.log1p(-(2.0 ** (-5.0 - jnp.arange(h, dtype=jnp.float32))))
    j = jnp.arange(CHUNK, dtype=jnp.float32)
    rel = j[:, None] - j[None, :]
    inner_decay = jnp.where(rel[None] >= 0,
                            jnp.exp(jnp.maximum(rel, 0.0)[None] * log_g[:, None, None]), 0.0)
    query_decay = jnp.exp((j + 1.0)[:, None] * log_g[None, :])[None, :, :, None]
    key_decay = jnp.exp((CHUNK - 1.0 - j)[:, None] * log_g[None, :])[None, :, :, None]
    chunk_decay = jnp.exp(CHUNK * log_g)[None, :, None, None]

    def to_chunks(t):
        return jnp.transpose(t.reshape(b, nc, CHUNK, h, dh), (1, 0, 2, 3, 4))

    def step(state, xs):
        qc, kc, vc = xs
        scores = jnp.einsum('bihd,bjhd->bhij', qc, kc) * inner_decay[None]
        inner = jnp.einsum('bhij,bjhd->bihd', scores, vc)
        cross = jnp.einsum('bihd,bhde->bihe', qc, state) * query_decay
        new_state = state * chunk_decay + jnp.einsum('bjhd,bjhe->bhde', kc * key_decay, vc)
        return new_state, inner + cross

    state0 = jnp.zeros((b, h, dh, dh), jnp.float32)
    _, ys = lax.scan(step, state0, (to_chunks(q), to_chunks(k), to_chunks(v)))
    return jnp.transpose(ys, (1, 0, 2, 3, 4)).reshape(b, s, h, dh)

def second_inputs(seed: int = 0) -> dict:
    key = jax.random.key(seed)
    ks = jax.random.split(key, 20)
    f32 = jnp.float32

    def nrm(k, shape, fan_in):
        return jax.random.normal(k, shape, f32) * fan_in ** -0.5

    def gain(k, shape):
        return 1.0 + 0.02 * jax.random.normal(k, shape, f32)

    return {
        "x": jax.random.normal(ks[0], (BATCH, SEQ, D_MODEL), f32),
        "norm1_w": gain(ks[1], (DEPTH_2, D_MODEL)),
        "w_in": nrm(ks[2], (DEPTH_2, D_MODEL, IN_WIDTH), D_MODEL),
        "q_norm_w": gain(ks[3], (DEPTH_2, HEAD_DIM)),
        "k_norm_w": gain(ks[4], (DEPTH_2, HEAD_DIM)),
        "kv_norm_w": gain(ks[5], (DEPTH_2, KV_LATENT)),
        "w_uk": nrm(ks[6], (DEPTH_2, KV_LATENT, HEAD_DIM), KV_LATENT),
        "w_uv": nrm(ks[7], (DEPTH_2, KV_LATENT, HEAD_DIM), KV_LATENT),
        "rel_bias": 0.1 * jax.random.normal(ks[8], (NUM_BUCKETS, A_HEADS), f32),
        "ret_gn_w": gain(ks[9], (DEPTH_2, B_WIDTH)),
        "ret_gn_b": 0.02 * jax.random.normal(ks[10], (DEPTH_2, B_WIDTH), f32),
        "w_out": nrm(ks[11], (DEPTH_2, MIX_WIDTH, D_MODEL), MIX_WIDTH),
        "norm2_w": gain(ks[12], (DEPTH_2, D_MODEL)),
        "w_gate": nrm(ks[13], (DEPTH_2, D_MODEL, FFN_HIDDEN), D_MODEL),
        "w_up": nrm(ks[14], (DEPTH_2, D_MODEL, FFN_HIDDEN), D_MODEL),
        "w_down": nrm(ks[15], (DEPTH_2, FFN_HIDDEN, D_MODEL), FFN_HIDDEN),
    }

def second_block(x, norm1_w, w_in, q_norm_w, k_norm_w, kv_norm_w, w_uk, w_uv, rel_bias,
              ret_gn_w, ret_gn_b, w_out, norm2_w, w_gate, w_up, w_down):
    b, s, _ = x.shape
    pos = jnp.arange(s)
    for l in range(DEPTH_2):
        h = rmsnorm(x, norm1_w[l])
        z = h @ w_in[l]
        qa, c_kv, iq, ik, iw, qb, kb, vb, gb = jnp.split(z, IN_OFFSETS, axis=-1)

        qa = rmsnorm(qa.reshape(b, s, A_HEADS, HEAD_DIM), q_norm_w[l])
        c = rmsnorm(c_kv, kv_norm_w[l])
        ka = rmsnorm(c @ w_uk[l], k_norm_w[l])
        va = c @ w_uv[l]
        out_a = indexed_sparse_attention(qa, ka, va,
                                         iq.reshape(b, s, IDX_HEADS, IDX_DIM), ik, iw, rel_bias)

        qr = rotary(qb.reshape(b, s, B_HEADS, HEAD_DIM).astype(jnp.float32), pos)
        kr = rotary(kb.reshape(b, s, B_HEADS, HEAD_DIM).astype(jnp.float32), pos) * HEAD_DIM ** -0.5
        vr = vb.reshape(b, s, B_HEADS, HEAD_DIM).astype(jnp.float32)
        y = chunkwise_retention(qr, kr, vr)
        mu = jnp.mean(y, axis=-1, keepdims=True)
        var = jnp.mean(jnp.square(y - mu), axis=-1, keepdims=True)
        y = ((y - mu) * lax.rsqrt(var + GN_EPS)).reshape(b, s, B_WIDTH)
        y = y * ret_gn_w[l].astype(jnp.float32) + ret_gn_b[l].astype(jnp.float32)
        out_b = (jax.nn.silu(gb.astype(jnp.float32)) * y).astype(x.dtype)

        x = x + jnp.concatenate([out_a, out_b], axis=-1) @ w_out[l]

        h2 = rmsnorm(x, norm2_w[l])
        x = x + (jax.nn.silu(h2 @ w_gate[l]) * (h2 @ w_up[l])) @ w_down[l]
    return x


def setup_inputs(seed=0):
    out = dict(first_inputs(seed))
    for name, value in second_inputs(seed + 1).items():
        if name != "x":
            out[name + "_2"] = value
    return out


def reference(
    x, mem, a_norm_attn, a_w_in, a_lambda, a_subln, a_mem_norm, a_w_mem_kv, a_w_out, a_norm_mlp,
    a_w_up, a_w_down, kv_norm, w_kv, b_norm_attn, b_w_in, b_mem_norm, b_w_mem_kv, b_w_out,
    b_norm_mlp, b_w_up, b_w_down, final_norm, norm1_w_2, w_in_2, q_norm_w_2, k_norm_w_2,
    kv_norm_w_2, w_uk_2, w_uv_2, rel_bias_2, ret_gn_w_2, ret_gn_b_2, w_out_2, norm2_w_2,
    w_gate_2, w_up_2, w_down_2,
):
    x = first_block(
        x, mem, a_norm_attn, a_w_in, a_lambda, a_subln, a_mem_norm, a_w_mem_kv, a_w_out,
        a_norm_mlp, a_w_up, a_w_down, kv_norm, w_kv, b_norm_attn, b_w_in, b_mem_norm,
        b_w_mem_kv, b_w_out, b_norm_mlp, b_w_up, b_w_down, final_norm,
    )
    return second_block(
        x, norm1_w_2, w_in_2, q_norm_w_2, k_norm_w_2, kv_norm_w_2, w_uk_2, w_uv_2, rel_bias_2,
        ret_gn_w_2, ret_gn_b_2, w_out_2, norm2_w_2, w_gate_2, w_up_2, w_down_2,
    )


_drawn_inputs = setup_inputs


def setup_inputs(seed=0):
    import zlib

    import numpy as np

    out = dict(_drawn_inputs(seed))
    spreads = {}
    factors = {'a_lambda': 3.282,
     'a_mem_norm': 8.0,
     'kv_norm': 4.868,
     'b_norm_attn': 8.0,
     'b_mem_norm': 8.0,
     'q_norm_w_2': 8.0,
     'k_norm_w_2': 8.0,
     'kv_norm_w_2': 6.984,
     'rel_bias_2': 5.981,
     'ret_gn_w_2': 7.887,
     'ret_gn_b_2': 6.938,
     'norm2_w_2': 4.229}
    for name, (base, spread) in spreads.items():
        noise = np.random.default_rng([zlib.crc32(name.encode()), seed]).standard_normal(out[name].shape)
        drawn = base * np.exp(spread * noise) if base else spread * noise
        out[name] = __import__('jax').numpy.asarray(drawn.astype(out[name].dtype))
    for name, factor in factors.items():
        out[name] = (out[name] * factor).astype(out[name].dtype)
    return out
```

```python
from contextlib import ExitStack
import math

import numpy as np
import concourse.bass as bass
from concourse import mybir

F32 = mybir.dt.float32
F32R = mybir.dt.float32r
BF16 = mybir.dt.bfloat16
ACT = mybir.ActivationFunctionType
ALU = mybir.AluOpType
AX_X = mybir.AxisListType.X

P = 128
TOK = 256
NT = TOK // P
D = 1024
KT = D // P
DH = 64
COLS = 512
UK = 4
RING = 4
FRING = 3
AHEAD = 3
SELF = 768
DFF = 4096
CHUNKS = DFF // COLS
FFN = 2816
FCHUNK = 256
FCHUNKS = FFN // FCHUNK
EPS = 1e-6
GN_EPS = 1e-5
NEG = -1e30
BELOW = -3.0e38
TAKEN = -3.4e38
TOPK = 64
CONSTS = 16 * 12
STATS = 340
Q_QB, Q_KA, Q_IK, Q_C = 16, 20, 21, 22
MAX8 = 8
LAM_INIT = 0.8 - 0.6 * math.exp(-0.3 * 0)
SCALE = DH ** -0.5
IDX_SCALE = 32 ** -0.5
IDX_W_SCALE = 4 ** -0.5
SMALL = 292

GAINS = ["a_mem_norm", "b_mem_norm", "a_norm_attn", "a_norm_mlp", "kv_norm", "b_norm_attn",
         "b_norm_mlp", "norm1_w_2", "final_norm", "norm2_w_2"]


def shape_tables():
    half = DH // 2
    pos = np.arange(TOK, dtype=np.float32)[:, None]
    a = np.arange(half, dtype=np.float32)
    ten = np.float32(10000.0)
    out = {}
    for name, inv in (("rope1", np.float32(1) / ten ** (a / np.float32(half))),
                      ("rope2", ten ** (-a / np.float32(half)))):
        ang = (pos * inv[None, :].astype(np.float32)).astype(np.float32)
        c, s = np.cos(ang), np.sin(ang)
        out[name] = np.concatenate([c, c, -s, s], axis=1).astype(np.float32)
    rel = np.arange(512) - 255
    n = np.abs(rel)
    nf = np.maximum(n, 1).astype(np.float32)
    large = 8 + (np.log(nf / np.float32(8)) / np.float32(math.log(16)) * np.float32(8)).astype(np.int32)
    bucket = np.where(rel > 0, 16, 0) + np.where(n < 8, n, np.minimum(large, 15))
    out["bucket_onehot"] = (np.arange(32)[:, None] == bucket[None, :]).astype(np.float32)
    log_g = np.log1p(-(2.0 ** (-5.0 - np.arange(8.0))))
    t = np.arange(TOK, dtype=np.float64)[:, None]
    out["decays"] = np.concatenate([np.exp(t * log_g), np.exp(-t * log_g) * SCALE], axis=1).astype(np.float32)
    return out


class Step:
    pass


def build(nc, A, out):
    UNITS = []

    def unit(w, rows, cols, nk=UK):
        n = sum(c for _, c in cols)
        view = lambda r, k, c0, c: w[r:r + P * k, c0:c0 + c].rearrange("(k p) n -> p k n", p=P)
        if len(cols) == 1:
            h = nk // 2
            parts = [(view(rows + P * h * i, h, cols[0][0], n), slice(h * i, h * i + h), slice(0, n))
                     for i in range(2)]
        else:
            at, parts = 0, []
            for c0, c in cols:
                parts.append((view(rows, nk, c0, c), slice(0, nk), slice(at, at + c)))
                at += c
        un = Step()
        un.n, un.nk, un.parts = n, nk, parts
        UNITS.append(un)
        return len(UNITS) - 1

    def chunk_units(w, cols):
        return [unit(w, h * UK * P, cols) for h in range(2)]

    STEPS = []
    count = Step()
    count.t, count.hi, count.chunk, count.s, count.o, count.item, count.resid = 0, 0, 0, 0, 0, 0, 0
    count.rstd, count.rope, count.exp, count.relu2, count.osq, count.ss = 0, 0, 0, 0, 0, 0
    count.decayed, count.w, count.dots = 0, 0, 0
    free = {}

    def add(kind):
        st = Step()
        st.kind = kind
        STEPS.append(st)
        return st

    ctx = ExitStack()
    with ctx:
        def sb(name, shape, dt=F32):
            return ctx.enter_context(nc.sbuf_tensor(name, shape, dt))

        def sem(name):
            return ctx.enter_context(nc.semaphore(name))

        raw = sb("raw", [P, RING, UK * COLS])
        whi = sb("whi", [P, RING, UK * COLS], F32R)
        wlo = sb("wlo", [P, RING, UK * COLS], F32R)
        x = sb("x", [P, NT, D])
        set_hi = [sb(f"set{i}_hi", [P, KT, TOK], F32R) for i in range(2)]
        set_lo = [sb(f"set{i}_lo", [P, KT, TOK], F32R) for i in range(2)]
        o_nat = sb("o_nat", [P, NT, D])
        zq = sb("zq", [P, 2, NT, COLS])
        rt = sb("rope_tmp", [P, 2, COLS])
        qk = sb("qk", [P, 24, TOK])
        v = sb("v", [P, NT, SELF])
        e = sb("e", [P, 2, COLS])
        wT = sb("wT", [P, 2, COLS])
        memkv = sb("memkv", [P, 2, COLS])
        rope1 = sb("rope1_sb", [P, NT, 4 * 32])
        rope2 = sb("rope2_sb", [P, NT, 4 * 32])
        ident = sb("ident", [P, P])
        identb = sb("identb", [P, P], BF16)
        cmask = sb("cmask", [P, P], BF16)
        flip = sb("flip", [P, P])
        tri = sb("tri", [P, P])
        gcol = sb("gcol", [P, len(GAINS) * KT])
        subln = sb("subln", [P, P])
        kvn = sb("kvn", [P, P])
        qkn = sb("qkn", [P, 2, DH])
        wukv = sb("wukv", [P, 2, DH])
        dec = sb("dec", [P, NT, 16])
        selmask = sb("selmask", [P, NT, TOK], BF16)
        stat = sb("stat", [P, STATS])
        newton = sb("newton", [P, 2, 8])
        epsc = sb("epsc", [P, 2])
        junk1 = sb("junk1", [P, P], BF16)
        rel8 = sb("rel8", [32, 8])
        mem_nat = o_nat
        hidden = zq[:, 0, :, :]
        zs = o_nat[:, 0, 0:2 * SMALL].rearrange("p (t n) -> p t n", t=2)
        sn = o_nat[:, 1, 0:768].rearrange("p (t b n) -> p t b n", t=2, b=3)
        relu_dots = wT[:, :, :].rearrange("p a b -> p (a b)").rearrange("p (h n) -> p h n", h=4)
        score = e[:, 0, 0:TOK]
        work = [e[:, 0, TOK:2 * TOK], e[:, 1, 0:TOK]]
        btoep = memkv[:, :, :].rearrange("p a b -> p (a b)").rearrange("p (h n) -> p h n", h=4)
        fgb = qk[:, 16:20, :].rearrange("p a b -> p (a b)")
        gn = zq[:, 0, :, :]
        junk = wT[:, :, :].rearrange("p a b -> p (a b)").bitcast(BF16).rearrange("p (t n) -> p t n", t=NT)
        lamrow = rt[:, 0, 0:256].rearrange("p (a b d) -> p a b d", a=2, b=2)
        lamprod = rt[:, 0, 256:384].rearrange("p (a d) -> p a d", a=2)
        onehot = e[0:32, 0, :]
        biasvec = e[0:8, 1, :]
        grow = qk[0:len(GAINS) * KT, 23, 0:P]
        headq = qk[:, 0:16, :].rearrange("p (b c) n -> p b c n", c=2)

        ncol = [0]

        def col(n):
            ncol[0] += n
            assert ncol[0] <= STATS, ncol
            return stat[:, ncol[0] - n:ncol[0]]

        pb = lambda n: ctx.enter_context(nc.psum_tensor(n, [P, COLS], F32))
        Pb = [pb(f"proj{i}") for i in range(2)]
        Tb = [pb(f"turn{i}") for i in range(2)]
        Sb = [pb(f"score{i}") for i in range(2)]
        Ob = [pb(f"outp{i}") for i in range(2)]
        for i in range(2):
            for b in "PTSO":
                free[b, i] = None

        landed = [sem(f"unit_landed{i}") for i in range(RING)]
        hi_done = sem("hi_done")
        lo_done = sem("lo_done")
        mul_done = sem("mul_done")
        t_full = sem("t_full")
        t_hi = sem("t_hi")
        t_evac = sem("t_evac")
        chunk_evac = sem("chunk_evac")
        rope_done = sem("rope_done")
        s_full = sem("s_full")
        nmax_done = sem("nmax_done")
        exp_done = sem("exp_done")
        w_done = sem("w_done")
        o_full = sem("o_full")
        osq_done = sem("osq_done")
        o_evac = sem("o_evac")
        resid_done = sem("resid_done")
        ss_done = sem("ss_done")
        rstd_done = sem("rstd_done")
        relu_done = sem("relu_done")
        relu2_done = sem("relu2_done")
        silu_done = sem("silu_done")
        dots_done = sem("dots_done")
        dots_used = sem("dots_used")
        sel_done = sem("sel_done")
        kava_done = sem("kava_done")
        ka_done = sem("ka_done")
        sn_done = sem("sn_done")
        qn_done = sem("qn_done")
        qsq_done = sem("qsq_done")
        decayed = sem("decayed")
        yc_done = sem("yc_done")
        ysq_done = sem("ysq_done")
        yn_done = sem("yn_done")
        ob_done = sem("ob_done")
        sum_done = sem("sum_done")
        guess_done = sem("guess_done")
        act_chain = sem("act_chain")
        dve_chain = sem("dve_chain")
        pool_chain = sem("pool_chain")
        heads_zeroed = sem("heads_zeroed")
        consts_made = sem("consts_made")
        mem_landed, x_landed, consts_landed = sem("mem_landed"), sem("x_landed"), sem("consts_landed")
        gain_full, gain_cols = sem("gain_full"), sem("gain_cols")
        lam_sum, lam_exp, lam_done = sem("lam_sum"), sem("lam_exp"), sem("lam_done")
        gains_landed, gn_landed = sem("gains_landed"), sem("gn_landed")
        bias_full, bias_vec, bias_stored = sem("bias_full"), sem("bias_vec"), sem("bias_stored")
        late_landed = sem("late_landed")
        stored = sem("stored")

        bias_dram = nc.dram_tensor("bias_by_distance", (8, 512), F32, kind="Internal").ap()

        def t_use():
            n = count.t
            count.t += 1
            return n

        def turn_operand(src, half, gains, ready, set_free, cols=None):
            st = add("turn_operand")
            st.src, st.half, st.gains, st.ready, st.set_free = src, half, gains, ready, set_free
            st.use, st.hi = [t_use(), t_use()], count.hi
            count.hi += 2
            return st.use

        def multiply(u, lhs, k0, use, bank, start, stop):
            st = add("multiply")
            st.u, st.lhs, st.k0, st.use, st.bank, st.start = u, lhs, k0, use, bank, start
            st.stop, st.freed = stop, [free[bank, t] for t in range(NT)] if start else None
            return st

        def evacuate(u, pieces, scale, slot=None, slot_free=None, silu=False):
            st = add("evacuate")
            st.u, st.pieces, st.scale, st.chunk = u, pieces, scale, count.chunk
            st.slot_free, st.silu = slot_free, silu
            for t in range(NT):
                free["P", t] = (chunk_evac, 2 * count.chunk + t + 1)
            count.chunk += 1
            return st

        def rope(slot, n, table):
            st = add("rope")
            st.slot, st.n, st.table, st.chunk, st.rope = slot, n, table, count.chunk, count.rope
            count.rope += 1
            return st

        def turn_heads(src, blocks, pieces, ready):
            st = add("turn_heads")
            st.src, st.blocks, st.pieces, st.ready = src, blocks, pieces, ready
            st.use = [t_use(), t_use()]
            return st.use

        LOW, HIGH, ALL = slice(0, DH), slice(DH, P), slice(0, P)
        tok = lambda t: slice(t * P, (t + 1) * P)

        def pairs(a, first, n):
            return [(ALL, slice(a, a + n), lambda t: qk[:, first:first + n, tok(t)])]

        def heads(a, first, n):
            return [(LOW, slice(a, a + n), lambda t: headq[LOW, first:first + n, 0, tok(t)]),
                    (HIGH, slice(a, a + n), lambda t: headq[HIGH, first:first + n, 1, tok(t)])]

        def s_use(release):
            n = count.s
            count.s += 1
            f = free["S", n % 2]
            free["S", n % 2] = release
            return n, f

        def o_use():
            n = count.o
            count.o += 1
            f = free["O", n % 2]
            free["O", n % 2] = (o_evac, n + 1)
            return n, f

        ITEMS = []

        def scores(kind, pair, t, q, k, need):
            it = Step()
            it.kind, it.pair, it.t, it.q, it.k, it.need = kind, pair, t, q, k, need
            it.n, it.buf, it.i, it.nm = P * (t + 1), len(ITEMS) % 2, len(ITEMS), col(2)
            it.rs, it.before = col(2), ITEMS[-2] if len(ITEMS) > 1 else None
            if kind == "mem":
                it.n = TOK
            if kind == "diff":
                it.oss, it.ors = col(1), col(1)
            it.exp = count.exp
            count.exp += 1
            it.s, it.s_free = s_use((exp_done, it.exp + 1))
            ITEMS.append(it)
            st = add("scores")
            st.it = it
            return it

        def mix(it):
            count.w += 1
            it.w = count.w
            st = add("mix")
            st.it = it

        def turn_weights(it):
            it.use = t_use()
            st = add("turn_weights")
            st.it = it

        def attend(it, vneed):
            it.o, it.o_free = o_use()
            it.vneed = vneed
            if it.kind == "diff":
                count.osq += 1
                it.osq = count.osq
            st = add("attend")
            st.it = it
            return it.o + 1

        def residual(half, bank, u, scale):
            st = add("residual")
            st.half, st.bank, st.u, st.scale, st.r = half, bank, u, scale, count.resid
            count.resid += 2
            for t in range(NT):
                free[bank, t] = (resid_done, st.r + t + 1)
            return st

        def statistics(src, ready, factor=None, kind="plain"):
            st = add("statistics")
            st.src, st.ready, st.n, st.ss, st.rs = src, ready, count.rstd, col(2), col(2)
            st.what, st.factor = kind, factor
            if kind == "final":
                st.ss2, st.r2 = col(2), col(2)
            st.sums = count.ss
            count.ss += 2 if kind == "final" else 1
            count.rstd += 2 if kind == "final" else 1
            st.n_done = count.rstd
            return st

        g_at = lambda name: GAINS.index(name) * KT

        zfree = [None, None]
        bias_s = s_use((bias_vec, 1))
        gain_s = s_use((gain_cols, 1))
        st = add("setup")
        st.lam = col(5)
        memA = chunk_units(A["a_w_mem_kv"][0], [(0, 512)])
        w = A["a_w_in"][0]
        vm = chunk_units(w, [(2 * SELF + 512, 512)])
        qk0 = chunk_units(w, [(0, 256), (SELF, 256)])
        v0 = chunk_units(w, [(2 * SELF, 512)])
        qk1 = chunk_units(w, [(256, 256), (SELF + 256, 256)])
        qk2 = chunk_units(w, [(512, 256), (SELF + 512, 256)])

        def out_units(w):
            a = unit(w, 0, [(0, 512)])
            b = unit(w, 512, [(0, 512)])
            c = unit(w, 0, [(512, 512)])
            d = unit(w, 512, [(512, 512)])
            return a, b, c, d

        def mul_chunk_half(us, h, lhs, uses):
            multiply(us[h], lhs, UK * h, uses[h], "P", h == 0, h == 1)

        rs_mem = statistics(mem_nat, (mem_landed, 16))
        m1 = [turn_operand(mem_nat, h, [(g_at("a_mem_norm"), 1, UK * h)], (mem_landed, 16), None)[-1] for h in range(2)]
        rs_x = statistics(x, (x_landed, 16))
        x1 = [turn_operand(x, h, [(g_at("a_norm_attn"), 0, UK * h)], (x_landed, 16), None)[-1] for h in range(2)]
        mul_chunk_half(memA, 0, 1, m1)
        mul_chunk_half(memA, 1, 1, m1)

        def mem_pieces(slot):
            return [((0, 256), lambda t: zq[:, slot, t, 0:256]),
                    ((256, 512), lambda t: memkv[:, 1, t * 256:t * 256 + 256])]

        mk = memkv[:, 0, :].rearrange("p (b n) -> p b n", b=2)
        mem_keys = [(ALL, slice(0, 2), lambda t: mk[:, :, tok(t)])]

        def chunk_ready(ch):
            return lambda t: (chunk_evac, 2 * ch + t + 1)

        def rope_ready(r):
            return lambda t: (rope_done, 2 * r + t + 1)

        ev = evacuate(memA[1], mem_pieces(0), rs_mem, slot_free=None)
        mul_chunk_half(vm, 0, 0, x1)
        u = turn_heads(zq[:, 0], [0, 1], mem_keys, chunk_ready(ev.chunk))
        mkA = u[-1]
        zfree[0] = u[-1] + 1
        mB = [turn_operand(mem_nat, h, [(g_at("b_mem_norm"), 1, UK * h)], (mem_landed, 16), 2 * memA[1] + 2)[-1]
              for h in range(2)]
        mul_chunk_half(vm, 1, 0, x1)
        ev = evacuate(vm[1], [((0, 256), lambda t: v[:, t, 512:768]), ((256, 512), lambda t: zq[:, 1, t, 0:256])],
                      rs_x)
        vA2 = ev.chunk
        mul_chunk_half(qk0, 0, 0, x1)
        u = turn_heads(zq[:, 1], [0, 1], heads(0, 6, 2), chunk_ready(ev.chunk))
        qm_use, zfree[1] = u[-1], u[-1] + 1
        qk_pieces = lambda a: heads(0, a, 2) + pairs(2, 16 + a, 2)
        mul_chunk_half(qk0, 1, 0, x1)
        evacuate(qk0[1], [((0, 512), lambda t: zq[:, 0, t, :])], rs_x, slot_free=zfree[0])
        r0 = rope(0, 512, rope1)

        def mem_item(p, t, qneed, kneed):
            return scores("mem", p, t, 6 + p, mk[:, p, :], max(qneed, kneed))

        m = [mem_item(0, 0, qm_use, mkA), mem_item(0, 1, qm_use, mkA)]
        mul_chunk_half(v0, 0, 0, x1)
        mix(m[0]); mix(m[1]); turn_weights(m[0]); turn_weights(m[1])
        m += [mem_item(1, 0, qm_use, mkA), mem_item(1, 1, qm_use, mkA)]
        h_use = [turn_heads(zq[:, 0], [0, 1, 2, 3], qk_pieces(0), rope_ready(r0.rope))[-1]]
        zfree[0] = h_use[0] + 1
        mul_chunk_half(v0, 1, 0, x1)
        ev = evacuate(v0[1], [((0, 512), lambda t: v[:, t, 0:512])], rs_x)
        vA = max(vA2, ev.chunk)
        memV = (chunk_evac, 2)
        mix(m[2]); mix(m[3]); attend(m[0], memV); attend(m[1], memV); turn_weights(m[2]); turn_weights(m[3])

        def diff_item(h, t):
            return scores("diff", h, t, h, qk[:, 16 + h, :], h_use[h // 2])

        d = [diff_item(0, 0), diff_item(0, 1)]
        mul_chunk_half(qk1, 0, 0, x1)
        vneed = (chunk_evac, 2 * vA + 2)
        mix(d[0]); mix(d[1]); attend(m[2], memV); attend(m[3], memV); turn_weights(d[0]); turn_weights(d[1])
        d += [diff_item(1, 0), diff_item(1, 1)]
        mul_chunk_half(qk1, 1, 0, x1)
        evacuate(qk1[1], [((0, 512), lambda t: zq[:, 1, t, :])], rs_x, slot_free=zfree[1])
        r1 = rope(1, 512, rope1)
        mix(d[2]); mix(d[3]); attend(d[0], vneed); attend(d[1], vneed); turn_weights(d[2]); turn_weights(d[3])
        mul_chunk_half(qk2, 0, 0, x1)
        h_use.append(turn_heads(zq[:, 1], [0, 1, 2, 3], qk_pieces(2), rope_ready(r1.rope))[-1])
        zfree[1] = h_use[1] + 1
        attend(d[2], vneed); attend(d[3], vneed)
        d += [diff_item(2, 0), diff_item(2, 1)]
        mul_chunk_half(qk2, 1, 0, x1)
        evacuate(qk2[1], [((0, 512), lambda t: zq[:, 0, t, :])], rs_x, slot_free=zfree[0])
        r2 = rope(0, 512, rope1)
        mix(d[4]); mix(d[5]); turn_weights(d[4]); turn_weights(d[5])
        d += [diff_item(3, 0), diff_item(3, 1)]
        memB = chunk_units(A["b_w_mem_kv"][0], [(0, 512)])
        mul_chunk_half(memB, 0, 1, mB)
        h_use.append(turn_heads(zq[:, 0], [0, 1, 2, 3], qk_pieces(4), rope_ready(r2.rope))[-1])
        zfree[0] = h_use[2] + 1
        mix(d[6]); mix(d[7]); attend(d[4], vneed); attend(d[5], vneed); turn_weights(d[6]); turn_weights(d[7])
        d += [diff_item(4, 0), diff_item(4, 1)]
        mul_chunk_half(memB, 1, 1, mB)
        ev = evacuate(memB[1], mem_pieces(1), rs_mem, slot_free=zfree[1])
        memB_chunk = ev.chunk
        mix(d[8]); mix(d[9]); attend(d[6], vneed); o8 = attend(d[7], vneed); turn_weights(d[8]); turn_weights(d[9])
        d += [diff_item(5, 0), diff_item(5, 1)]
        mkB = turn_heads(zq[:, 1], [0, 1], mem_keys, chunk_ready(ev.chunk))[-1]
        zfree[1] = mkB + 1

        def finish_attention(w, items, o_half, last_qset_unit, xset, gains, vneed, ready1=None):
            ua, ub, uc, ud = out_units(w)
            o1 = turn_operand(o_nat, 0, [(None, 0, 0)], (o_evac, o_half), 2 * last_qset_unit + 2)[-1]
            attend(items[0], vneed); attend(items[1], vneed)
            multiply(ua, 0, 0, o1, "P", True, False)
            mix(items[2]); mix(items[3]); turn_weights(items[2]); turn_weights(items[3])
            attend(items[2], vneed)
            o_all = attend(items[3], vneed)
            o2 = turn_operand(o_nat, 1, [(None, 0, UK)], ready1 or (o_evac, o_all), 2 * last_qset_unit + 2)[-1]
            return out_tail(ua, ub, uc, ud, 0, o1, o2, xset, gains)

        def out_tail(ua, ub, uc, ud, oset, o1, o2, xset, gain):
            multiply(ub, oset, UK, o2, "P", False, True)
            r = residual(0, "P", ub, None)
            multiply(uc, oset, 0, o1, "S", True, False)
            a = turn_operand(x, 0, [(gain, xset, 0)], (resid_done, r.r + 2), 0)[-1]
            multiply(ud, oset, UK, o2, "S", False, True)
            r = residual(1, "S", ud, None)
            return a, r

        uses_a, r = finish_attention(A["a_w_out"][0], [d[8], d[9], d[10], d[11]], o8, qk2[1], 1,
                                     g_at("a_norm_mlp"), vneed)

        def mlp_units(w_up, w_down):
            base = len(UNITS)
            up = lambda j: [unit(w_up, h * UK * P, [(j * COLS, COLS)]) for h in range(2)]
            down = lambda j: [unit(w_down, j * COLS, [(c * COLS, COLS)]) for c in range(2)]
            up(0)
            for j in range(CHUNKS - 1):
                up(j + 1)
                down(j)
            down(CHUNKS - 1)
            return base

        def mlp(w_up, w_down, hset, use0, r1, gain):
            base = mlp_units(w_up, w_down)
            multiply(base, hset, 0, use0, "P", True, False)
            use1 = turn_operand(x, 1, [(gain, hset, UK)], (resid_done, r1.r + 2), 0)[-1]
            stt = statistics(x, (resid_done, r1.r + 2), kind="square")
            multiply(base + 1, hset, UK, use1, "P", False, True)
            st = add("mlp")
            st.base, st.hset, st.uset, st.t0, st.hi0 = base, hset, 1 - hset, count.t, count.hi
            st.relu0, st.freed = count.relu2, {b: [free[b, t] for t in range(NT)] for b in "SO"}
            st.w = (w_up, w_down)
            count.t += 2 * CHUNKS
            count.hi += 2 * CHUNKS
            count.relu2 += 2 * CHUNKS
            for t in range(NT):
                free["P", t] = (relu2_done, count.relu2 - 1 + t)
            return stt, base

        def mlp_end(base, gains, scale):
            ul = base + 4 * CHUNKS - 2
            uset = STEPS[-1].uset
            multiply(ul, uset, UK, count.t - 1, "S", False, True)
            r0 = residual(0, "S", ul, scale)
            multiply(ul + 1, uset, UK, count.t - 1, "O", False, True)
            a = turn_operand(x, 0, gains(0), (resid_done, r0.r + 2), 0)[-1]
            r1 = residual(1, "O", ul + 1, scale)
            return a, r1

        sc, base = mlp(A["a_w_up"][0], A["a_w_down"][0], 1, uses_a, r, g_at("a_norm_mlp"))
        bg = lambda h: [(g_at("b_norm_attn"), 0, UK * h), (g_at("kv_norm"), 1, UK * h)]
        a0, r1 = mlp_end(base, bg, sc)
        w, wkv = A["b_w_in"][0], A["w_kv"]
        q1 = chunk_units(w, [(512, 512)])
        q0 = chunk_units(w, [(0, 512)])
        k0 = chunk_units(wkv, [(0, 512)])
        kv1 = chunk_units(wkv, [(512, 512)])
        v1 = chunk_units(wkv, [(1024, 512)])
        multiply(q1[0], 0, 0, a0, "P", True, False)
        a1 = turn_operand(x, 1, bg(1), (resid_done, r1.r + 2), 0)[-1]
        xb = [a0, a1]
        rs_b = statistics(x, (resid_done, r1.r + 2))
        mul_chunk_half(q1, 1, 0, xb)
        evacuate(q1[1], [((0, 512), lambda t: zq[:, 1, t, :])], rs_b, slot_free=zfree[1])
        r1_ = rope(1, 256, rope1)
        mul_chunk_half(q0, 0, 0, xb)
        qm_use = turn_heads(zq[:, 1], [0, 1, 2, 3], heads(0, 4, 4), rope_ready(r1_.rope))[-1]
        zfree[1] = qm_use + 1
        m = [mem_item(0, 0, qm_use, mkB), mem_item(0, 1, qm_use, mkB)]
        mul_chunk_half(q0, 1, 0, xb)
        evacuate(q0[1], [((0, 512), lambda t: zq[:, 0, t, :])], rs_b, slot_free=zfree[0])
        r0_ = rope(0, 512, rope1)
        mix(m[0]); mix(m[1]); turn_weights(m[0]); turn_weights(m[1])
        m += [mem_item(1, 0, qm_use, mkB), mem_item(1, 1, qm_use, mkB)]
        mul_chunk_half(k0, 0, 1, xb)
        q_use = turn_heads(zq[:, 0], [0, 1, 2, 3], heads(0, 0, 4), rope_ready(r0_.rope))[-1]
        zfree[0] = q_use + 1
        memV = (chunk_evac, 2 * memB_chunk + 2)
        mix(m[2]); mix(m[3]); attend(m[0], memV); attend(m[1], memV); turn_weights(m[2]); turn_weights(m[3])
        mul_chunk_half(k0, 1, 1, xb)
        evacuate(k0[1], [((0, 512), lambda t: zq[:, 1, t, :])], rs_b, slot_free=zfree[1])
        r2_ = rope(1, 512, rope1)
        attend(m[2], memV); attend(m[3], memV)
        mul_chunk_half(kv1, 0, 1, xb)
        k_use = turn_heads(zq[:, 1], [0, 1, 2, 3], pairs(0, 16, 4), rope_ready(r2_.rope))[-1]
        zfree[1] = k_use + 1

        def causal_item(p, t):
            return scores("causal", p, t, p, qk[:, 16 + p, :], k_use if p < 4 else k2_use)

        c = [causal_item(0, 0), causal_item(0, 1)]
        mul_chunk_half(kv1, 1, 1, xb)
        ev = evacuate(kv1[1], [((0, 256), lambda t: zq[:, 0, t, 0:256]), ((256, 512), lambda t: v[:, t, 0:256])],
                      rs_b, slot_free=zfree[0])
        v_first = (chunk_evac, 2 * ev.chunk + 2)
        r3_ = rope(0, 256, rope1)
        mix(c[0]); mix(c[1]); turn_weights(c[0]); turn_weights(c[1])
        c += [causal_item(1, 0), causal_item(1, 1)]
        mul_chunk_half(v1, 0, 1, xb)
        k2_use = turn_heads(zq[:, 0], [0, 1], pairs(0, 20, 2), rope_ready(r3_.rope))[-1]
        zfree[0] = k2_use + 1
        mix(c[2]); mix(c[3]); attend(c[0], v_first); attend(c[1], v_first); turn_weights(c[2]); turn_weights(c[3])
        c += [causal_item(2, 0), causal_item(2, 1)]
        mul_chunk_half(v1, 1, 1, xb)
        ev = evacuate(v1[1], [((0, 512), lambda t: v[:, t, 256:768])], rs_b)
        v_all = (chunk_evac, 2 * ev.chunk + 2)
        mix(c[4]); mix(c[5]); attend(c[2], v_first); attend(c[3], v_first); turn_weights(c[4]); turn_weights(c[5])
        c += [causal_item(3, 0), causal_item(3, 1)]
        attend(c[4], v_all); attend(c[5], v_all)
        mix(c[6]); mix(c[7]); turn_weights(c[6]); turn_weights(c[7])
        c += [causal_item(4, 0), causal_item(4, 1)]
        attend(c[6], v_all); o8 = attend(c[7], v_all)
        mix(c[8]); mix(c[9]); turn_weights(c[8]); turn_weights(c[9])
        c += [causal_item(5, 0), causal_item(5, 1)]
        uses_a, r = finish_attention(A["b_w_out"][0], [c[8], c[9], c[10], c[11]], o8, q0[1], 1,
                                     g_at("b_norm_mlp"), v_all)
        st = add("late_loads")
        st.o, st.e = count.o, ITEMS[-1].exp + 1
        sc, base = mlp(A["b_w_up"][0], A["b_w_down"][0], 1, uses_a, r, g_at("b_norm_mlp"))

        b2 = lambda h: [(g_at("norm1_w_2"), 0, UK * h)]
        a0, r1 = mlp_end(base, b2, sc)
        w = A["w_in_2"][0]
        qa = chunk_units(w, [(0, 512)])
        sm = [unit(w, h * UK * P, [(512, SMALL)]) for h in range(2)]
        at = 512 + SMALL
        qb, kb, vb, gb = ([(at + 512 * i, 512)] for i in range(4))
        kb, qb, vb, gb = (chunk_units(w, s) for s in (kb, qb, vb, gb))
        multiply(qa[0], 0, 0, a0, "P", True, False)
        a1 = turn_operand(x, 1, b2(1), (resid_done, r1.r + 2), 0)[-1]
        xb = [a0, a1]
        rs_2 = statistics(x, (resid_done, r1.r + 2), kind="final", factor=a1 + 1)
        mul_chunk_half(qa, 1, 0, xb)
        evacuate(qa[1], [((0, 512), lambda t: zq[:, 0, t, :])], rs_2, slot_free=zfree[0])
        qn = add("query_norm")
        qn.chunk, qn.ss = count.chunk, [col(8) for _ in range(2)]
        qn.rs = [col(8) for _ in range(2)]
        mul_chunk_half(sm, 0, 0, xb)
        qa_use = turn_heads(zq[:, 0], [0, 1, 2, 3], heads(0, 0, 4), lambda t: (qn_done, t + 1))[-1]
        zfree[0] = qa_use + 1
        mul_chunk_half(sm, 1, 0, xb)
        ev = evacuate(sm[1], [((0, SMALL), lambda t: zs[:, t, :])], rs_2)
        st = add("small_norm")
        st.chunk, st.ss = count.chunk, [col(1) for _ in range(2)]
        st.rs = [col(1) for _ in range(2)]
        mul_chunk_half(kb, 0, 0, xb)
        INDEX_BLOCK = [8, 10, 9, 11]
        index_q = lambda h: (lambda t: qk[32 * h:32 * h + 32, INDEX_BLOCK[h]:INDEX_BLOCK[h] + 1, tok(t)])
        sn_use = turn_heads(sn[:, :, :, :].rearrange("p t b n -> p t (b n)"), [0, 1, 2],
                            [(slice(32 * h, 32 * h + 32), slice(0, 1), index_q(h)) for h in range(4)] +
                            pairs(1, Q_IK, 2), lambda t: (sn_done, t + 1))[-1]

        def index_scores(t):
            n = P * (t + 1)
            per = COLS // n
            st = add("index_scores")
            st.t, st.n, st.per, st.use, st.banks, st.dots = t, n, per, sn_use, [], count.dots
            st.m8, st.ind = col(8), col(4)
            for b in range(4 // per):
                count.dots += 1
                st.banks.append(s_use((dots_done, count.dots)))
            return st

        i0 = index_scores(0)
        kava = add("shared_kv")
        kava.use, kava.s, kava.ss, kava.rs = sn_use, s_use((kava_done, 1)), col(2), col(2)
        mul_chunk_half(kb, 1, 0, xb)
        evacuate(kb[1], [((0, 512), lambda t: zq[:, 1, t, :])], rs_2, slot_free=zfree[1])
        rk = rope(1, 512, rope2)
        st = add("shared_key_norm")
        st.st = kava
        st = add("select")
        st.st = i0
        i1 = index_scores(1)
        mul_chunk_half(qb, 0, 0, xb)
        ka_use = turn_heads(sn[:, :, 0, :].rearrange("p t n -> p t n"), [0], pairs(0, Q_KA, 1), lambda t: (ka_done, t + 1))[-1]
        kb_use = turn_heads(zq[:, 1], [0, 1, 2, 3], heads(0, 4, 4), rope_ready(rk.rope))[-1]
        zfree[1] = kb_use + 1
        mul_chunk_half(qb, 1, 0, xb)
        evacuate(qb[1], [((0, 512), lambda t: zq[:, 0, t, :])], rs_2, slot_free=zfree[0])
        rq = rope(0, 512, rope2)
        st = add("select")
        st.st = i1
        mul_chunk_half(vb, 0, 0, xb)
        qb_use = turn_heads(zq[:, 0], [0, 1, 2, 3], pairs(0, Q_QB, 4), rope_ready(rq.rope))[-1]
        zfree[0] = qb_use + 1

        def idx_item(p, t):
            return scores("idx", p, t, p, qk[:, Q_KA, :], max(ka_use, qa_use))

        va_need = (kava_done, 1)
        st = add("gain_load")
        st.free = zfree[0]
        d = [idx_item(0, 0), idx_item(0, 1)]
        mul_chunk_half(vb, 1, 0, xb)
        ev = evacuate(vb[1], [((0, 512), lambda t: v[:, t, 0:512])], rs_2)
        vr_need = (chunk_evac, 2 * ev.chunk + 2)
        mix(d[0]); mix(d[1]); turn_weights(d[0]); turn_weights(d[1])
        d += [idx_item(1, 0), idx_item(1, 1)]
        st = add("bias_load")
        st.s = d[-1].s
        mul_chunk_half(gb, 0, 0, xb)
        mix(d[2]); mix(d[3]); attend(d[0], va_need); attend(d[1], va_need); turn_weights(d[2]); turn_weights(d[3])
        d += [idx_item(2, 0), idx_item(2, 1)]
        mul_chunk_half(gb, 1, 0, xb)
        evacuate(gb[1], [((0, 512), lambda t: zq[:, 1, t, :])], rs_2, slot_free=zfree[1], silu=True)
        gate_ready = (chunk_evac, 2 * count.chunk)
        mix(d[4]); mix(d[5]); attend(d[2], va_need); attend(d[3], va_need); turn_weights(d[4]); turn_weights(d[5])
        d += [idx_item(3, 0), idx_item(3, 1)]
        attend(d[4], va_need); attend(d[5], va_need)
        mix(d[6]); mix(d[7]); turn_weights(d[6]); turn_weights(d[7])
        attend(d[6], va_need)
        o_a = attend(d[7], va_need)

        def retention_pair(p):
            st = add("retention_scores")
            st.p, st.o_before, st.use, st.banks = p, ro[0][0] + 2 * p, max(kb_use, qb_use), []
            st.d0, st.first = count.decayed, p == 0
            for a in range(2):
                count.decayed += 1
                st.banks.append(s_use((decayed, count.decayed)))
            return st

        ua, ub, uc, ud = out_units(A["w_out_2"][0])
        o1 = turn_operand(o_nat, 0, [(None, 1, 0)], (o_evac, o_a), 0)[-1]
        ro = [o_use() for _ in range(2)]
        for p in range(4):
            decayed_pair = retention_pair(p)
            st = add("retention_out")
            st.p, st.st, st.ro, st.need = p, decayed_pair, ro, vr_need
        multiply(ua, 1, 0, o1, "P", True, False)
        st = add("group_norm")
        st.ro, st.o_end, st.gate, st.mu = ro, ro[0][0] + 8, gate_ready, [col(8) for _ in range(2)]
        st.va, st.rs = [col(8) for _ in range(2)], [col(8) for _ in range(2)]
        o2 = turn_operand(o_nat, 1, [(None, 1, UK)], (ob_done, 2), 0)[-1]
        uses_a, r = out_tail(ua, ub, uc, ud, 1, o1, o2, 0, g_at("norm2_w_2"))

        fbase = len(UNITS)
        gate_up = lambda j: [unit_gate(j, h) for h in range(2)]

        def unit_gate(j, h):
            n = 2 * FCHUNK
            parts = [(A[nm][0][h * UK * P:(h + 1) * UK * P, j * FCHUNK:(j + 1) * FCHUNK]
                      .rearrange("(k p) n -> p k n", p=P), slice(0, UK), slice(i * FCHUNK, (i + 1) * FCHUNK))
                     for i, nm in enumerate(("w_gate_2", "w_up_2"))]
            un = Step()
            un.n, un.nk, un.parts = n, UK, parts
            UNITS.append(un)
            return len(UNITS) - 1

        def unit_fdown(j):
            return unit(A["w_down_2"][0], j * FCHUNK, [(0, D)], nk=2)

        gate_up(0)
        for j in range(FCHUNKS - 1):
            gate_up(j + 1)
            unit_fdown(j)
        unit_fdown(FCHUNKS - 1)
        multiply(fbase, 0, 0, uses_a, "P", True, False)
        use1 = turn_operand(x, 1, [(g_at("norm2_w_2"), 0, UK)], (resid_done, r.r + 2), 0)[-1]
        rs_f = statistics(x, (resid_done, r.r + 2))
        multiply(fbase + 1, 0, UK, use1, "P", False, True)
        st = add("ffn")
        st.base, st.uset, st.hset, st.t0, st.hi0 = fbase, 1, 0, count.t, count.hi
        st.relu0, st.rs = count.relu2, rs_f
        st.freed = {b: [free[b, t] for t in range(NT)] for b in "SO"}
        st = add("store")
        st.u, st.rs, st.r = len(UNITS) - 1, rs_f, count.resid

        N_UNITS = len(UNITS)
        slot, prev, fills = [], [], []
        owner, filled = [None] * RING, [0] * RING
        for u in range(N_UNITS):
            s = u % RING if u < fbase else (fbase + (u - fbase) % FRING) % RING
            slot.append(s)
            prev.append(owner[s])
            owner[s] = u
            filled[s] += 1
            fills.append(filled[s])
        assert fbase % RING == 0

        def shaped(buf, u):
            un = UNITS[u]
            return buf[:, slot[u], 0:un.nk * un.n].rearrange("p (k n) -> p k n", k=un.nk)

        out_rows = out[0].rearrange("(t p) n -> p t n", p=P)

        block = ctx.enter_context(nc.Block())

        @block.sync
        def _(sp):
            def load(u):
                if prev[u] is not None:
                    sp.wait_ge(hi_done, prev[u] + 1)
                    sp.wait_ge(lo_done, prev[u] + 1)
                dst = shaped(raw, u)
                for src, ks, cs in UNITS[u].parts:
                    sp.dma_start(dst[:, ks, cs], src).then_inc(landed[slot[u]], 16)

            def load_mlp(base, w_up, w_down):
                with sp.Fori(0, CHUNKS - 1) as j:
                    for c in range(4):
                        u = base + 2 + c
                        sp.wait_ge(hi_done, j * 4 + (prev[u] + 1))
                        sp.wait_ge(lo_done, j * 4 + (prev[u] + 1))
                        dst = shaped(raw, u)
                        for i in range(2):
                            if c < 2:
                                rows = (c * UK + 2 * i) * P
                                src = w_up[rows:rows + 2 * P, bass.ds(j * COLS + COLS, COLS)]
                            else:
                                src = w_down[bass.ds(j * COLS + 2 * i * P, 2 * P), (c - 2) * COLS:(c - 1) * COLS]
                            sp.dma_start(dst[:, 2 * i:2 * i + 2, :], src.rearrange("(k p) n -> p k n", p=P))\
                              .then_inc(landed[slot[u]], 16)

            def load_ffn(base):
                with sp.Fori(1, FCHUNKS - 2) as j:
                    for c in range(3):
                        u = base + 2 + 3 + c
                        sp.wait_ge(hi_done, j * 3 + (prev[u] + 1 - 3))
                        sp.wait_ge(lo_done, j * 3 + (prev[u] + 1 - 3))
                        dst = shaped(raw, u)
                        for i in range(2):
                            if c < 2:
                                wsrc = A[("w_gate_2", "w_up_2")[i]][0]
                                src = wsrc[c * UK * P:(c + 1) * UK * P, bass.ds(j * FCHUNK + FCHUNK, FCHUNK)]
                                d_ = dst[:, :, i * FCHUNK:(i + 1) * FCHUNK]
                            else:
                                src = A["w_down_2"][0][bass.ds(j * FCHUNK + i * P, P), :]
                                d_ = dst[:, i:i + 1, :]
                            sp.dma_start(d_, src.rearrange("(k p) n -> p k n", p=P)).then_inc(landed[slot[u]], 16)

            mlps = {st.base: st.w for st in STEPS if st.kind == "mlp"}
            u = 0
            while u < N_UNITS:
                if u - 2 in mlps:
                    load_mlp(u - 2, *mlps[u - 2])
                    u += 4 * (CHUNKS - 1)
                elif u == fbase + 5:
                    load_ffn(fbase)
                    u += 3 * (FCHUNKS - 3)
                else:
                    load(u)
                    u += 1
            last = STEPS[-1]
            for i, (half, t) in enumerate((c, t) for c in range(2) for t in range(NT)):
                sp.wait_ge(resid_done, last.r + i + 1)
                sp.dma_start(out_rows[:, t, half * COLS:(half + 1) * COLS], x[:, t, half * COLS:(half + 1) * COLS])\
                  .then_inc(stored, 16)
            sp.wait_ge(stored, 16 * 4)

        @block.gpsimd
        def _(pool):
            chain = [0]

            def behind(ins):
                chain[0] += 1
                ins.then_inc(pool_chain, 1)
                pool.wait_ge(pool_chain, chain[0])

            def do_rope(st):
                nh = st.n // DH
                for t in range(NT):
                    pool.wait_ge(chunk_evac, 2 * (st.chunk - 1) + t + 1)
                    if st.rope or t:
                        pool.wait_ge(rope_done, 2 * st.rope + t)
                    z = zq[:, st.slot, t, 0:st.n].rearrange("p (h d) -> p h d", d=DH)
                    zh = zq[:, st.slot, t, 0:st.n].rearrange("p (h x d) -> p h x d", x=2, d=DH // 2)
                    t1 = rt[:, 0, 0:st.n].rearrange("p (h d) -> p h d", d=DH)
                    t2 = rt[:, 1, 0:st.n].rearrange("p (h x d) -> p h x d", x=2, d=DH // 2)
                    cos = st.table[:, t, 0:64].unsqueeze(1).broadcast_to([P, nh, DH])
                    pool.tensor_tensor(t1, z, cos, ALU.mult)
                    for i in range(2):
                        sin = st.table[:, t, 64 + 32 * i:96 + 32 * i].unsqueeze(1).broadcast_to([P, nh, DH // 2])
                        last = pool.tensor_tensor(t2[:, :, i, :], zh[:, :, 1 - i, :], sin, ALU.mult)
                    behind(last)
                    pool.tensor_tensor(zq[:, st.slot, t, 0:st.n], rt[:, 0, 0:st.n], rt[:, 1, 0:st.n], ALU.add)\
                        .then_inc(rope_done, 1)

            for st in STEPS:
                if st.kind == "setup":
                    pool.memset(ident[:], 0.0)
                    pool.memset(tri[:], 1.0)
                    pool.memset(flip[:], 0.0)
                    pool.memset(epsc[:, 0:1], EPS)
                    pool.memset(epsc[:, 1:2], GN_EPS)
                    pool.memset(identb[:], 0.0)
                    behind(pool.memset(cmask[:], 0.0))
                    pool.affine_select(out=ident[:], in_=ident[:], compare_op=ALU.not_equal, fill=1.0, base=0,
                                       pattern=[[-1, P]], channel_multiplier=1).then_inc(consts_made, 1)
                    pool.affine_select(out=identb[:], in_=identb[:], compare_op=ALU.not_equal, fill=1.0, base=0,
                                       pattern=[[-1, P]], channel_multiplier=1).then_inc(consts_made, 1)
                    pool.affine_select(out=flip[:], in_=flip[:], compare_op=ALU.not_equal, fill=1.0 / SCALE,
                                       base=1 - P, pattern=[[1, P]], channel_multiplier=1).then_inc(consts_made, 1)
                    pool.affine_select(out=cmask[:], in_=cmask[:], compare_op=ALU.is_ge, fill=NEG, base=0,
                                       pattern=[[-1, P]], channel_multiplier=1).then_inc(consts_made, 1)
                    pool.affine_select(out=tri[:], in_=tri[:], compare_op=ALU.is_ge, fill=0.0, base=0,
                                       pattern=[[1, P]], channel_multiplier=-1).then_inc(consts_made, 1)
                    pool.memset(qk[:, 0:16, :], 0.0).then_inc(heads_zeroed, 1)
                    pool.wait_ge(bias_vec, 1)
                    pool.dma_start(bias_dram, biasvec).then_inc(bias_stored, 16)
                    pool.wait_ge(lam_done, 1)
                elif st.kind == "rope":
                    do_rope(st)
                elif st.kind == "late_loads":
                    pool.wait_ge(o_evac, st.o)
                    pool.memset(qk[:, 0:16, :], 0.0).then_inc(heads_zeroed, 1)
                elif st.kind == "query_norm":
                    for t in range(NT):
                        pool.wait_ge(chunk_evac, 2 * (st.chunk - 1) + t + 1)
                        pool.tensor_tensor(rt[:, t, :], zq[:, 0, t, :], zq[:, 0, t, :], ALU.mult).then_inc(qsq_done, 1)
                elif st.kind == "small_norm":
                    pool.wait_ge(qn_done, 2)
                elif st.kind == "group_norm":
                    for t in range(NT):
                        pool.wait_ge(yc_done, t + 1)
                        y = o_nat[:, t, 512:1024]
                        pool.tensor_tensor(rt[:, t, :], y, y, ALU.mult).then_inc(ysq_done, 1)
                    for t in range(NT):
                        y = o_nat[:, t, 512:1024]
                        pool.wait_ge(yn_done, t + 1)
                        pool.wait_ge(*st.gate)
                        pool.wait_ge(gn_landed, 32)
                        behind(pool.tensor_tensor(y, y, gn[:, 0, :], ALU.mult))
                        behind(pool.tensor_tensor(y, y, gn[:, 1, :], ALU.add))
                        pool.tensor_tensor(y, y, zq[:, 1, t, :], ALU.mult).then_inc(ob_done, 1)

        @block.scalar
        def _(act):
            chain = [0]
            sums = [0]

            def behind(ins):
                chain[0] += 1
                ins.then_inc(act_chain, 1)
                act.wait_ge(act_chain, chain[0])

            def guess_inverse_rms(dst, ss, n, eps=0):
                behind(act.activation(dst, ss, ACT.Ln, scale=1.0 / n, bias=epsc[:, eps:eps + 1]))
                act.activation(dst, dst, ACT.Exp, scale=-0.5).then_inc(guess_done, 1)

            def guess_from_vector(dst, ss, n, eps=0):
                sums[0] += 1
                act.wait_ge(sum_done, sums[0])
                guess_inverse_rms(dst, ss, n, eps)

            def split_hi(u):
                if u >= N_UNITS:
                    return
                act.wait_ge(landed[slot[u]], 32 * fills[u])
                if prev[u] is not None:
                    act.wait_ge(mul_done, 2 * prev[u] + 2)
                act.activation(shaped(whi, u), shaped(raw, u), ACT.Copy).then_inc(hi_done, 1)

            def split_hi_loop(u, j, j0, per):
                act.wait_ge(landed[slot[u]], j * 32 + (32 * fills[u] - 32 * j0))
                act.wait_ge(mul_done, j * (2 * per) + (2 * prev[u] + 2 - 2 * per * j0))
                act.activation(shaped(whi, u), shaped(raw, u), ACT.Copy).then_inc(hi_done, 1)

            def mlp_chunk(st, j, peel):
                u0 = st.base + 2 + AHEAD + (4 * peel)
                one = (lambda u: split_hi(u)) if isinstance(j, int) else (lambda u: split_hi_loop(u, j, peel, 4))
                one(u0)
                for b in range(2):
                    act.wait_ge(t_full, j * 2 + (st.t0 + b + 1))
                    k = UK + 2 * b
                    act.activation(set_hi[st.uset][:, k:k + 2, :], Tb[(st.t0 + b) % 2][:], ACT.Copy)\
                       .then_inc(t_hi, 1)
                one(u0 + 1)
                relu(j * 8 + (2 * st.base + 6))
                one(u0 + 2)
                one(u0 + 3)

            def relu(multiplied):
                for t in range(NT):
                    act.wait_ge(mul_done, multiplied + (t + 1))
                    act.activation(hidden[:, t, :], Pb[t][:], ACT.Relu).then_inc(relu_done, 1)

            def ffn_chunk(st, j, peel):
                u0 = st.base + 2 + AHEAD + 3 * peel
                one = (lambda u: split_hi(u)) if isinstance(j, int) else (lambda u: split_hi_loop(u, j, peel, 3))
                one(u0)
                hidden_hi(st, j)
                one(u0 + 1)
                silu(st, j * 6 + (2 * st.base + 6))
                one(u0 + 2)

            def hidden_hi(st, j):
                for b in range(2):
                    act.wait_ge(t_full, j * 2 + (st.t0 + b + 1))
                    act.activation(set_hi[st.uset][:, b, :], Tb[(st.t0 + b) % 2][:, 0:TOK], ACT.Copy)\
                       .then_inc(t_hi, 1)

            def silu(st, multiplied):
                for t in range(NT):
                    act.wait_ge(mul_done, multiplied + (t + 1))
                    act.activation(zq[:, 1, t, 0:FCHUNK], Pb[t][:, 0:FCHUNK], ACT.Silu, scale=st.rs.rs[:, t:t + 1])\
                       .then_inc(silu_done, 1)

            def biases(h):
                return bass.AP(bias_dram.tensor, h * 512, [[1, P], [512, 4], [1, TOK]])

            for st in STEPS:
                if st.kind == "setup":
                    act.dma_start(mem_nat[:], A["mem"][0].rearrange("(t p) n -> p t n", p=P)).then_inc(mem_landed, 16)
                    for i, g in enumerate(GAINS):
                        g_ap = A[g] if len(A[g].shape) == 1 else A[g][0]
                        act.dma_start(grow[i * KT:(i + 1) * KT, :], g_ap.rearrange("(k p) -> k p", p=P))\
                           .then_inc(gains_landed, 16)
                    act.dma_start(x[:], A["x"][0].rearrange("(t p) n -> p t n", p=P)).then_inc(x_landed, 16)
                    def spread(dst, src):
                        act.dma_start(dst, src.partition_broadcast(P)).then_inc(consts_landed, 16)
                    spread(subln[:], A["a_subln"][0])
                    act.dma_start(rt[:, 0, 0:256], A["a_lambda"][0].rearrange("a d -> (a d)").partition_broadcast(P))\
                       .then_inc(consts_landed, 16)
                    spread(kvn[:], A["kv_norm_w_2"][0])
                    spread(qkn[:, 0, :], A["q_norm_w_2"][0])
                    spread(qkn[:, 1, :], A["k_norm_w_2"][0])
                    for dst, name in ((rope1, "rope1"), (rope2, "rope2"), (dec, "decays")):
                        act.dma_start(dst[:], A[name].rearrange("(t p) n -> p t n", p=P)).then_inc(consts_landed, 16)
                    act.dma_start(onehot, A["bucket_onehot"]).then_inc(consts_landed, 16)
                    act.dma_start(rel8[:], A["rel_bias_2"]).then_inc(consts_landed, 16)
                    act.dma_start(wukv[:, 0, :], A["w_uk_2"][0]).then_inc(consts_landed, 16)
                    act.dma_start(wukv[:, 1, :], A["w_uv_2"][0]).then_inc(consts_landed, 16)
                    for u in range(AHEAD):
                        split_hi(u)
                    act.wait_ge(consts_made, 5)
                    act.wait_ge(lam_sum, 1)
                    act.activation(st.lam[:, 2:4], st.lam[:, 0:2], ACT.Exp).then_inc(lam_exp, 1)
                elif st.kind == "multiply":
                    split_hi(st.u + AHEAD)
                elif st.kind == "statistics":
                    act.wait_ge(*st.ready)
                    for r, ss in enumerate([st.ss, st.ss2] if st.what == "final" else [st.ss]):
                        if r:
                            act.wait_ge(rstd_done, st.n + 1)
                        for t in range(NT):
                            ins = act.activation(junk[:, t, :], st.src[:, t, :], ACT.Square, accum_out=ss[:, t:t + 1])
                        ins.then_inc(ss_done, 1)
                        if st.what != "square":
                            act.wait_ge(ss_done, st.sums + r + 1)
                            guess_inverse_rms(st.r2 if r else st.rs, ss, D)
                elif st.kind == "turn_operand":
                    for b in range(2):
                        n = st.use[b]
                        act.wait_ge(t_full, n + 1)
                        if st.set_free and b == 0:
                            act.wait_ge(mul_done, st.set_free)
                        for g, s, k0 in st.gains:
                            k = k0 + 2 * b
                            if g is None:
                                ins = act.activation(set_hi[s][:, k:k + 2, :], Tb[n % 2][:], ACT.Copy)
                            else:
                                kk = 4 * st.half + 2 * b
                                act.wait_ge(gain_cols, 2)
                                for i in range(2):
                                    ins = act.activation(set_hi[s][:, k + i, :], Tb[n % 2][:, i * TOK:(i + 1) * TOK],
                                                         ACT.Copy, scale=gcol[:, g + kk + i:g + kk + i + 1])
                        ins.then_inc(t_hi, 1)
                elif st.kind == "evacuate":
                    act.wait_ge(rstd_done, st.scale.n_done)
                    for t in range(NT):
                        act.wait_ge(mul_done, 2 * st.u + t + 1)
                        if st.slot_free and t == 0:
                            act.wait_ge(t_full, st.slot_free)
                        for i, ((a, b), dst) in enumerate(st.pieces):
                            ins = act.activation(dst(t), Pb[t][:, a:b], ACT.Silu if st.silu else ACT.Copy,
                                                 scale=st.scale.rs[:, t:t + 1])
                        ins.then_inc(chunk_evac, 1)
                elif st.kind == "scores":
                    it = st.it
                    act.wait_ge(nmax_done, it.i + 1)
                    if it.i == 0:
                        act.wait_ge(bias_stored, 16)
                    if it.before:
                        act.wait_ge(t_full, it.before.use + 1)
                    for c in range(2):
                        dst = e[:, it.buf, c * it.n:(c + 1) * it.n]
                        src = Sb[it.s % 2][:, c * it.n:(c + 1) * it.n]
                        ins = act.activation(dst, src, ACT.Exp, bias=it.nm[:, c:c + 1], scale=SCALE,
                                             accum_out=it.rs[:, c:c + 1])
                    ins.then_inc(exp_done, 1)
                elif st.kind == "attend":
                    it = st.it
                    if it.kind == "diff":
                        act.wait_ge(o_full, it.o + 1)
                        act.activation(junk1[:], Ob[it.o % 2][:, 0:P], ACT.Square, accum_out=it.oss).then_inc(osq_done, 1)
                        act.wait_ge(osq_done, it.osq)
                        guess_inverse_rms(it.ors, it.oss, P)
                elif st.kind == "late_loads":
                    act.wait_ge(o_evac, st.o)
                    act.dma_start(fgb, A["final_norm"].partition_broadcast(P)).then_inc(late_landed, 16)
                    act.dma_start(btoep, biases(0)).then_inc(late_landed, 16)
                elif st.kind == "bias_load":
                    act.wait_ge(s_full, st.s + 1)
                    act.dma_start(btoep, biases(4)).then_inc(late_landed, 16)
                elif st.kind == "gain_load":
                    act.wait_ge(t_full, st.free)
                    for i, g in enumerate(("ret_gn_w_2", "ret_gn_b_2")):
                        act.dma_start(gn[:, i, :], A[g][0].partition_broadcast(P)).then_inc(gn_landed, 16)
                elif st.kind == "index_scores":
                    for b in range(4 // st.per):
                        s = st.banks[b][0]
                        act.wait_ge(s_full, s + 1)
                        if st.t == 1 and b == 0:
                            act.wait_ge(dots_used, 1)
                        act.activation(relu_dots[:, b * st.per:(b + 1) * st.per, 0:st.n],
                                       Sb[s % 2][:, 0:st.per * st.n].rearrange("p (h n) -> p h n", h=st.per),
                                       ACT.Relu, scale=IDX_SCALE).then_inc(dots_done, 1)
                elif st.kind == "query_norm":
                    for t in range(NT):
                        guess_from_vector(st.rs[t], st.ss[t], DH)
                elif st.kind == "small_norm":
                    for t in range(NT):
                        guess_from_vector(st.rs[t], st.ss[t], P)
                elif st.kind == "shared_key_norm":
                    for t in range(NT):
                        guess_from_vector(st.st.rs[:, t:t + 1], st.st.ss[:, t:t + 1], DH)
                elif st.kind == "group_norm":
                    for t in range(NT):
                        guess_from_vector(st.rs[t], st.va[t], DH, eps=1)
                elif st.kind == "shared_kv":
                    s = st.s[0]
                    act.wait_ge(s_full, s + 1)
                    for t in range(NT):
                        act.activation(sn[:, t, 1, 0:DH], Sb[s % 2][:, t * P:t * P + DH], ACT.Copy)
                        ins = act.activation(v[:, t, 512:512 + DH], Sb[s % 2][:, t * P + DH:t * P + P], ACT.Copy)
                    ins.then_inc(kava_done, 1)
                elif st.kind == "mlp":
                    relu(2 * (st.base + 1))
                    mlp_chunk(st, 0, 0)
                    with act.Fori(1, CHUNKS - 1) as j:
                        mlp_chunk(st, j, 1)
                    for b in range(2):
                        n = st.t0 + 2 * (CHUNKS - 1) + b
                        act.wait_ge(t_full, n + 1)
                        k = UK + 2 * b
                        act.activation(set_hi[st.uset][:, k:k + 2, :], Tb[n % 2][:], ACT.Copy).then_inc(t_hi, 1)
                elif st.kind == "ffn":
                    act.wait_ge(rstd_done, st.rs.n_done)
                    silu(st, 2 * (st.base + 1))
                    ffn_chunk(st, 0, 0)
                    with act.Fori(1, FCHUNKS - 2) as j:
                        ffn_chunk(st, j, 1)
                    ffn_chunk(st, FCHUNKS - 2, FCHUNKS - 2)
                    hidden_hi(st, FCHUNKS - 1)

        @block.tensor
        def _(pe):
            def wait(pair):
                if pair is not None:
                    pe.wait_ge(*pair)

            def products(out_, hi, lo, wh, wl, start, stop):
                pe.matmul(out_, hi, wh, start=start, stop=False)
                pe.matmul(out_, hi, wl, start=False, stop=False)
                return pe.matmul(out_, lo, wh, start=False, stop=stop)

            def half_unit(u, t, lhs, k0, out_, start, stop):
                n = UNITS[u].n
                wh, wl = shaped(whi, u), shaped(wlo, u)
                for k in range(UK):
                    ins = products(out_[:, 0:n], set_hi[lhs][:, k0 + k, tok(t)], set_lo[lhs][:, k0 + k, tok(t)],
                                   wh[:, k, :], wl[:, k, :], start and k == 0, stop and k == UK - 1)
                ins.then_inc(mul_done, 1)

            banks = {"P": Pb, "S": Sb, "O": Ob}

            def turn_bank(n, src, tiles):
                for i, k in enumerate(tiles):
                    for t in range(NT):
                        at = (i * NT + t) * P
                        ins = pe.transpose(Tb[n % 2][:, at:at + P], src(t, k), ident[:])
                ins.then_inc(t_full, 1)

            def hidden_block(t, k):
                return hidden[:, t, k * P:(k + 1) * P]

            def mlp_chunk(st, j, peel, first):
                u0 = st.base + 2 + 4 * peel
                at = lambda base, per: j * per + (base - per * peel)
                for h in range(2):
                    u = u0 + h
                    pe.wait_ge(lo_done, at(u + 1, 4))
                    for t in range(NT):
                        if h == 0:
                            pe.wait_ge(relu2_done, at(st.relu0 + 2 * peel + t + 1, 2))
                        half_unit(u, t, st.hset, UK * h, Pb[t], h == 0, h == 1)
                    if h == 0:
                        hidden_turns(st, j)
                pe.wait_ge(t_evac, j * 2 + (st.t0 + 2))
                for c, b in enumerate("SO"):
                    u = u0 + 2 + c
                    pe.wait_ge(lo_done, at(u + 1, 4))
                    for t in range(NT):
                        if first:
                            wait(st.freed[b][t])
                        half_unit(u, t, st.uset, UK, banks[b][t], first, False)

            def hidden_turns(st, j):
                pe.wait_ge(relu2_done, j * 2 + (st.relu0 + 2))
                for b in range(2):
                    pe.wait_ge(t_evac, j * 2 + (st.t0 + b - 1))
                    turn_bank(st.t0 + b, hidden_block, [2 * b, 2 * b + 1])

            def ffn_down(st, u, first, last):
                wh, wl = shaped(whi, u), shaped(wlo, u)
                for c, b in enumerate("SO"):
                    for t in range(NT):
                        if first:
                            wait(st.freed[b][t])
                        for k in range(2):
                            cs = slice(c * COLS, (c + 1) * COLS)
                            ins = products(banks[b][t][:], set_hi[st.uset][:, k, tok(t)], set_lo[st.uset][:, k, tok(t)],
                                           wh[:, k, cs], wl[:, k, cs], first and k == 0, last and k == 1)
                        if last or c == 1:
                            ins.then_inc(mul_done, 1)

            def ffn_turns(st, j):
                pe.wait_ge(relu2_done, j * 2 + (st.relu0 + 2))
                for b in range(2):
                    pe.wait_ge(t_evac, j * 2 + (st.t0 + b - 1))
                    turn_bank(st.t0 + b, hidden_block, [b])

            def ffn_chunk(st, j, peel, first):
                u0 = st.base + 2 + 3 * peel
                at = lambda base, per: j * per + (base - per * peel)
                for h in range(2):
                    u = u0 + h
                    pe.wait_ge(lo_done, at(u + 1, 3))
                    for t in range(NT):
                        if h == 0:
                            pe.wait_ge(relu2_done, at(st.relu0 + 2 * peel + t + 1, 2))
                        half_unit(u, t, st.hset, UK * h, Pb[t], h == 0, h == 1)
                    if h == 0:
                        ffn_turns(st, j)
                pe.wait_ge(t_evac, j * 2 + (st.t0 + 2))
                pe.wait_ge(lo_done, at(u0 + 3, 3))
                ffn_down(st, u0 + 2, first, False)

            for st in STEPS:
                if st.kind == "setup":
                    pe.wait_ge(consts_made, 5)
                    pe.wait_ge(gains_landed, 16 * len(GAINS))
                    ng = len(GAINS) * KT
                    pe.wait_ge(consts_landed, CONSTS)
                    pe.matmul(Sb[bias_s[0] % 2][0:8, :], rel8[:], onehot, start=True, stop=True).then_inc(s_full, 1)
                    pe.transpose(Sb[gain_s[0] % 2][:, 0:ng], grow, ident[0:ng, 0:ng]).then_inc(s_full, 1)
                elif st.kind == "turn_operand":
                    wait(st.ready)
                    for b in range(2):
                        n = st.use[b]
                        if n >= 2:
                            pe.wait_ge(t_evac, n - 1)
                        k0 = UK * st.half + 2 * b
                        turn_bank(n, lambda t, k: st.src[:, t, k * P:(k + 1) * P], [k0, k0 + 1])
                elif st.kind == "multiply":
                    pe.wait_ge(t_evac, st.use + 1)
                    pe.wait_ge(lo_done, st.u + 1)
                    for t in range(NT):
                        if st.start:
                            wait(st.freed[t])
                        half_unit(st.u, t, st.lhs, st.k0, banks[st.bank][t], st.start, st.stop)
                elif st.kind == "turn_heads":
                    for t in range(NT):
                        n = st.use[t]
                        pe.wait_ge(*st.ready(t))
                        pe.wait_ge(t_evac, n - 1)
                        for i, b in enumerate(st.blocks):
                            ins = pe.transpose(Tb[n % 2][:, i * P:(i + 1) * P], st.src[:, t, b * P:(b + 1) * P],
                                               ident[:])
                        ins.then_inc(t_full, 1)
                elif st.kind == "scores":
                    it = st.it
                    pe.wait_ge(t_evac, it.need + 1)
                    wait(it.s_free)
                    if it.kind == "idx":
                        pe.wait_ge(sel_done, it.t + 1)
                        pe.wait_ge(late_landed, 32 if it.pair < 2 else 48)
                    S = Sb[it.s % 2]
                    for c in range(2):
                        o = c * it.n
                        ins = pe.matmul(S[:, o:o + it.n], headq[:, it.q, c, tok(it.t)], it.k[:, 0:it.n],
                                        start=True, stop=it.kind == "mem")
                        if it.kind == "idx":
                            c0 = P - P * it.t
                            pe.matmul(S[:, o:o + it.n], flip[:], btoep[:, 2 * it.pair % 4 + c, c0:c0 + it.n],
                                      start=False, stop=False)
                            ins = pe.matmul(S[:, o:o + it.n], identb[:], selmask[:, it.t, 0:it.n],
                                            start=False, stop=True)
                        elif it.kind != "mem":
                            ins = pe.matmul(S[:, o + it.n - P:o + it.n], identb[:], cmask[:], start=False, stop=True)
                    ins.then_inc(s_full, 1)
                elif st.kind == "turn_weights":
                    it = st.it
                    if it.kind == "diff":
                        pe.wait_ge(w_done, it.w)
                    else:
                        pe.wait_ge(exp_done, it.exp + 1)
                    pe.wait_ge(t_evac, it.use - 1)
                    nb = it.n // P * (1 if it.kind == "diff" else 2)
                    for b in range(nb):
                        ins = pe.transpose(Tb[it.use % 2][:, b * P:(b + 1) * P], e[:, it.buf, b * P:(b + 1) * P],
                                           ident[:])
                    ins.then_inc(t_full, 1)
                elif st.kind == "attend":
                    it = st.it
                    pe.wait_ge(t_evac, it.use + 1)
                    wait(it.o_free)
                    pe.wait_ge(*it.vneed)
                    nk = it.n // P
                    O = Ob[it.o % 2]
                    for c in range(1 if it.kind == "diff" else 2):
                        for k in range(nk):
                            b = c * nk + k
                            wt = wT[:, it.buf, b * P:(b + 1) * P]
                            h = 2 * it.pair + c
                            dst = O[:, c * DH:(c + 1) * DH]
                            if it.kind == "diff":
                                val, dst = v[:, k, it.pair * P:(it.pair + 1) * P], O[:, 0:P]
                            elif it.kind == "mem":
                                val = memkv[:, 1, k * 256 + h * DH:k * 256 + (h + 1) * DH]
                            elif it.kind == "causal":
                                val = v[:, k, h * DH:(h + 1) * DH]
                            else:
                                val = v[:, k, 512:512 + DH]
                            ins = pe.matmul(dst, wt, val, start=k == 0, stop=k == nk - 1)
                    ins.then_inc(o_full, 1)
                elif st.kind == "mlp":
                    mlp_chunk(st, 0, 0, True)
                    with pe.Fori(1, CHUNKS - 1) as j:
                        mlp_chunk(st, j, 1, False)
                    hidden_turns(st, CHUNKS - 1)
                elif st.kind == "index_scores":
                    pe.wait_ge(t_evac, st.use + 1)
                    for b, (s, freed) in enumerate(st.banks):
                        wait(freed)
                        for i in range(st.per):
                            h = b * st.per + i
                            ins = pe.matmul(Sb[s % 2][:, i * st.n:(i + 1) * st.n], qk[:, INDEX_BLOCK[h], tok(st.t)],
                                            qk[:, Q_IK, 0:st.n], start=True, stop=True)
                        ins.then_inc(s_full, 1)
                elif st.kind == "shared_kv":
                    pe.wait_ge(t_evac, st.use + 1)
                    s, freed = st.s
                    wait(freed)
                    for t in range(NT):
                        ins = pe.matmul(Sb[s % 2][:, tok(t)], qk[:, Q_C, tok(t)],
                                        wukv[:, :, :].rearrange("p a b -> p (a b)"), start=True, stop=True)
                    ins.then_inc(s_full, 1)
                elif st.kind == "retention_scores":
                    pe.wait_ge(t_evac, st.use + 1)
                    for a, (s, freed) in enumerate(st.banks):
                        wait(freed)
                        n = TOK - a * P
                        for c in range(2):
                            ins = pe.matmul(Sb[s % 2][:, c * n:(c + 1) * n], headq[:, 4 + st.p, c, tok(a)],
                                            qk[:, Q_QB + st.p, a * P:TOK], start=True, stop=True)
                        ins.then_inc(s_full, 1)
                elif st.kind == "retention_out":
                    pe.wait_ge(*st.need)
                    pe.wait_ge(decayed, st.st.d0 + 2)
                    for t in range(NT):
                        o, freed = st.ro[t]
                        if st.p == 0:
                            wait(freed)
                        for c in range(2):
                            h = 2 * st.p + c
                            for a in range(t + 1):
                                n = TOK - a * P
                                wt = e[:, a, c * n + (t - a) * P:c * n + (t - a + 1) * P]
                                ins = pe.matmul(Ob[o % 2][:, h * DH:(h + 1) * DH], wt, v[:, a, h * DH:(h + 1) * DH],
                                                start=a == 0, stop=a == t)
                        ins.then_inc(o_full, 1)
                elif st.kind == "ffn":
                    ffn_chunk(st, 0, 0, True)
                    with pe.Fori(1, FCHUNKS - 2) as j:
                        ffn_chunk(st, j, 1, False)
                    ffn_chunk(st, FCHUNKS - 2, FCHUNKS - 2, False)
                    ffn_turns(st, FCHUNKS - 1)
                    pe.wait_ge(t_evac, st.t0 + 2 * FCHUNKS)
                    u = st.base + 3 * FCHUNKS - 1
                    pe.wait_ge(lo_done, u + 1)
                    ffn_down(st, u, False, True)

        @block.vector
        def _(dve):
            chain = [0]

            def behind(ins):
                chain[0] += 1
                ins.then_inc(dve_chain, 1)
                dve.wait_ge(dve_chain, chain[0])

            def split_lo(u, hi=None):
                if u >= N_UNITS:
                    return
                dve.wait_ge(hi_done, u + 1 if hi is None else hi)
                dve.tensor_tensor(shaped(wlo, u), shaped(raw, u), shaped(whi, u), ALU.subtract).then_inc(lo_done, 1)

            guesses = [0]

            def inverse_rms(dst, ss, n, eps=EPS):
                var, sq = newton[:, 0, 0:dst.shape[1]], newton[:, 1, 0:dst.shape[1]]
                guesses[0] += 1
                dve.wait_ge(guess_done, guesses[0])
                dve.tensor_scalar(var, ss, 1.0 / n, eps, ALU.mult, ALU.add)
                behind(dve.tensor_tensor(sq, dst, dst, ALU.mult))
                behind(dve.scalar_tensor_tensor(out=sq, in0=sq, scalar=-0.5, in1=var, op0=ALU.mult, op1=ALU.mult))
                return dve.scalar_tensor_tensor(out=dst, in0=sq, scalar=1.5, in1=dst, op0=ALU.add, op1=ALU.mult)

            def relu2(st, j):
                for t in range(NT):
                    dve.wait_ge(relu_done, j * 2 + (st.relu0 + t + 1))
                    dve.tensor_tensor(hidden[:, t, :], hidden[:, t, :], Pb[t][:], ALU.mult).then_inc(relu2_done, 1)

            def gated(st, j):
                for t in range(NT):
                    dve.wait_ge(silu_done, j * 2 + (t + 1))
                    dve.tensor_tensor(hidden[:, t, 0:FCHUNK], zq[:, 1, t, 0:FCHUNK], Pb[t][:, FCHUNK:2 * FCHUNK],
                                      ALU.mult).then_inc(relu2_done, 1)

            def hidden_lo(st, j, k0, per):
                for b in range(2):
                    dve.wait_ge(t_hi, j * 2 + (st.hi0 + b + 1))
                    ks = slice(k0 + per * b, k0 + per * b + per)
                    dve.tensor_tensor(set_lo[st.uset][:, ks, :], Tb[(st.t0 + b) % 2][:, 0:per * TOK]
                                      .rearrange("p (k n) -> p k n", k=per), set_hi[st.uset][:, ks, :],
                                      ALU.subtract).then_inc(t_evac, 1)

            def mlp_chunk(st, j, peel):
                u0 = st.base + 2 + AHEAD + 4 * peel
                hi = lambda u: j * 4 + (u + 1 - 4 * peel)
                split_lo(u0, hi(u0))
                hidden_lo(st, j, UK, 2)
                split_lo(u0 + 1, hi(u0 + 1))
                relu2(st, j + 1)
                split_lo(u0 + 2, hi(u0 + 2))
                split_lo(u0 + 3, hi(u0 + 3))

            def ffn_chunk(st, j, peel):
                u0 = st.base + 2 + AHEAD + 3 * peel
                hi = lambda u: j * 3 + (u + 1 - 3 * peel)
                split_lo(u0, hi(u0))
                hidden_lo(st, j, 0, 1)
                split_lo(u0 + 1, hi(u0 + 1))
                gated(st, j + 1)
                split_lo(u0 + 2, hi(u0 + 2))

            bank_of = {"P": Pb, "S": Sb, "O": Ob}
            heads_view = lambda ap, n=8: ap.rearrange("p (h d) -> p h d", h=n)
            spread = lambda ap, n: ap.unsqueeze(2).broadcast_to([P, ap.shape[1], n])

            for st in STEPS:
                if st.kind == "setup":
                    lam = st.lam
                    dve.wait_ge(consts_landed, CONSTS)
                    behind(dve.tensor_tensor(lamprod, lamrow[:, :, 0, :], lamrow[:, :, 1, :], ALU.mult))
                    dve.tensor_reduce(lam[:, 0:2], lamprod, AX_X, ALU.add).then_inc(lam_sum, 1)
                    dve.tensor_scalar(subln[:], subln[:], 1.0 - LAM_INIT, None, ALU.mult)
                    behind(dve.tensor_tensor(qkn[:, 0, :], qkn[:, 0, :], qkn[:, 1, :], ALU.mult))
                    dve.wait_ge(s_full, 1)
                    dve.tensor_copy(biasvec, Sb[bias_s[0] % 2][0:8, :]).then_inc(bias_vec, 1)
                    dve.wait_ge(s_full, 2)
                    ng = len(GAINS) * KT
                    dve.tensor_copy(gcol[:], Sb[gain_s[0] % 2][:, 0:ng]).then_inc(gain_cols, 1)
                    dve.wait_ge(gain_cols, 1)
                    a, b = g_at("norm1_w_2"), g_at("final_norm")
                    dve.tensor_tensor(gcol[:, a:a + KT], gcol[:, a:a + KT], gcol[:, b:b + KT], ALU.mult)\
                       .then_inc(gain_cols, 1)
                    dve.wait_ge(gain_cols, 2)
                    for u in range(AHEAD):
                        split_lo(u)
                    dve.wait_ge(lam_exp, 1)
                    dve.scalar_tensor_tensor(out=lam[:, 4:5], in0=lam[:, 2:3], scalar=LAM_INIT, in1=lam[:, 3:4],
                                             op0=ALU.add, op1=ALU.subtract).then_inc(lam_done, 1)
                    dve.wait_ge(lam_done, 1)
                    dve.wait_ge(heads_zeroed, 1)
                elif st.kind == "multiply":
                    split_lo(st.u + AHEAD)
                elif st.kind == "turn_operand":
                    for b in range(2):
                        n = st.use[b]
                        dve.wait_ge(t_hi, st.hi + b + 1)
                        for g, s, k0 in st.gains:
                            k = k0 + 2 * b
                            T = Tb[n % 2][:].rearrange("p (k n) -> p k n", k=2)
                            if g is None:
                                ins = dve.tensor_tensor(set_lo[s][:, k:k + 2, :], T, set_hi[s][:, k:k + 2, :],
                                                        ALU.subtract)
                            else:
                                for i in range(2):
                                    gi = g + UK * st.half + 2 * b + i
                                    ins = dve.scalar_tensor_tensor(
                                        out=set_lo[s][:, k + i, :], in0=T[:, i, :], scalar=gcol[:, gi:gi + 1],
                                        in1=set_hi[s][:, k + i, :], op0=ALU.mult, op1=ALU.subtract)
                        ins.then_inc(t_evac, 1)
                elif st.kind == "turn_heads":
                    for t in range(NT):
                        n = st.use[t]
                        dve.wait_ge(t_full, n + 1)
                        T = Tb[n % 2][:].rearrange("p (b n) -> p b n", b=4)
                        for ps, bs, dst in st.pieces:
                            ins = dve.tensor_copy(dst(t), T[ps, bs, :])
                        ins.then_inc(t_evac, 1)
                elif st.kind == "statistics":
                    if st.what == "plain":
                        inverse_rms(st.rs, st.ss, D).then_inc(rstd_done, 1)
                    elif st.what == "square":
                        dve.wait_ge(ss_done, st.sums + 1)
                        behind(dve.tensor_scalar(st.rs, st.ss, 1.0 / D, EPS, ALU.mult, ALU.add))
                        dve.reciprocal(st.rs, st.rs).then_inc(rstd_done, 1)
                    else:
                        behind(inverse_rms(st.rs, st.ss, D))
                        dve.wait_ge(late_landed, 32)
                        dve.wait_ge(t_full, st.factor)
                        for t in range(NT):
                            ins = dve.scalar_tensor_tensor(out=x[:, t, :], in0=x[:, t, :], scalar=st.rs[:, t:t + 1],
                                                           in1=fgb, op0=ALU.mult, op1=ALU.mult)
                        ins.then_inc(rstd_done, 1)
                        behind(inverse_rms(st.r2, st.ss2, D))
                        dve.tensor_tensor(st.rs, st.rs, st.r2, ALU.mult).then_inc(rstd_done, 1)
                    dve.wait_ge(rstd_done, st.n_done)
                elif st.kind == "scores":
                    it = st.it
                    dve.wait_ge(s_full, it.s + 1)
                    S = Sb[it.s % 2][:, 0:2 * it.n].rearrange("p (c n) -> p c n", c=2)
                    behind(dve.tensor_reduce(it.nm, S, AX_X, ALU.max))
                    dve.tensor_scalar(it.nm, it.nm, -SCALE, None, ALU.mult)\
                       .then_inc(nmax_done, 1)
                elif st.kind == "mix":
                    it = st.it
                    dve.wait_ge(exp_done, it.exp + 1)
                    ins = dve.reciprocal(it.rs, it.rs)
                    if it.kind == "diff":
                        behind(ins)
                        behind(dve.tensor_tensor(it.rs[:, 1:2], it.rs[:, 1:2], lam[:, 4:5], ALU.mult))
                        e0, e1 = e[:, it.buf, 0:it.n], e[:, it.buf, it.n:2 * it.n]
                        behind(dve.tensor_scalar(e1, e1, it.rs[:, 1:2], None, ALU.mult))
                        ins = dve.scalar_tensor_tensor(out=e0, in0=e0, scalar=it.rs[:, 0:1], in1=e1,
                                                       op0=ALU.mult, op1=ALU.subtract)
                    ins.then_inc(w_done, 1)
                elif st.kind == "turn_weights":
                    it = st.it
                    dve.wait_ge(t_full, it.use + 1)
                    if it.before:
                        dve.wait_ge(o_full, it.before.o + 1)
                    m = it.n * (1 if it.kind == "diff" else 2)
                    dve.tensor_copy(wT[:, it.buf, 0:m], Tb[it.use % 2][:, 0:m]).then_inc(t_evac, 1)
                elif st.kind == "attend":
                    it = st.it
                    O = Ob[it.o % 2][:, 0:P]
                    at = it.pair * P + (SELF if it.kind == "mem" else 0)
                    dst = o_nat[:, it.t, at:at + P]
                    if it.kind == "diff":
                        behind(inverse_rms(it.ors, it.oss, P))
                        dve.scalar_tensor_tensor(out=dst, in0=O, scalar=it.ors, in1=subln[:], op0=ALU.mult,
                                                 op1=ALU.mult).then_inc(o_evac, 1)
                    else:
                        dve.wait_ge(o_full, it.o + 1)
                        dve.wait_ge(w_done, it.w)
                        dve.tensor_tensor(heads_view(dst, 2), heads_view(O, 2), spread(it.rs, DH), ALU.mult)\
                           .then_inc(o_evac, 1)
                elif st.kind == "residual":
                    for t in range(NT):
                        dve.wait_ge(mul_done, 2 * st.u + t + 1)
                        xs = x[:, t, st.half * COLS:(st.half + 1) * COLS]
                        if st.scale is None:
                            ins = dve.tensor_tensor(xs, xs, bank_of[st.bank][t][:], ALU.add)
                        else:
                            ins = dve.scalar_tensor_tensor(out=xs, in0=bank_of[st.bank][t][:],
                                                           scalar=st.scale.rs[:, t:t + 1], in1=xs,
                                                           op0=ALU.mult, op1=ALU.add)
                        ins.then_inc(resid_done, 1)
                elif st.kind == "mlp":
                    relu2(st, 0)
                    mlp_chunk(st, 0, 0)
                    with dve.Fori(1, CHUNKS - 1) as j:
                        mlp_chunk(st, j, 1)
                    hidden_lo(st, CHUNKS - 1, UK, 2)
                elif st.kind == "query_norm":
                    dve.wait_ge(heads_zeroed, 2)
                    for t in range(NT):
                        dve.wait_ge(qsq_done, t + 1)
                        dve.tensor_reduce(st.ss[t], heads_view(rt[:, t, :]), AX_X, ALU.add).then_inc(sum_done, 1)
                        behind(inverse_rms(st.rs[t], st.ss[t], DH))
                        z = heads_view(zq[:, 0, t, :])
                        dve.tensor_tensor(z, z, spread(st.rs[t], DH), ALU.mult).then_inc(qn_done, 1)
                elif st.kind == "small_norm":
                    for t in range(NT):
                        dve.wait_ge(chunk_evac, 2 * (st.chunk - 1) + t + 1)
                        z = zs[:, t, :]
                        dve.tensor_tensor_reduce(sn[:, t, 2, :], z[:, 0:P], z[:, 0:P], 1.0, 0.0, ALU.mult,
                                                 ALU.add, st.ss[t]).then_inc(sum_done, 1)
                        behind(inverse_rms(st.rs[t], st.ss[t], P))
                        dve.scalar_tensor_tensor(out=sn[:, t, 2, :], in0=z[:, 0:P], scalar=st.rs[t], in1=kvn[:],
                                                 op0=ALU.mult, op1=ALU.mult)
                        dve.tensor_copy(sn[:, t, 0, :], z[:, P:2 * P])
                        dve.tensor_copy(sn[:, t, 1, :].rearrange("p (r d) -> p r d", r=4),
                                        z[:, 2 * P:2 * P + 32].unsqueeze(1).broadcast_to([P, 4, 32])).then_inc(sn_done, 1)
                elif st.kind == "shared_key_norm":
                    kv = st.st
                    dve.wait_ge(kava_done, 1)
                    for t in range(NT):
                        ka = sn[:, t, 1, 0:DH]
                        dve.tensor_tensor_reduce(sn[:, t, 2, 0:DH], ka, ka, 1.0, 0.0, ALU.mult, ALU.add,
                                                 kv.ss[:, t:t + 1]).then_inc(sum_done, 1)
                        behind(inverse_rms(kv.rs[:, t:t + 1], kv.ss[:, t:t + 1], DH))
                        for c in range(2):
                            ins = dve.scalar_tensor_tensor(out=sn[:, t, 0, c * DH:(c + 1) * DH], in0=ka,
                                                           scalar=kv.rs[:, t:t + 1], in1=qkn[:, 0, :],
                                                           op0=ALU.mult, op1=ALU.mult)
                        ins.then_inc(ka_done, 1)
                elif st.kind == "select":
                    ix = st.st
                    t, n = ix.t, ix.n
                    behind(dve.tensor_scalar(ix.ind, zs[:, t, 2 * P + 32:SMALL], IDX_W_SCALE, None, ALU.mult))
                    dve.wait_ge(dots_done, ix.dots + len(ix.banks))
                    sc = score[:, 0:n]
                    behind(dve.tensor_scalar(sc, relu_dots[:, 0, 0:n], ix.ind[:, 0:1], None, ALU.mult))
                    for h in range(1, 4):
                        ins = dve.scalar_tensor_tensor(out=sc, in0=relu_dots[:, h, 0:n], scalar=ix.ind[:, h:h + 1],
                                                       in1=sc, op0=ALU.mult, op1=ALU.add)
                        if h < 3:
                            behind(ins)
                    ins.then_inc(dots_used, 1)
                    dve.wait_ge(dots_used, t + 1)
                    behind(dve.memset(score[0:DH, n - DH:n], BELOW))
                    src = sc
                    for r in range(TOPK // MAX8):
                        dst = work[r % 2][:, 0:n]
                        behind(dve.max(ix.m8, src))
                        behind(dve.match_replace(dst, ix.m8, src, TAKEN))
                        src = dst
                    dve.tensor_scalar(selmask[:, t, 0:n], src, TAKEN, NEG, ALU.not_equal, ALU.mult)\
                       .then_inc(sel_done, 1)
                elif st.kind == "retention_scores":
                    for a, (s, _) in enumerate(st.banks):
                        dve.wait_ge(s_full, s + 1)
                        n = TOK - a * P
                        if st.first:
                            dve.wait_ge(t_full, ITEMS[-1].use + 1)
                        else:
                            dve.wait_ge(o_full, st.o_before)
                        for c in range(2):
                            h = 2 * st.p + c
                            o = c * n
                            dst, src = e[:, a, o:o + n], Sb[s % 2][:, o:o + n]
                            ins = dve.scalar_tensor_tensor(out=dst[:, 0:P], in0=src[:, 0:P],
                                                           scalar=dec[:, a, 8 + h:9 + h], in1=tri[:], op0=ALU.mult,
                                                           op1=ALU.mult)
                            if n > P:
                                ins = dve.tensor_scalar(dst[:, P:n], src[:, P:n], dec[:, a, 8 + h:9 + h], None,
                                                        ALU.mult)
                        ins.then_inc(decayed, 1)
                elif st.kind == "group_norm":
                    for t in range(NT):
                        dve.wait_ge(o_full, st.o_end - 1 + t)
                        y = heads_view(o_nat[:, t, 512:1024])
                        o = st.ro[t][0]
                        dve.tensor_tensor(y, heads_view(Ob[o % 2][:]), spread(dec[:, t, 0:8], DH), ALU.mult)\
                           .then_inc(o_evac, 1)
                        dve.wait_ge(o_evac, o + 1)
                        behind(dve.tensor_reduce(st.mu[t], y, AX_X, ALU.add))
                        behind(dve.tensor_scalar(st.mu[t], st.mu[t], 1.0 / DH, None, ALU.mult))
                        dve.tensor_tensor(y, y, spread(st.mu[t], DH), ALU.subtract).then_inc(yc_done, 1)
                    for t in range(NT):
                        dve.wait_ge(ysq_done, t + 1)
                        y = heads_view(o_nat[:, t, 512:1024])
                        dve.tensor_reduce(st.va[t], heads_view(rt[:, t, :]), AX_X, ALU.add).then_inc(sum_done, 1)
                        behind(inverse_rms(st.rs[t], st.va[t], DH, eps=GN_EPS))
                        dve.tensor_tensor(y, y, spread(st.rs[t], DH), ALU.mult).then_inc(yn_done, 1)
                elif st.kind == "ffn":
                    gated(st, 0)
                    ffn_chunk(st, 0, 0)
                    with dve.Fori(1, FCHUNKS - 2) as j:
                        ffn_chunk(st, j, 1)
                    ffn_chunk(st, FCHUNKS - 2, FCHUNKS - 2)
                    hidden_lo(st, FCHUNKS - 1, 0, 1)
                elif st.kind == "store":
                    for i, (c, t) in enumerate((c, t) for c in range(2) for t in range(NT)):
                        dve.wait_ge(mul_done, 2 * st.u + i + 1)
                        xs = x[:, t, c * COLS:(c + 1) * COLS]
                        dve.scalar_tensor_tensor(out=xs, in0=bank_of["SO"[c]][t][:], scalar=st.rs.rs[:, t:t + 1],
                                                 in1=xs, op0=ALU.mult, op1=ALU.add).then_inc(resid_done, 1)


def kernel(**inputs):
    import concourse.bacc as bacc
    from concourse.bass_utils import run_bass_kernel_spmd

    nc = bacc.Bacc("TRN2", target_bir_lowering=False, num_devices=1)
    arrays, aps = {}, {}
    for name, a in [*inputs.items(), *shape_tables().items()]:
        a = np.ascontiguousarray(a)
        arrays[f"in_{name}"] = a
        aps[name] = nc.dram_tensor(f"in_{name}", a.shape, mybir.dt.from_np(a.dtype), kind="ExternalInput").ap()
    out = nc.dram_tensor("out_0", (1, TOK, D), F32, kind="ExternalOutput").ap()
    build(nc, aps, out)
    return run_bass_kernel_spmd(nc, [arrays], core_ids=[0]).results[0]["out_0"]
```

```python
from contextlib import ExitStack
import math

import numpy as np
import concourse.bass as bass
from concourse import mybir

F32 = mybir.dt.float32
F32R = mybir.dt.float32r
BF16 = mybir.dt.bfloat16
ACT = mybir.ActivationFunctionType
ALU = mybir.AluOpType
AX_X = mybir.AxisListType.X

P = 128
TOK = 256
NT = TOK // P
D = 1024
KT = D // P
DH = 64
COLS = 512
UK = 4
RING = 4
FRING = 3
AHEAD = 3
SELF = 768
DFF = 4096
CHUNKS = DFF // COLS
FFN = 2816
FCHUNK = 256
FCHUNKS = FFN // FCHUNK
EPS = 1e-6
GN_EPS = 1e-5
NEG = -1e30
BELOW = -3.0e38
TAKEN = -3.4e38
TOPK = 64
CONSTS = 16 * 12
STATS = 340
Q_QB, Q_KA, Q_IK, Q_C = 16, 20, 21, 22
MAX8 = 8
LAM_INIT = 0.8 - 0.6 * math.exp(-0.3 * 0)
SCALE = DH ** -0.5
IDX_SCALE = 32 ** -0.5
IDX_W_SCALE = 4 ** -0.5
SMALL = 292

GAINS = ["a_mem_norm", "b_mem_norm", "a_norm_attn", "a_norm_mlp", "kv_norm", "b_norm_attn",
         "b_norm_mlp", "norm1_w_2", "final_norm", "norm2_w_2"]
FIRST = 3


def shape_tables():
    half = DH // 2
    pos = np.arange(TOK, dtype=np.float32)[:, None]
    a = np.arange(half, dtype=np.float32)
    ten = np.float32(10000.0)
    out = {}
    for name, inv in (("rope1", np.float32(1) / ten ** (a / np.float32(half))),
                      ("rope2", ten ** (-a / np.float32(half)))):
        ang = (pos * inv[None, :].astype(np.float32)).astype(np.float32)
        c, s = np.cos(ang), np.sin(ang)
        out[name] = np.concatenate([c, c, -s, s], axis=1).astype(np.float32)
    rel = np.arange(512) - 255
    n = np.abs(rel)
    nf = np.maximum(n, 1).astype(np.float32)
    large = 8 + (np.log(nf / np.float32(8)) / np.float32(math.log(16)) * np.float32(8)).astype(np.int32)
    bucket = np.where(rel > 0, 16, 0) + np.where(n < 8, n, np.minimum(large, 15))
    out["bucket_onehot"] = (np.arange(32)[:, None] == bucket[None, :]).astype(np.float32)
    log_g = np.log1p(-(2.0 ** (-5.0 - np.arange(8.0))))
    t = np.arange(TOK, dtype=np.float64)[:, None]
    out["decays"] = np.concatenate([np.exp(t * log_g), np.exp(-t * log_g) * SCALE], axis=1).astype(np.float32)
    return out


class Step:
    pass


def build(nc, A, out):
    UNITS = []

    def unit(w, rows, cols, nk=UK):
        n = sum(c for _, c in cols)
        view = lambda r, k, c0, c: w[r:r + P * k, c0:c0 + c].rearrange("(k p) n -> p k n", p=P)
        if len(cols) == 1:
            h = nk // 2
            parts = [(view(rows + P * h * i, h, cols[0][0], n), slice(h * i, h * i + h), slice(0, n))
                     for i in range(2)]
        else:
            at, parts = 0, []
            for c0, c in cols:
                parts.append((view(rows, nk, c0, c), slice(0, nk), slice(at, at + c)))
                at += c
        un = Step()
        un.n, un.nk, un.parts = n, nk, parts
        UNITS.append(un)
        return len(UNITS) - 1

    def chunk_units(w, cols):
        return [unit(w, h * UK * P, cols) for h in range(2)]

    STEPS = []
    count = Step()
    count.t, count.hi, count.chunk, count.s, count.o, count.item, count.resid = 0, 0, 0, 0, 0, 0, 0
    count.rstd, count.rope, count.exp, count.relu2, count.osq, count.ss = 0, 0, 0, 0, 0, 0
    count.decayed, count.w, count.dots = 0, 0, 0
    free = {}

    def add(kind):
        st = Step()
        st.kind = kind
        STEPS.append(st)
        return st

    ctx = ExitStack()
    with ctx:
        def sb(name, shape, dt=F32):
            return ctx.enter_context(nc.sbuf_tensor(name, shape, dt))

        def sem(name):
            return ctx.enter_context(nc.semaphore(name))

        raw = sb("raw", [P, RING, UK * COLS])
        whi = sb("whi", [P, RING, UK * COLS], F32R)
        wlo = sb("wlo", [P, RING, UK * COLS], F32R)
        x = sb("x", [P, NT, D])
        set_hi = [sb(f"set{i}_hi", [P, KT, TOK], F32R) for i in range(2)]
        set_lo = [sb(f"set{i}_lo", [P, KT, TOK], F32R) for i in range(2)]
        o_nat = sb("o_nat", [P, NT, D])
        zq = sb("zq", [P, 2, NT, COLS])
        rt = sb("rope_tmp", [P, 2, COLS])
        qk = sb("qk", [P, 24, TOK])
        v = sb("v", [P, NT, SELF])
        e = sb("e", [P, 2, COLS])
        wT = sb("wT", [P, 2, COLS])
        memkv = sb("memkv", [P, 2, COLS])
        rope1 = sb("rope1_sb", [P, NT, 4 * 32])
        rope2 = sb("rope2_sb", [P, NT, 4 * 32])
        ident = sb("ident", [P, P])
        identb = sb("identb", [P, P], BF16)
        cmask = sb("cmask", [P, P], BF16)
        flip = sb("flip", [P, P])
        tri = sb("tri", [P, P])
        gcol = sb("gcol", [P, len(GAINS) * KT])
        subln = sb("subln", [P, P])
        kvn = sb("kvn", [P, P])
        qkn = sb("qkn", [P, 2, DH])
        wukv = sb("wukv", [P, 2, DH])
        dec = sb("dec", [P, NT, 16])
        selmask = sb("selmask", [P, NT, TOK], BF16)
        stat = sb("stat", [P, STATS])
        newton = sb("newton", [P, 2, 16])
        minus_half = sb("minus_half", [P, 16])
        junk1 = sb("junk1", [P, P], BF16)
        rel8 = sb("rel8", [32, 8])
        mem_nat = o_nat
        hidden = zq[:, 0, :, :]
        zs = o_nat[:, 0, 0:2 * SMALL].rearrange("p (t n) -> p t n", t=2)
        sn = o_nat[:, 1, 0:768].rearrange("p (t b n) -> p t b n", t=2, b=3)
        relu_dots = wT[:, :, :].rearrange("p a b -> p (a b)").rearrange("p (h n) -> p h n", h=4)
        score = [o_nat[:, 0, 840:968], o_nat[:, 0, 584:840]]
        work = o_nat[:, 1, 768:1024]
        btoep = memkv[:, :, :].rearrange("p a b -> p (a b)").rearrange("p (h n) -> p h n", h=4)
        fgb = qk[:, 16:20, :].rearrange("p a b -> p (a b)")
        gn = zq[:, 0, :, :]
        junk = wT[:, :, :].rearrange("p a b -> p (a b)").bitcast(BF16).rearrange("p (t n) -> p t n", t=NT)
        lamrow = rt[:, 0, 0:256].rearrange("p (a b d) -> p a b d", a=2, b=2)
        lamprod = rt[:, 0, 256:384].rearrange("p (a d) -> p a d", a=2)
        onehot = e[0:32, 0, :]
        biasvec = e[0:8, 1, :]
        grow = [qk[0:len(group) * KT, 23 - i, 0:P] for i, group in enumerate((GAINS[:FIRST], GAINS[FIRST:]))]
        headq = qk[:, 0:16, :].rearrange("p (b c) n -> p b c n", c=2)

        ncol = [0]

        def col(n):
            ncol[0] += n
            assert ncol[0] <= STATS, ncol
            return stat[:, ncol[0] - n:ncol[0]]

        pb = lambda n: ctx.enter_context(nc.psum_tensor(n, [P, COLS], F32))
        Pb = [pb(f"proj{i}") for i in range(2)]
        Tb = [pb(f"turn{i}") for i in range(2)]
        Sb = [pb(f"score{i}") for i in range(2)]
        Ob = [pb(f"outp{i}") for i in range(2)]
        for i in range(2):
            for b in "PTSO":
                free[b, i] = None

        landed = [sem(f"unit_landed{i}") for i in range(RING)]
        hi_done = sem("hi_done")
        lo_done = sem("lo_done")
        mul_done = sem("mul_done")
        t_full = sem("t_full")
        t_hi = sem("t_hi")
        t_evac = sem("t_evac")
        chunk_evac = sem("chunk_evac")
        rope_done = sem("rope_done")
        s_full = sem("s_full")
        nmax_done = sem("nmax_done")
        exp_done = sem("exp_done")
        w_done = sem("w_done")
        o_full = sem("o_full")
        osq_done = sem("osq_done")
        o_evac = sem("o_evac")
        resid_done = sem("resid_done")
        ss_done = sem("ss_done")
        rstd_done = sem("rstd_done")
        relu_done = sem("relu_done")
        relu2_done = sem("relu2_done")
        silu_done = sem("silu_done")
        dots_done = sem("dots_done")
        dots_used = sem("dots_used")
        sel_done = sem("sel_done")
        kava_done = sem("kava_done")
        ka_done = sem("ka_done")
        sn_done = sem("sn_done")
        qn_done = sem("qn_done")
        qsq_done = sem("qsq_done")
        decayed = sem("decayed")
        decayed_used = sem("decayed_used")
        yc_done = sem("yc_done")
        ysq_done = sem("ysq_done")
        yn_done = sem("yn_done")
        ob_done = sem("ob_done")
        sum_done = sem("sum_done")
        inverse_done = sem("inverse_done")
        x_normed = sem("x_normed")
        dve_chain = sem("dve_chain")
        pool_chain = sem("pool_chain")
        heads_zeroed = sem("heads_zeroed")
        consts_made = sem("consts_made")
        mem_landed = [sem(f"mem_landed{i}") for i in range(2)]
        x_landed, consts_landed = sem("x_landed"), sem("consts_landed")
        gain_full, gain_cols = sem("gain_full"), sem("gain_cols")
        lam_sum, lam_exp, lam_done = sem("lam_sum"), sem("lam_exp"), sem("lam_done")
        gains_landed, gn_landed = [sem(f"gains_landed{i}") for i in range(2)], sem("gn_landed")
        bias_full, bias_vec, bias_stored = sem("bias_full"), sem("bias_vec"), sem("bias_stored")
        late_landed = sem("late_landed")
        stored = sem("stored")

        bias_dram = nc.dram_tensor("bias_by_distance", (8, 512), F32, kind="Internal").ap()

        def t_use():
            n = count.t
            count.t += 1
            return n

        def turn_operand(src, half, gains, ready, set_free, cols=None):
            st = add("turn_operand")
            st.src, st.half, st.gains, st.ready, st.set_free = src, half, gains, ready, set_free
            st.use, st.hi = [t_use(), t_use()], count.hi
            count.hi += 2
            return st.use

        split_next = [0]

        def split(u):
            while split_next[0] <= u:
                st = add("split")
                st.u = split_next[0]
                split_next[0] += 1

        def multiply(u, lhs, k0, use, bank, start, stop, hold=False, tiles=range(NT)):
            st = add("multiply")
            st.u, st.lhs, st.k0, st.use, st.bank, st.start = u, lhs, k0, use, bank, start
            st.stop, st.freed, st.tiles = stop, [free[bank, t] for t in range(NT)] if start else None, tiles
            if not hold:
                split(u + AHEAD)

        def multiply_around(action, *a):
            multiply(*a, hold=True, tiles=[0])
            done = action()
            multiply(*a, hold=True, tiles=[1])
            return done

        def half_around(action, us, h, lhs, use, bank="P"):
            done = multiply_around(action, us[h], lhs, UK * h, use, bank, h == 0, h == 1)
            split(us[h] + AHEAD)
            return done

        def evacuate(u, pieces, scale, slot_free=None, silu=False, bank="P"):
            st = add("evacuate")
            st.u, st.pieces, st.scale, st.chunk = u, pieces, scale, count.chunk
            st.slot_free, st.silu, st.bank = slot_free, silu, bank
            for t in range(NT):
                free[bank, t] = (chunk_evac, 2 * count.chunk + t + 1)
            count.chunk += 1
            return st

        def rope(slot, n, table):
            st = add("rope")
            st.slot, st.n, st.table, st.chunk, st.rope = slot, n, table, count.chunk, count.rope
            count.rope += 1
            return st

        def turn_heads(src, blocks, pieces, ready):
            st = add("turn_heads")
            st.src, st.blocks, st.pieces, st.ready = src, blocks, pieces, ready
            st.use = [t_use(), t_use()]
            return st.use

        LOW, HIGH, ALL = slice(0, DH), slice(DH, P), slice(0, P)
        tok = lambda t: slice(t * P, (t + 1) * P)

        def pairs(a, first, n):
            return [(ALL, slice(a, a + n), lambda t: qk[:, first:first + n, tok(t)])]

        def heads(a, first, n):
            return [(LOW, slice(a, a + n), lambda t: headq[LOW, first:first + n, 0, tok(t)]),
                    (HIGH, slice(a, a + n), lambda t: headq[HIGH, first:first + n, 1, tok(t)])]

        def s_use(release):
            n = count.s
            count.s += 1
            f = free["S", n % 2]
            free["S", n % 2] = release
            return n, f

        def o_use():
            n = count.o
            count.o += 1
            f = free["O", n % 2]
            free["O", n % 2] = (o_evac, n + 1)
            return n, f

        ITEMS = []

        def scores(kind, pair, t, q, k, need):
            it = Step()
            it.kind, it.pair, it.t, it.q, it.k, it.need = kind, pair, t, q, k, need
            it.n, it.buf, it.i, it.nm = P * (t + 1), len(ITEMS) % 2, len(ITEMS), col(2)
            it.rs, it.before = col(2), ITEMS[-2] if len(ITEMS) > 1 else None
            if kind == "mem":
                it.n = TOK
            if kind == "diff":
                both = (col(2), col(2)) if t == 0 else ITEMS[-1].both
                it.both, it.oss, it.ors = both, both[0][:, t:t + 1], both[1][:, t:t + 1]
            it.exp = count.exp
            count.exp += 1
            it.s, it.s_free = s_use((exp_done, it.exp + 1))
            ITEMS.append(it)
            st = add("scores")
            st.it = it
            return it

        def mix(it):
            count.w += 1
            it.w = count.w
            st = add("mix")
            st.it = it

        def turn_weights(it):
            it.use = t_use()
            st = add("turn_weights")
            st.it = it

        def attend(it, vneed):
            it.o, it.o_free = o_use()
            it.vneed = vneed
            if it.kind == "diff":
                count.osq += 1
                it.osq = count.osq
            st = add("attend")
            st.it = it
            return it.o + 1

        def norm(pair):
            st = add("diff_norm")
            st.items, (st.oss, st.ors) = pair, pair[0].both


        def residual(half, bank, u, scale):
            st = add("residual")
            st.half, st.bank, st.u, st.scale, st.r = half, bank, u, scale, count.resid
            count.resid += 2
            for t in range(NT):
                free[bank, t] = (resid_done, st.r + t + 1)
            return st

        def statistics(src, ready, factor=None, kind="plain"):
            st = add("statistics")
            st.src, st.ready, st.n, st.ss, st.rs = src, ready, count.rstd, col(2), col(2)
            st.what, st.factor = kind, factor
            if kind == "final":
                st.ss2, st.r2 = col(2), col(2)
            st.sums = count.ss
            count.ss += 2 if kind == "final" else 1
            count.rstd += 2 if kind == "final" else 1
            st.n_done = count.rstd
            return st

        g_at = lambda name: GAINS.index(name) * KT

        zfree = [None, None]
        gain_s = [s_use((gain_cols, 1))[0]]
        add("setup")
        memA = chunk_units(A["a_w_mem_kv"][0], [(0, 512)])
        w = A["a_w_in"][0]
        qk0 = chunk_units(w, [(0, 256), (SELF, 256)])
        vm = chunk_units(w, [(2 * SELF + 512, 512)])
        v0 = chunk_units(w, [(2 * SELF, 512)])
        qk1 = chunk_units(w, [(256, 256), (SELF + 256, 256)])
        qk2 = chunk_units(w, [(512, 256), (SELF + 512, 256)])

        def out_units(w, rows=(0, 512)):
            return [unit(w, r, [(c, COLS)]) for r in rows for c in (0, COLS)]

        def mul_chunk_half(us, h, lhs, uses, bank="P", mixed=()):
            multiply(us[h], lhs, UK * h, uses[h], bank, h == 0, h == 1, hold=True)
            for it in mixed:
                mix(it)
            split(us[h] + AHEAD)

        def turn_mem(name, h, free):
            return turn_operand(mem_nat, h, [(g_at(name), 1, UK * h)], (mem_landed[h], 16), free)[-1]

        def turn_x(h, name, s):
            return turn_operand(x, h, [(g_at(name), s, UK * h)], (x_landed, 16), None)[-1]

        m1 = [turn_mem("a_mem_norm", 0, None)]
        split(0)
        m1.append(multiply_around(lambda: turn_mem("a_mem_norm", 1, None), memA[0], 1, 0, m1[0], "P", True, False))
        split(2)
        rs_mem = statistics(mem_nat, (mem_landed[1], 16))
        x1 = [half_around(lambda: turn_x(0, "a_norm_attn", 0), memA, 1, 1, m1[1])]
        gain_s.append(s_use((gain_cols, 2))[0])
        bias_s = s_use((bias_vec, 1))
        constants = add("constants")
        constants.lam = col(5)

        def mem_pieces(slot):
            return [((0, 256), lambda t: zq[:, slot, t, 0:256]),
                    ((256, 512), lambda t: memkv[:, 1, t * 256:t * 256 + 256])]

        mk = memkv[:, 0, :].rearrange("p (b n) -> p b n", b=2)
        mem_keys = [(ALL, slice(0, 2), lambda t: mk[:, :, tok(t)])]

        def chunk_ready(ch):
            return lambda t: (chunk_evac, 2 * ch + t + 1)

        def rope_ready(r):
            return lambda t: (rope_done, 2 * r + t + 1)

        ev = evacuate(memA[1], mem_pieces(0), rs_mem)
        memV = (chunk_evac, 2)
        x1.append(half_around(lambda: turn_x(1, "a_norm_attn", 0), qk0, 0, 0, x1[0], "O"))
        rs_x = statistics(x, (x_landed, 16))
        mkA = turn_heads(zq[:, 0], [0, 1], mem_keys, chunk_ready(ev.chunk))[-1]
        zfree[0] = mkA + 1
        mB = [half_around(lambda: turn_mem("b_mem_norm", 0, 2 * memA[1] + 2), qk0, 1, 0, x1[1], "O")]
        evacuate(qk0[1], [((0, 512), lambda t: zq[:, 1, t, :])], rs_x, bank="O")
        r0 = rope(1, 512, rope1)
        mB.append(half_around(lambda: turn_mem("b_mem_norm", 1, 2 * memA[1] + 2), vm, 0, 0, x1[0]))
        mul_chunk_half(vm, 1, 0, x1)
        ev = evacuate(vm[1], [((0, 256), lambda t: v[:, t, 512:768]), ((256, 512), lambda t: zq[:, 0, t, 0:256])],
                      rs_x, slot_free=zfree[0])
        qk_pieces = lambda a: heads(0, a, 2) + pairs(2, 16 + a, 2)
        h_use = [turn_heads(zq[:, 1], [0, 1, 2, 3], qk_pieces(0), rope_ready(r0.rope))[-1]]
        zfree[1] = h_use[0] + 1

        def mem_item(p, t, qneed, kneed):
            return scores("mem", p, t, 6 + p, mk[:, p, :], max(qneed, kneed))

        def diff_item(h, t):
            return scores("diff", h, t, h, qk[:, 16 + h, :], h_use[h // 2])

        d = [diff_item(0, 0), diff_item(0, 1)]
        mul_chunk_half(v0, 0, 0, x1, mixed=(d[0], d[1]))
        qm_use = turn_heads(zq[:, 0], [0, 1], heads(0, 6, 2), chunk_ready(ev.chunk))[-1]
        zfree[0] = qm_use + 1
        turn_weights(d[0]); turn_weights(d[1])
        d += [diff_item(1, 0), diff_item(1, 1)]
        mul_chunk_half(v0, 1, 0, x1, mixed=(d[2], d[3]))
        ev = evacuate(v0[1], [((0, 512), lambda t: v[:, t, 0:512])], rs_x)
        vneed = (chunk_evac, 2 * ev.chunk + 2)
        mul_chunk_half(qk1, 0, 0, x1)
        attend(d[0], vneed); attend(d[1], vneed); turn_weights(d[2]); turn_weights(d[3])
        m = [mem_item(0, 0, qm_use, mkA), mem_item(0, 1, qm_use, mkA)]
        norm(d[0:2])
        mul_chunk_half(qk1, 1, 0, x1, mixed=m[0:2])
        evacuate(qk1[1], [((0, 512), lambda t: zq[:, 1, t, :])], rs_x, slot_free=zfree[1])
        r1 = rope(1, 512, rope1)
        attend(d[2], vneed); attend(d[3], vneed); turn_weights(m[0]); turn_weights(m[1])
        m += [mem_item(1, 0, qm_use, mkA), mem_item(1, 1, qm_use, mkA)]
        norm(d[2:4])
        mul_chunk_half(qk2, 0, 0, x1, mixed=m[2:4])
        attend(m[0], memV); attend(m[1], memV); turn_weights(m[2]); turn_weights(m[3])
        mul_chunk_half(qk2, 1, 0, x1)
        evacuate(qk2[1], [((0, 512), lambda t: zq[:, 0, t, :])], rs_x, slot_free=zfree[0])
        r2 = rope(0, 512, rope1)
        attend(m[2], memV); attend(m[3], memV)
        h_use.append(turn_heads(zq[:, 1], [0, 1, 2, 3], qk_pieces(2), rope_ready(r1.rope))[-1])
        zfree[1] = h_use[1] + 1
        d += [diff_item(2, 0), diff_item(2, 1)]
        memB = chunk_units(A["b_w_mem_kv"][0], [(0, 512)])
        mul_chunk_half(memB, 0, 1, mB, mixed=d[4:6])
        turn_weights(d[4]); turn_weights(d[5])
        d += [diff_item(3, 0), diff_item(3, 1)]
        h_use.append(turn_heads(zq[:, 0], [0, 1, 2, 3], qk_pieces(4), rope_ready(r2.rope))[-1])
        zfree[0] = h_use[2] + 1
        multiply(memB[1], 1, UK, mB[1], "P", False, True, hold=True, tiles=[0])
        mix(d[6]); mix(d[7])
        split(memB[1] + AHEAD)
        attend(d[4], vneed); attend(d[5], vneed); turn_weights(d[6]); turn_weights(d[7])
        d += [diff_item(4, 0), diff_item(4, 1)]
        norm(d[4:6])
        multiply(memB[1], 1, UK, mB[1], "P", False, True, hold=True, tiles=[1])
        mix(d[8]); mix(d[9])
        ev = evacuate(memB[1], mem_pieces(1), rs_mem, slot_free=zfree[1])
        memB_chunk = ev.chunk
        attend(d[6], vneed); o8 = attend(d[7], vneed); turn_weights(d[8]); turn_weights(d[9])
        d += [diff_item(5, 0), diff_item(5, 1)]
        norm(d[6:8])
        mkB = turn_heads(zq[:, 1], [0, 1], mem_keys, chunk_ready(ev.chunk))[-1]
        zfree[1] = mkB + 1

        def finish_attention(w, items, o_half, last_qset_unit, oset, gain, vneed):
            ua, ub, uc, ud = out_units(w)
            o1 = turn_operand(o_nat, 0, [(None, oset, 0)], (o_evac, o_half), 2 * last_qset_unit + 2)[-1]
            attend(items[0], vneed); attend(items[1], vneed)
            mix(items[2]); mix(items[3])
            if items[0].kind == "diff":
                norm(items[0:2])

            def weights():
                turn_weights(items[2]); turn_weights(items[3])

            multiply_around(weights, ua, oset, 0, o1, "P", True, False)
            attend(items[2], vneed)
            o_all = attend(items[3], vneed)
            split(ua + AHEAD)
            if items[0].kind == "diff":
                norm(items[2:4])
            o2 = multiply_around(lambda: turn_operand(o_nat, 1, [(None, oset, UK)], (o_evac, o_all), 0)[-1],
                                 ub, oset, 0, o1, "S", True, False)
            return out_tail(ub, (uc, oset, UK, o2), (ud, oset, UK, o2), 1 - oset, gain)

        def out_tail(u, third, fourth, xset, gain):
            multiply(*third, "P", False, True, hold=True)
            split(u + AHEAD)
            r = residual(0, "P", third[0], None)
            a = multiply_around(lambda: turn_operand(x, 0, [(gain, xset, 0)], (resid_done, r.r + 2), 0)[-1],
                                *fourth, "S", False, True)
            split(third[0] + AHEAD)
            return a, residual(1, "S", fourth[0], None)

        uses_a, r = finish_attention(A["a_w_out"][0], d[8:12], o8, qk2[1], 0, g_at("a_norm_mlp"), vneed)

        def mlp_units(w_up, w_down):
            base = len(UNITS)
            up = lambda j: [unit(w_up, h * UK * P, [(j * COLS, COLS)]) for h in range(2)]
            down = lambda j: [unit(w_down, j * COLS, [(c * COLS, COLS)]) for c in range(2)]
            up(0)
            for j in range(CHUNKS - 1):
                up(j + 1)
                down(j)
            down(CHUNKS - 1)
            return base

        def mlp(w_up, w_down, hset, use0, r1, gain):
            base = mlp_units(w_up, w_down)
            use1 = multiply_around(lambda: turn_operand(x, 1, [(gain, hset, UK)], (resid_done, r1.r + 2), 0)[-1],
                                   base, hset, 0, use0, "O", True, False)
            split(base + AHEAD)
            stt = statistics(x, (resid_done, r1.r + 2), kind="square")
            multiply(base + 1, hset, UK, use1, "O", False, True)
            for t in range(NT):
                free["O", t] = (relu2_done, count.relu2 + t + 1)
            st = add("mlp")
            st.base, st.hset, st.uset, st.t0, st.hi0 = base, hset, 1 - hset, count.t, count.hi
            st.relu0, st.freed = count.relu2, {b: [free[b, t] for t in range(NT)] for b in "PSO"}
            st.w = (w_up, w_down)
            split_next[0] += 4 * (CHUNKS - 1)
            count.t += 2 * CHUNKS
            count.hi += 2 * CHUNKS
            count.relu2 += 2 * CHUNKS
            for t in range(NT):
                free["P", t] = (relu2_done, count.relu2 - 1 + t)
            return stt, base

        def mlp_end(base, gain, scale):
            ul = base + 4 * CHUNKS - 2
            mlp_step = STEPS[-1]
            uset, xset = mlp_step.uset, mlp_step.hset
            multiply(ul, uset, 0, count.t - 1, "S", False, True)
            r0 = residual(0, "S", ul, scale)
            hidden_use = count.t - 1
            a = multiply_around(lambda: turn_operand(x, 0, [(gain, xset, 0)], (resid_done, r0.r + 2), 0)[-1],
                                ul + 1, uset, 0, hidden_use, "O", False, True)
            return a, residual(1, "O", ul + 1, scale), ul + 1

        sc, base = mlp(A["a_w_up"][0], A["a_w_down"][0], 1, uses_a, r, g_at("a_norm_mlp"))
        a0, r1, last = mlp_end(base, g_at("b_norm_attn"), sc)
        w, wkv = A["b_w_in"][0], A["w_kv"]
        q1 = chunk_units(w, [(512, 512)])
        q0 = chunk_units(w, [(0, 512)])
        k0 = chunk_units(wkv, [(0, 512)])
        kv1 = chunk_units(wkv, [(512, 512)])
        v1 = chunk_units(wkv, [(1024, 512)])
        a1 = multiply_around(lambda: turn_operand(x, 1, [(g_at("b_norm_attn"), 1, UK)], (resid_done, r1.r + 2), 0)[-1],
                             q1[0], 1, 0, a0, "P", True, False)
        split(q1[0] + AHEAD)
        xb = [a0, a1]
        rs_b = statistics(x, (resid_done, r1.r + 2))
        mul_chunk_half(q1, 1, 1, xb)
        evacuate(q1[1], [((0, 512), lambda t: zq[:, 1, t, :])], rs_b, slot_free=zfree[1])
        r1_ = rope(1, 256, rope1)
        mul_chunk_half(q0, 0, 1, xb, "O")
        xk = [turn_operand(x, h, [(g_at("kv_norm"), 0, UK * h)], (resid_done, r1.r + 2), 2 * last + 2)[-1]
              for h in range(2)]
        mul_chunk_half(q0, 1, 1, xb, "O")
        evacuate(q0[1], [((0, 512), lambda t: zq[:, 0, t, :])], rs_b, slot_free=zfree[0], bank="O")
        r0_ = rope(0, 512, rope1)
        qm_use = turn_heads(zq[:, 1], [0, 1, 2, 3], heads(0, 4, 4), rope_ready(r1_.rope))[-1]
        zfree[1] = qm_use + 1
        m = [mem_item(0, 0, qm_use, mkB), mem_item(0, 1, qm_use, mkB)]
        mul_chunk_half(k0, 0, 0, xk, mixed=(m[0], m[1]))
        turn_weights(m[0]); turn_weights(m[1])
        m += [mem_item(1, 0, qm_use, mkB), mem_item(1, 1, qm_use, mkB)]
        q_use = turn_heads(zq[:, 0], [0, 1, 2, 3], heads(0, 0, 4), rope_ready(r0_.rope))[-1]
        zfree[0] = q_use + 1
        memV = (chunk_evac, 2 * memB_chunk + 2)
        mix(m[2]); mix(m[3]); attend(m[0], memV); attend(m[1], memV); turn_weights(m[2]); turn_weights(m[3])
        mul_chunk_half(k0, 1, 0, xk)
        evacuate(k0[1], [((0, 512), lambda t: zq[:, 1, t, :])], rs_b, slot_free=zfree[1])
        r2_ = rope(1, 512, rope1)
        attend(m[2], memV); attend(m[3], memV)
        mul_chunk_half(kv1, 0, 0, xk)
        k_use = turn_heads(zq[:, 1], [0, 1, 2, 3], pairs(0, 16, 4), rope_ready(r2_.rope))[-1]
        zfree[1] = k_use + 1

        def causal_item(p, t):
            return scores("causal", p, t, p, qk[:, 16 + p, :], k_use if p < 4 else k2_use)

        c = [causal_item(0, 0), causal_item(0, 1)]
        mul_chunk_half(kv1, 1, 0, xk, mixed=(c[0], c[1]))
        ev = evacuate(kv1[1], [((0, 256), lambda t: zq[:, 0, t, 0:256]), ((256, 512), lambda t: v[:, t, 0:256])],
                      rs_b, slot_free=zfree[0])
        v_first = (chunk_evac, 2 * ev.chunk + 2)
        r3_ = rope(0, 256, rope1)
        turn_weights(c[0]); turn_weights(c[1])
        c += [causal_item(1, 0), causal_item(1, 1)]
        mul_chunk_half(v1, 0, 0, xk, mixed=(c[2], c[3]))
        k2_use = turn_heads(zq[:, 0], [0, 1], pairs(0, 20, 2), rope_ready(r3_.rope))[-1]
        zfree[0] = k2_use + 1
        attend(c[0], v_first); attend(c[1], v_first); turn_weights(c[2]); turn_weights(c[3])
        c += [causal_item(2, 0), causal_item(2, 1)]
        mul_chunk_half(v1, 1, 0, xk, mixed=(c[4], c[5]))
        ev = evacuate(v1[1], [((0, 512), lambda t: v[:, t, 256:768])], rs_b)
        v_all = (chunk_evac, 2 * ev.chunk + 2)
        attend(c[2], v_first); attend(c[3], v_first); turn_weights(c[4]); turn_weights(c[5])
        c += [causal_item(3, 0), causal_item(3, 1)]
        attend(c[4], v_all); attend(c[5], v_all)
        mix(c[6]); mix(c[7]); turn_weights(c[6]); turn_weights(c[7])
        c += [causal_item(4, 0), causal_item(4, 1)]
        attend(c[6], v_all); o8 = attend(c[7], v_all)
        mix(c[8]); mix(c[9]); turn_weights(c[8]); turn_weights(c[9])
        c += [causal_item(5, 0), causal_item(5, 1)]
        uses_a, r = finish_attention(A["b_w_out"][0], c[8:12], o8, q0[1], 1, g_at("b_norm_mlp"), v_all)
        st = add("late_loads")
        st.o, st.e = count.o, ITEMS[-1].exp + 1
        sc, base = mlp(A["b_w_up"][0], A["b_w_down"][0], 0, uses_a, r, g_at("b_norm_mlp"))

        a0, r1, _ = mlp_end(base, g_at("norm1_w_2"), sc)
        w = A["w_in_2"][0]
        sm = [unit(w, h * UK * P, [(512, SMALL)]) for h in range(2)]
        at = 512 + SMALL
        kb, qb, vb = (chunk_units(w, [(at + COLS * i, COLS)]) for i in (1, 0, 2))
        qa = chunk_units(w, [(0, 512)])
        gb = chunk_units(w, [(at + COLS * 3, COLS)])
        a1 = multiply_around(lambda: turn_operand(x, 1, [(g_at("norm1_w_2"), 0, UK)], (resid_done, r1.r + 2), 0)[-1],
                             sm[0], 0, 0, a0, "P", True, False)
        split(sm[0] + AHEAD)
        xb = [a0, a1]
        rs_2 = statistics(x, (resid_done, r1.r + 2), kind="final", factor=a1 + 1)
        mul_chunk_half(sm, 1, 0, xb)
        mul_chunk_half(kb, 0, 0, xb, "O")
        ev = evacuate(sm[1], [((0, SMALL), lambda t: zs[:, t, :])], rs_2)
        small = add("small_norm")
        small.chunk, small.ss, small.rs = ev.chunk, col(2), col(2)
        mul_chunk_half(kb, 1, 0, xb, "O")
        evacuate(kb[1], [((0, 512), lambda t: zq[:, 1, t, :])], rs_2, slot_free=zfree[1], bank="O")
        rk = rope(1, 512, rope2)
        mul_chunk_half(qb, 0, 0, xb)
        INDEX_BLOCK = [8, 10, 9, 11]
        index_q = lambda h: (lambda t: qk[32 * h:32 * h + 32, INDEX_BLOCK[h]:INDEX_BLOCK[h] + 1, tok(t)])
        sn_use = turn_heads(sn[:, :, :, :].rearrange("p t b n -> p t (b n)"), [0, 1, 2],
                            [(slice(32 * h, 32 * h + 32), slice(0, 1), index_q(h)) for h in range(4)] +
                            pairs(1, Q_IK, 2), lambda t: (sn_done, t + 1))[-1]

        def index_scores(t):
            n = P * (t + 1)
            per = COLS // n
            st = add("index_scores")
            st.t, st.n, st.per, st.use, st.banks, st.dots = t, n, per, sn_use, [], count.dots
            st.m8, st.ind = col(8), col(4)
            for b in range(4 // per):
                count.dots += 1
                st.banks.append(s_use((dots_done, count.dots)))
            return st

        def retention_scores(p):
            st = add("retention_scores")
            st.p, st.use, st.banks, st.before = p, max(kb_use, qb_use), [], ITEMS[-1].use
            for a in range(2):
                count.decayed += 1
                st.banks.append(s_use((decayed, count.decayed)))

        def retention_out(p):
            st = add("retention_out")
            st.p, st.ro, st.need = p, ro, vr_need

        def idx_item(p, t):
            return scores("idx", p, t, p, qk[:, Q_KA, :], max(ka_use, qa_use))

        def select(ix, first, last):
            st = add("select")
            st.st, st.rounds = ix, (first, last)

        def step(kind, of):
            add(kind).st = of

        mul_chunk_half(qb, 1, 0, xb)
        evacuate(qb[1], [((0, 512), lambda t: zq[:, 0, t, :])], rs_2, slot_free=zfree[0])
        i0 = index_scores(0)
        kava = add("shared_kv")
        kava.use, kava.s, kava.ss, kava.rs = sn_use, s_use((kava_done, 1)), col(2), col(2)
        step("index_sum", i0)
        step("shared_key_norm", kava)
        rq = rope(0, 512, rope2)
        mul_chunk_half(vb, 0, 0, xb, "O")
        i1 = index_scores(1)
        kb_use = turn_heads(zq[:, 1], [0, 1, 2, 3], heads(0, 4, 4), rope_ready(rk.rope))[-1]
        zfree[1] = kb_use + 1
        select(i0, 0, 2)
        mul_chunk_half(vb, 1, 0, xb, "O")
        ev = evacuate(vb[1], [((0, 512), lambda t: v[:, t, 0:512])], rs_2, bank="O")
        vr_need = (chunk_evac, 2 * ev.chunk + 2)
        select(i0, 2, 6)
        qb_use = turn_heads(zq[:, 0], [0, 1, 2, 3], pairs(0, Q_QB, 4), rope_ready(rq.rope))[-1]
        zfree[0] = qb_use + 1
        ro = [o_use() for _ in range(2)]
        retention_scores(0)
        mul_chunk_half(qa, 0, 0, xb)
        select(i0, 6, 8)
        ka_use = turn_heads(sn[:, :, 0, :].rearrange("p t n -> p t n"), [0], pairs(0, Q_KA, 1),
                            lambda t: (ka_done, t + 1))[-1]
        retention_out(0); retention_scores(1)
        step("index_sum", i1)
        mul_chunk_half(qa, 1, 0, xb)
        ev = evacuate(qa[1], [((0, 512), lambda t: zq[:, 0, t, :])], rs_2, slot_free=zfree[0])
        qn = add("query_norm")
        qn.chunk, qn.ss, qn.rs = ev.chunk, col(16), col(16)
        retention_out(1); retention_scores(2)
        select(i1, 0, 3)
        step("query_scale", qn)

        def third_pair():
            retention_out(2); retention_scores(3)

        half_around(third_pair, gb, 0, 0, xb[0])
        qa_use = turn_heads(zq[:, 0], [0, 1, 2, 3], heads(0, 0, 4), lambda t: (qn_done, t + 1))[-1]
        zfree[0] = qa_use + 1
        st = add("gain_load")
        st.free = zfree[0]
        select(i1, 3, 8)
        va_need = (kava_done, 1)

        def first_items():
            retention_out(3)
            return [idx_item(0, 0), idx_item(0, 1)]

        d = half_around(first_items, gb, 1, 0, xb[1])
        group = add("group_center")
        group.ro, group.mu, group.va, group.rs = ro, col(16), col(16), col(16)
        evacuate(gb[1], [((0, 512), lambda t: zq[:, 1, t, :])], rs_2, slot_free=zfree[1], silu=True)
        group.gate = (chunk_evac, 2 * count.chunk)
        mix(d[0]); mix(d[1]); turn_weights(d[0]); turn_weights(d[1])
        d += [idx_item(1, 0), idx_item(1, 1)]
        st = add("bias_load")
        st.s = d[-1].s
        attend(d[0], va_need); attend(d[1], va_need)
        mix(d[2]); mix(d[3]); turn_weights(d[2]); turn_weights(d[3])
        d += [idx_item(2, 0), idx_item(2, 1)]
        step("group_scale", group)
        attend(d[2], va_need); attend(d[3], va_need)
        mix(d[4]); mix(d[5]); turn_weights(d[4]); turn_weights(d[5])
        d += [idx_item(3, 0), idx_item(3, 1)]
        step("group_gate", group)
        ua, ub, uc, ud = out_units(A["w_out_2"][0], (512, 0))
        attend(d[4], va_need); attend(d[5], va_need)
        mix(d[6]); mix(d[7])
        o2 = turn_operand(o_nat, 1, [(None, 1, UK)], (ob_done, 2), 0)[-1]

        def last_weights():
            turn_weights(d[6]); turn_weights(d[7])

        multiply_around(last_weights, ua, 1, UK, o2, "P", True, False)
        attend(d[6], va_need)
        o_a = attend(d[7], va_need)
        split(ua + AHEAD)
        o1 = multiply_around(lambda: turn_operand(o_nat, 0, [(None, 1, 0)], (o_evac, o_a), 0)[-1],
                             ub, 1, UK, o2, "S", True, False)
        uses_a, r = out_tail(ub, (uc, 1, 0, o1), (ud, 1, 0, o1), 0, g_at("norm2_w_2"))

        fbase = len(UNITS)
        gate_up = lambda j: [unit_gate(j, h) for h in range(2)]

        def unit_gate(j, h):
            n = 2 * FCHUNK
            parts = [(A[nm][0][h * UK * P:(h + 1) * UK * P, j * FCHUNK:(j + 1) * FCHUNK]
                      .rearrange("(k p) n -> p k n", p=P), slice(0, UK), slice(i * FCHUNK, (i + 1) * FCHUNK))
                     for i, nm in enumerate(("w_gate_2", "w_up_2"))]
            un = Step()
            un.n, un.nk, un.parts = n, UK, parts
            UNITS.append(un)
            return len(UNITS) - 1

        def unit_fdown(j):
            return unit(A["w_down_2"][0], j * FCHUNK, [(0, D)], nk=2)

        gate_up(0)
        for j in range(FCHUNKS - 1):
            gate_up(j + 1)
            unit_fdown(j)
        unit_fdown(FCHUNKS - 1)
        use1 = multiply_around(lambda: turn_operand(x, 1, [(g_at("norm2_w_2"), 0, UK)], (resid_done, r.r + 2), 0)[-1],
                               fbase, 0, 0, uses_a, "O", True, False)
        split(fbase + AHEAD)
        rs_f = statistics(x, (resid_done, r.r + 2))
        multiply(fbase + 1, 0, UK, use1, "O", False, True)
        for t in range(NT):
            free["O", t] = (relu2_done, count.relu2 + t + 1)
        st = add("ffn")
        st.base, st.uset, st.hset, st.t0, st.hi0 = fbase, 1, 0, count.t, count.hi
        st.relu0, st.rs = count.relu2, rs_f
        st.freed = {b: [free[b, t] for t in range(NT)] for b in "PSO"}
        st = add("store")
        st.u, st.rs, st.r = len(UNITS) - 1, rs_f, count.resid

        N_UNITS = len(UNITS)
        slot, prev, fills = [], [], []
        owner, filled = [None] * RING, [0] * RING
        for u in range(N_UNITS):
            s = u % RING if u < fbase else (fbase + (u - fbase) % FRING) % RING
            slot.append(s)
            prev.append(owner[s])
            owner[s] = u
            filled[s] += 1
            fills.append(filled[s])
        assert fbase % RING == 0

        def shaped(buf, u):
            un = UNITS[u]
            return buf[:, slot[u], 0:un.nk * un.n].rearrange("p (k n) -> p k n", k=un.nk)

        out_rows = out[0].rearrange("(t p) n -> p t n", p=P)

        block = ctx.enter_context(nc.Block())

        @block.sync
        def _(sp):
            def load(u):
                if prev[u] is not None:
                    sp.wait_ge(hi_done, prev[u] + 1)
                    sp.wait_ge(lo_done, prev[u] + 1)
                dst = shaped(raw, u)
                for src, ks, cs in UNITS[u].parts:
                    sp.dma_start(dst[:, ks, cs], src).then_inc(landed[slot[u]], 16)

            def load_mlp(base, w_up, w_down):
                with sp.Fori(0, CHUNKS - 1) as j:
                    for c in range(4):
                        u = base + 2 + c
                        sp.wait_ge(hi_done, j * 4 + (prev[u] + 1))
                        sp.wait_ge(lo_done, j * 4 + (prev[u] + 1))
                        dst = shaped(raw, u)
                        for i in range(2):
                            if c < 2:
                                rows = (c * UK + 2 * i) * P
                                src = w_up[rows:rows + 2 * P, bass.ds(j * COLS + COLS, COLS)]
                            else:
                                src = w_down[bass.ds(j * COLS + 2 * i * P, 2 * P), (c - 2) * COLS:(c - 1) * COLS]
                            sp.dma_start(dst[:, 2 * i:2 * i + 2, :], src.rearrange("(k p) n -> p k n", p=P))\
                              .then_inc(landed[slot[u]], 16)

            def load_ffn(base):
                with sp.Fori(1, FCHUNKS - 2) as j:
                    for c in range(3):
                        u = base + 2 + 3 + c
                        sp.wait_ge(hi_done, j * 3 + (prev[u] + 1 - 3))
                        sp.wait_ge(lo_done, j * 3 + (prev[u] + 1 - 3))
                        dst = shaped(raw, u)
                        for i in range(2):
                            if c < 2:
                                wsrc = A[("w_gate_2", "w_up_2")[i]][0]
                                src = wsrc[c * UK * P:(c + 1) * UK * P, bass.ds(j * FCHUNK + FCHUNK, FCHUNK)]
                                d_ = dst[:, :, i * FCHUNK:(i + 1) * FCHUNK]
                            else:
                                src = A["w_down_2"][0][bass.ds(j * FCHUNK + i * P, P), :]
                                d_ = dst[:, i:i + 1, :]
                            sp.dma_start(d_, src.rearrange("(k p) n -> p k n", p=P)).then_inc(landed[slot[u]], 16)

            def load_gains(group):
                names = (GAINS[:FIRST], GAINS[FIRST:])[group]
                for i, g in enumerate(names):
                    g_ap = A[g] if len(A[g].shape) == 1 else A[g][0]
                    sp.dma_start(grow[group][i * KT:(i + 1) * KT, :], g_ap.rearrange("(k p) -> k p", p=P))\
                      .then_inc(gains_landed[group], 16)

            def load_constants():
                load_gains(1)
                def spread(dst, src):
                    sp.dma_start(dst, src.partition_broadcast(P)).then_inc(consts_landed, 16)
                spread(subln[:], A["a_subln"][0])
                sp.dma_start(rt[:, 0, 0:256], A["a_lambda"][0].rearrange("a d -> (a d)").partition_broadcast(P))\
                   .then_inc(consts_landed, 16)
                spread(kvn[:], A["kv_norm_w_2"][0])
                spread(qkn[:, 0, :], A["q_norm_w_2"][0])
                spread(qkn[:, 1, :], A["k_norm_w_2"][0])
                for dst, name in ((rope1, "rope1"), (rope2, "rope2"), (dec, "decays")):
                    sp.dma_start(dst[:], A[name].rearrange("(t p) n -> p t n", p=P)).then_inc(consts_landed, 16)
                sp.dma_start(onehot, A["bucket_onehot"]).then_inc(consts_landed, 16)
                sp.dma_start(rel8[:], A["rel_bias_2"]).then_inc(consts_landed, 16)
                sp.dma_start(wukv[:, 0, :], A["w_uk_2"][0]).then_inc(consts_landed, 16)
                sp.dma_start(wukv[:, 1, :], A["w_uv_2"][0]).then_inc(consts_landed, 16)

            mlps = {st.base: st.w for st in STEPS if st.kind == "mlp"}
            load_gains(0)

            def load_memory(h):
                cols = slice(h * COLS, (h + 1) * COLS)
                sp.dma_start(mem_nat[:, :, cols], A["mem"][0][:, cols].rearrange("(t p) n -> p t n", p=P))\
                  .then_inc(mem_landed[h], 16)

            load_memory(0)
            u = 0
            while u < N_UNITS:
                if u == 1:
                    load_memory(1)
                if u == 2:
                    sp.dma_start(x[:], A["x"][0].rearrange("(t p) n -> p t n", p=P)).then_inc(x_landed, 16)
                if u == RING:
                    load_constants()
                if u - 2 in mlps:
                    load_mlp(u - 2, *mlps[u - 2])
                    u += 4 * (CHUNKS - 1)
                elif u == fbase + 5:
                    load_ffn(fbase)
                    u += 3 * (FCHUNKS - 3)
                else:
                    load(u)
                    u += 1
            last = STEPS[-1]
            for i, (half, t) in enumerate((c, t) for c in range(2) for t in range(NT)):
                sp.wait_ge(resid_done, last.r + i + 1)
                sp.dma_start(out_rows[:, t, half * COLS:(half + 1) * COLS], x[:, t, half * COLS:(half + 1) * COLS])\
                  .then_inc(stored, 16)
            sp.wait_ge(stored, 16 * 4)

        @block.gpsimd
        def _(pool):
            chain = [0]

            def behind(ins):
                chain[0] += 1
                ins.then_inc(pool_chain, 1)
                pool.wait_ge(pool_chain, chain[0])

            def inverse_rms(dst, ss, n, eps=EPS):
                width = dst.shape[1]
                var, r2 = newton[:, 0, 0:width], newton[:, 1, 0:width]
                behind(pool.tensor_scalar(var, ss, 1.0 / n, eps, ALU.mult, ALU.add))
                behind(pool.tensor_tensor(dst, var, minus_half[:, 0:width], ALU.pow))
                behind(pool.tensor_tensor(r2, dst, dst, ALU.mult))
                behind(pool.tensor_tensor(r2, r2, var, ALU.mult))
                behind(pool.tensor_scalar(r2, r2, -0.5, 1.5, ALU.mult, ALU.add))
                return pool.tensor_tensor(dst, dst, r2, ALU.mult)

            sums = [0]

            def inverse_of_sums(dst, ss, n, eps=EPS):
                sums[0] += 1
                pool.wait_ge(sum_done, sums[0])
                inverse_rms(dst, ss, n, eps).then_inc(inverse_done, 1)

            def do_rope(st):
                nh = st.n // DH
                for t in range(NT):
                    pool.wait_ge(chunk_evac, 2 * (st.chunk - 1) + t + 1)
                    if st.rope or t:
                        pool.wait_ge(rope_done, 2 * st.rope + t)
                    z = zq[:, st.slot, t, 0:st.n].rearrange("p (h d) -> p h d", d=DH)
                    zh = zq[:, st.slot, t, 0:st.n].rearrange("p (h x d) -> p h x d", x=2, d=DH // 2)
                    t1 = rt[:, 0, 0:st.n].rearrange("p (h d) -> p h d", d=DH)
                    t2 = rt[:, 1, 0:st.n].rearrange("p (h x d) -> p h x d", x=2, d=DH // 2)
                    cos = st.table[:, t, 0:64].unsqueeze(1).broadcast_to([P, nh, DH])
                    pool.tensor_tensor(t1, z, cos, ALU.mult)
                    for i in range(2):
                        sin = st.table[:, t, 64 + 32 * i:96 + 32 * i].unsqueeze(1).broadcast_to([P, nh, DH // 2])
                        last = pool.tensor_tensor(t2[:, :, i, :], zh[:, :, 1 - i, :], sin, ALU.mult)
                    behind(last)
                    pool.tensor_tensor(zq[:, st.slot, t, 0:st.n], rt[:, 0, 0:st.n], rt[:, 1, 0:st.n], ALU.add)\
                        .then_inc(rope_done, 1)

            for st in STEPS:
                if st.kind == "setup":
                    behind(pool.memset(ident[:], 0.0))
                    pool.affine_select(out=ident[:], in_=ident[:], compare_op=ALU.not_equal, fill=1.0, base=0,
                                       pattern=[[-1, P]], channel_multiplier=1).then_inc(consts_made, 1)
                    pool.memset(minus_half[:], -0.5)
                    pool.memset(tri[:], 1.0)
                    pool.memset(flip[:], 0.0)
                    pool.memset(identb[:], 0.0)
                    behind(pool.memset(cmask[:], 0.0))
                    pool.affine_select(out=identb[:], in_=identb[:], compare_op=ALU.not_equal, fill=1.0, base=0,
                                       pattern=[[-1, P]], channel_multiplier=1).then_inc(consts_made, 1)
                    pool.affine_select(out=flip[:], in_=flip[:], compare_op=ALU.not_equal, fill=1.0 / SCALE,
                                       base=1 - P, pattern=[[1, P]], channel_multiplier=1).then_inc(consts_made, 1)
                    pool.affine_select(out=cmask[:], in_=cmask[:], compare_op=ALU.is_ge, fill=NEG, base=0,
                                       pattern=[[-1, P]], channel_multiplier=1).then_inc(consts_made, 1)
                    pool.affine_select(out=tri[:], in_=tri[:], compare_op=ALU.is_ge, fill=0.0, base=0,
                                       pattern=[[1, P]], channel_multiplier=-1).then_inc(consts_made, 1)
                    pool.memset(qk[:, 0:16, :], 0.0).then_inc(heads_zeroed, 1)
                elif st.kind == "constants":
                    pool.wait_ge(bias_vec, 1)
                    pool.dma_start(bias_dram, biasvec).then_inc(bias_stored, 16)
                    pool.wait_ge(lam_done, 1)
                elif st.kind == "rope":
                    do_rope(st)
                elif st.kind == "statistics":
                    pool.wait_ge(ss_done, st.sums + 1)
                    ins = inverse_rms(st.rs, st.ss, D)
                    if st.what == "square":
                        behind(ins)
                        ins = pool.tensor_tensor(st.rs, st.rs, st.rs, ALU.mult)
                    ins.then_inc(rstd_done, 1)
                    if st.what == "final":
                        pool.wait_ge(ss_done, st.sums + 2)
                        behind(inverse_rms(st.r2, st.ss2, D))
                        pool.tensor_tensor(st.rs, st.rs, st.r2, ALU.mult).then_inc(rstd_done, 1)
                elif st.kind == "diff_norm":
                    pool.wait_ge(osq_done, st.items[1].osq)
                    inverse_rms(st.ors, st.oss, P).then_inc(inverse_done, 1)
                elif st.kind == "late_loads":
                    pool.wait_ge(o_evac, st.o)
                    pool.memset(qk[:, 0:16, :], 0.0).then_inc(heads_zeroed, 1)
                elif st.kind == "query_norm":
                    for t in range(NT):
                        pool.wait_ge(chunk_evac, 2 * st.chunk + t + 1)
                        pool.tensor_tensor(rt[:, t, :], zq[:, 0, t, :], zq[:, 0, t, :], ALU.mult).then_inc(qsq_done, 1)
                    inverse_of_sums(st.rs, st.ss, DH)
                elif st.kind == "small_norm":
                    inverse_of_sums(st.rs, st.ss, P)
                elif st.kind == "shared_key_norm":
                    inverse_of_sums(st.st.rs, st.st.ss, DH)
                elif st.kind == "group_center":
                    for t in range(NT):
                        pool.wait_ge(yc_done, t + 1)
                        y = o_nat[:, t, 512:1024]
                        pool.tensor_tensor(rt[:, t, :], y, y, ALU.mult).then_inc(ysq_done, 1)
                elif st.kind == "group_scale":
                    inverse_of_sums(st.st.rs, st.st.va, DH, GN_EPS)
                elif st.kind == "group_gate":
                    y = o_nat[:, 0, 512:1024]
                    pool.wait_ge(yn_done, 1)
                    pool.wait_ge(*st.st.gate)
                    pool.wait_ge(gn_landed, 32)
                    behind(pool.tensor_tensor(y, y, gn[:, 0, :], ALU.mult))
                    behind(pool.tensor_tensor(y, y, gn[:, 1, :], ALU.add))
                    pool.tensor_tensor(y, y, zq[:, 1, 0, :], ALU.mult).then_inc(ob_done, 1)

        @block.scalar
        def _(act):
            def split_hi(u):
                if u >= N_UNITS:
                    return
                act.wait_ge(landed[slot[u]], 32 * fills[u])
                if prev[u] is not None:
                    act.wait_ge(mul_done, 2 * prev[u] + 2)
                act.activation(shaped(whi, u), shaped(raw, u), ACT.Copy).then_inc(hi_done, 1)

            def split_hi_loop(u, j, j0, per):
                act.wait_ge(landed[slot[u]], j * 32 + (32 * fills[u] - 32 * j0))
                act.wait_ge(mul_done, j * (2 * per) + (2 * prev[u] + 2 - 2 * per * j0))
                act.activation(shaped(whi, u), shaped(raw, u), ACT.Copy).then_inc(hi_done, 1)

            def mlp_chunk(st, j, peel, last=False):
                u0 = st.base + 2 + AHEAD + (4 * peel)
                one = (lambda u: split_hi(u)) if isinstance(j, int) else (lambda u: split_hi_loop(u, j, peel, 4))
                one(u0)
                hidden_hi(st, j, UK, 2)
                one(u0 + 1)
                relu(j * 8 + (2 * st.base + 6))
                one(u0 + 2)
                if last:
                    hidden_hi(st, j + 1, 0, 2)
                one(u0 + 3)

            def relu(multiplied, bank=Pb):
                for t in range(NT):
                    act.wait_ge(mul_done, multiplied + (t + 1))
                    act.activation(hidden[:, t, :], bank[t][:], ACT.Relu).then_inc(relu_done, 1)

            def ffn_chunk(st, j, peel):
                u0 = st.base + 2 + AHEAD + 3 * peel
                one = (lambda u: split_hi(u)) if isinstance(j, int) else (lambda u: split_hi_loop(u, j, peel, 3))
                one(u0)
                hidden_hi(st, j, 0, 1)
                one(u0 + 1)
                silu(st, j * 6 + (2 * st.base + 6))
                one(u0 + 2)

            def hidden_hi(st, j, k0, per):
                for b in range(2):
                    act.wait_ge(t_full, j * 2 + (st.t0 + b + 1))
                    k = k0 + per * b
                    act.activation(set_hi[st.uset][:, k:k + per, :], Tb[(st.t0 + b) % 2][:, 0:per * TOK], ACT.Copy)\
                       .then_inc(t_hi, 1)

            def silu(st, multiplied, bank=Pb):
                for t in range(NT):
                    act.wait_ge(mul_done, multiplied + (t + 1))
                    act.activation(zq[:, 1, t, 0:FCHUNK], bank[t][:, 0:FCHUNK], ACT.Silu, scale=st.rs.rs[:, t:t + 1])\
                       .then_inc(silu_done, 1)

            def biases(h):
                return bass.AP(bias_dram.tensor, h * 512, [[1, P], [512, 4], [1, TOK]])

            banks = {"P": Pb, "S": Sb, "O": Ob}

            for st in STEPS:
                if st.kind == "constants":
                    act.wait_ge(lam_sum, 1)
                    act.activation(st.lam[:, 2:4], st.lam[:, 0:2], ACT.Exp).then_inc(lam_exp, 1)
                elif st.kind == "split":
                    split_hi(st.u)
                elif st.kind == "statistics":
                    act.wait_ge(*st.ready)
                    if st.src is mem_nat:
                        act.wait_ge(mem_landed[0], 16)
                    for r, ss in enumerate([st.ss, st.ss2] if st.what == "final" else [st.ss]):
                        if r:
                            act.wait_ge(x_normed, 1)
                        for t in range(NT):
                            ins = act.activation(junk[:, t, :], st.src[:, t, :], ACT.Square, accum_out=ss[:, t:t + 1])
                        ins.then_inc(ss_done, 1)
                elif st.kind == "turn_operand":
                    for b in range(2):
                        n = st.use[b]
                        act.wait_ge(t_full, n + 1)
                        if st.set_free and b == 0:
                            act.wait_ge(mul_done, st.set_free)
                        for g, s, k0 in st.gains:
                            k = k0 + 2 * b
                            if g is None:
                                ins = act.activation(set_hi[s][:, k:k + 2, :], Tb[n % 2][:], ACT.Copy)
                            else:
                                kk = 4 * st.half + 2 * b
                                act.wait_ge(gain_cols, 1 if g < FIRST * KT else 3)
                                for i in range(2):
                                    ins = act.activation(set_hi[s][:, k + i, :], Tb[n % 2][:, i * TOK:(i + 1) * TOK],
                                                         ACT.Copy, scale=gcol[:, g + kk + i:g + kk + i + 1])
                        ins.then_inc(t_hi, 1)
                elif st.kind == "evacuate":
                    act.wait_ge(rstd_done, st.scale.n_done)
                    for t in range(NT):
                        act.wait_ge(mul_done, 2 * st.u + t + 1)
                        if st.slot_free and t == 0:
                            act.wait_ge(t_full, st.slot_free)
                        for i, ((a, b), dst) in enumerate(st.pieces):
                            ins = act.activation(dst(t), banks[st.bank][t][:, a:b], ACT.Silu if st.silu else ACT.Copy,
                                                 scale=st.scale.rs[:, t:t + 1])
                        ins.then_inc(chunk_evac, 1)
                elif st.kind == "scores":
                    it = st.it
                    act.wait_ge(nmax_done, it.i + 1)
                    if it.i == 0:
                        act.wait_ge(bias_stored, 16)
                    if it.kind == "idx" and it.pair == 0:
                        act.wait_ge(o_full, ro[1][0] + 1)
                    elif it.before:
                        act.wait_ge(t_full, it.before.use + 1)
                    for c in range(2):
                        dst = e[:, it.buf, c * it.n:(c + 1) * it.n]
                        src = Sb[it.s % 2][:, c * it.n:(c + 1) * it.n]
                        ins = act.activation(dst, src, ACT.Exp, bias=it.nm[:, c:c + 1], scale=SCALE,
                                             accum_out=it.rs[:, c:c + 1])
                    ins.then_inc(exp_done, 1)
                elif st.kind == "attend":
                    it = st.it
                    if it.kind == "diff":
                        act.wait_ge(o_full, it.o + 1)
                        if it.osq > 1:
                            act.wait_ge(osq_done, it.osq - 1)
                        act.activation(junk1[:], Ob[it.o % 2][:, 0:P], ACT.Square, accum_out=it.oss).then_inc(osq_done, 1)
                elif st.kind == "late_loads":
                    act.wait_ge(o_evac, st.o)
                    act.dma_start(fgb, A["final_norm"].partition_broadcast(P)).then_inc(late_landed, 16)
                    act.dma_start(btoep, biases(0)).then_inc(late_landed, 16)
                elif st.kind == "bias_load":
                    act.wait_ge(s_full, st.s + 1)
                    act.dma_start(btoep, biases(4)).then_inc(late_landed, 16)
                elif st.kind == "gain_load":
                    act.wait_ge(t_full, st.free)
                    for i, g in enumerate(("ret_gn_w_2", "ret_gn_b_2")):
                        act.dma_start(gn[:, i, :], A[g][0].partition_broadcast(P)).then_inc(gn_landed, 16)
                elif st.kind == "index_scores":
                    for b in range(4 // st.per):
                        s = st.banks[b][0]
                        act.wait_ge(s_full, s + 1)
                        if st.t == 1 and b == 0:
                            act.wait_ge(dots_used, 1)
                        act.activation(relu_dots[:, b * st.per:(b + 1) * st.per, 0:st.n],
                                       Sb[s % 2][:, 0:st.per * st.n].rearrange("p (h n) -> p h n", h=st.per),
                                       ACT.Relu, scale=IDX_SCALE).then_inc(dots_done, 1)
                elif st.kind == "shared_kv":
                    s = st.s[0]
                    act.wait_ge(s_full, s + 1)
                    for t in range(NT):
                        act.activation(sn[:, t, 1, 0:DH], Sb[s % 2][:, t * P:t * P + DH], ACT.Copy)
                        ins = act.activation(v[:, t, 512:512 + DH], Sb[s % 2][:, t * P + DH:t * P + P], ACT.Copy)
                    ins.then_inc(kava_done, 1)
                elif st.kind == "mlp":
                    relu(2 * (st.base + 1), Ob)
                    mlp_chunk(st, 0, 0)
                    with act.Fori(1, CHUNKS - 2) as j:
                        mlp_chunk(st, j, 1)
                    mlp_chunk(st, CHUNKS - 2, CHUNKS - 2, last=True)
                elif st.kind == "ffn":
                    act.wait_ge(rstd_done, st.rs.n_done)
                    silu(st, 2 * (st.base + 1), Ob)
                    ffn_chunk(st, 0, 0)
                    with act.Fori(1, FCHUNKS - 2) as j:
                        ffn_chunk(st, j, 1)
                    ffn_chunk(st, FCHUNKS - 2, FCHUNKS - 2)
                    hidden_hi(st, FCHUNKS - 1, 2, 1)

        @block.tensor
        def _(pe):
            def wait(pair):
                if pair is not None:
                    pe.wait_ge(*pair)

            def products(out_, hi, lo, wh, wl, start, stop):
                pe.matmul(out_, hi, wh, start=start, stop=False)
                pe.matmul(out_, hi, wl, start=False, stop=False)
                return pe.matmul(out_, lo, wh, start=False, stop=stop)

            def half_unit(u, t, lhs, k0, out_, start, stop):
                n = UNITS[u].n
                wh, wl = shaped(whi, u), shaped(wlo, u)
                for k in range(UK):
                    ins = products(out_[:, 0:n], set_hi[lhs][:, k0 + k, tok(t)], set_lo[lhs][:, k0 + k, tok(t)],
                                   wh[:, k, :], wl[:, k, :], start and k == 0, stop and k == UK - 1)
                ins.then_inc(mul_done, 1)

            banks = {"P": Pb, "S": Sb, "O": Ob}

            def turn_gains(group):
                n = (FIRST, len(GAINS) - FIRST)[group] * KT
                pe.wait_ge(gains_landed[group], 16 * (n // KT))
                if group:
                    pe.wait_ge(gain_cols, 1)
                pe.transpose(Sb[gain_s[group] % 2][:, 0:n], grow[group], ident[0:n, 0:n]).then_inc(s_full, 1)

            def turn_bank(n, src, tiles):
                for i, k in enumerate(tiles):
                    for t in range(NT):
                        at = (i * NT + t) * P
                        ins = pe.transpose(Tb[n % 2][:, at:at + P], src(t, k), ident[:])
                ins.then_inc(t_full, 1)

            def hidden_block(t, k):
                return hidden[:, t, k * P:(k + 1) * P]

            def mlp_chunk(st, j, peel, first, last=False):
                u0 = st.base + 2 + 4 * peel
                at = lambda base, per: j * per + (base - per * peel)
                for h in range(2):
                    u = u0 + h
                    pe.wait_ge(lo_done, at(u + 1, 4))
                    for t in range(NT):
                        if h == 0 and first:
                            wait(st.freed["P"][t])
                        elif h == 0:
                            pe.wait_ge(relu2_done, at(st.relu0 + 2 * peel + t + 1, 2))
                        half_unit(u, t, st.hset, UK * h, Pb[t], h == 0, h == 1)
                    if h == 0:
                        hidden_turns(st, j)
                pe.wait_ge(t_evac, j * 2 + (st.t0 + 2))
                for c, b in enumerate("SO"):
                    u = u0 + 2 + c
                    pe.wait_ge(lo_done, at(u + 1, 4))
                    for t in range(NT):
                        if first:
                            wait(st.freed[b][t])
                        half_unit(u, t, st.uset, UK, banks[b][t], first, False)
                    if last and c == 0:
                        hidden_turns(st, j + 1)

            def hidden_turns(st, j):
                pe.wait_ge(relu2_done, j * 2 + (st.relu0 + 2))
                for b in range(2):
                    pe.wait_ge(t_evac, j * 2 + (st.t0 + b - 1))
                    turn_bank(st.t0 + b, hidden_block, [2 * b, 2 * b + 1])

            def ffn_down(st, u, k0, first, last, between=None):
                wh, wl = shaped(whi, u), shaped(wlo, u)
                for c, b in enumerate("SO"):
                    for t in range(NT):
                        if first:
                            wait(st.freed[b][t])
                        for k in range(2):
                            cs = slice(c * COLS, (c + 1) * COLS)
                            ins = products(banks[b][t][:], set_hi[st.uset][:, k0 + k, tok(t)],
                                           set_lo[st.uset][:, k0 + k, tok(t)],
                                           wh[:, k, cs], wl[:, k, cs], first and k == 0, last and k == 1)
                        if last or c == 1:
                            ins.then_inc(mul_done, 1)
                    if between and c == 0:
                        between()

            def ffn_turns(st, j):
                pe.wait_ge(relu2_done, j * 2 + (st.relu0 + 2))
                for b in range(2):
                    pe.wait_ge(t_evac, j * 2 + (st.t0 + b - 1))
                    turn_bank(st.t0 + b, hidden_block, [b])

            def ffn_chunk(st, j, peel, first, between=None):
                u0 = st.base + 2 + 3 * peel
                at = lambda base, per: j * per + (base - per * peel)
                for h in range(2):
                    u = u0 + h
                    pe.wait_ge(lo_done, at(u + 1, 3))
                    for t in range(NT):
                        if h == 0 and first:
                            wait(st.freed["P"][t])
                        elif h == 0:
                            pe.wait_ge(relu2_done, at(st.relu0 + 2 * peel + t + 1, 2))
                        half_unit(u, t, st.hset, UK * h, Pb[t], h == 0, h == 1)
                    if h == 0:
                        ffn_turns(st, j)
                pe.wait_ge(t_evac, j * 2 + (st.t0 + 2))
                pe.wait_ge(lo_done, at(u0 + 3, 3))
                ffn_down(st, u0 + 2, 0, first, False, between)

            for st in STEPS:
                if st.kind == "setup":
                    pe.wait_ge(consts_made, 1)
                    turn_gains(0)
                elif st.kind == "constants":
                    pe.wait_ge(consts_made, 5)
                    turn_gains(1)
                    pe.wait_ge(consts_landed, CONSTS)
                    pe.matmul(Sb[bias_s[0] % 2][0:8, :], rel8[:], onehot, start=True, stop=True).then_inc(s_full, 1)
                elif st.kind == "turn_operand":
                    wait(st.ready)
                    for b in range(2):
                        n = st.use[b]
                        if n >= 2:
                            pe.wait_ge(t_evac, n - 1)
                        k0 = UK * st.half + 2 * b
                        turn_bank(n, lambda t, k: st.src[:, t, k * P:(k + 1) * P], [k0, k0 + 1])
                elif st.kind == "multiply":
                    pe.wait_ge(t_evac, st.use + 1)
                    pe.wait_ge(lo_done, st.u + 1)
                    for t in st.tiles:
                        if st.start:
                            wait(st.freed[t])
                        half_unit(st.u, t, st.lhs, st.k0, banks[st.bank][t], st.start, st.stop)
                elif st.kind == "turn_heads":
                    for t in range(NT):
                        n = st.use[t]
                        pe.wait_ge(*st.ready(t))
                        pe.wait_ge(t_evac, n - 1)
                        for i, b in enumerate(st.blocks):
                            ins = pe.transpose(Tb[n % 2][:, i * P:(i + 1) * P], st.src[:, t, b * P:(b + 1) * P],
                                               ident[:])
                        ins.then_inc(t_full, 1)
                elif st.kind == "scores":
                    it = st.it
                    pe.wait_ge(t_evac, it.need + 1)
                    wait(it.s_free)
                    if it.kind == "idx":
                        pe.wait_ge(sel_done, it.t + 1)
                        pe.wait_ge(late_landed, 32 if it.pair < 2 else 48)
                    S = Sb[it.s % 2]
                    for c in range(2):
                        o = c * it.n
                        ins = pe.matmul(S[:, o:o + it.n], headq[:, it.q, c, tok(it.t)], it.k[:, 0:it.n],
                                        start=True, stop=it.kind == "mem")
                        if it.kind == "idx":
                            c0 = P - P * it.t
                            pe.matmul(S[:, o:o + it.n], flip[:], btoep[:, 2 * it.pair % 4 + c, c0:c0 + it.n],
                                      start=False, stop=False)
                            ins = pe.matmul(S[:, o:o + it.n], identb[:], selmask[:, it.t, 0:it.n],
                                            start=False, stop=True)
                        elif it.kind != "mem":
                            ins = pe.matmul(S[:, o + it.n - P:o + it.n], identb[:], cmask[:], start=False, stop=True)
                    ins.then_inc(s_full, 1)
                elif st.kind == "turn_weights":
                    it = st.it
                    if it.kind == "diff":
                        pe.wait_ge(w_done, it.w)
                    else:
                        pe.wait_ge(exp_done, it.exp + 1)
                    pe.wait_ge(t_evac, it.use - 1)
                    nb = it.n // P * (1 if it.kind == "diff" else 2)
                    for b in range(nb):
                        ins = pe.transpose(Tb[it.use % 2][:, b * P:(b + 1) * P], e[:, it.buf, b * P:(b + 1) * P],
                                           ident[:])
                    ins.then_inc(t_full, 1)
                elif st.kind == "attend":
                    it = st.it
                    pe.wait_ge(t_evac, it.use + 1)
                    wait(it.o_free)
                    pe.wait_ge(*it.vneed)
                    nk = it.n // P
                    O = Ob[it.o % 2]
                    for c in range(1 if it.kind == "diff" else 2):
                        for k in range(nk):
                            b = c * nk + k
                            wt = wT[:, it.buf, b * P:(b + 1) * P]
                            h = 2 * it.pair + c
                            dst = O[:, c * DH:(c + 1) * DH]
                            if it.kind == "diff":
                                val, dst = v[:, k, it.pair * P:(it.pair + 1) * P], O[:, 0:P]
                            elif it.kind == "mem":
                                val = memkv[:, 1, k * 256 + h * DH:k * 256 + (h + 1) * DH]
                            elif it.kind == "causal":
                                val = v[:, k, h * DH:(h + 1) * DH]
                            else:
                                val = v[:, k, 512:512 + DH]
                            ins = pe.matmul(dst, wt, val, start=k == 0, stop=k == nk - 1)
                    ins.then_inc(o_full, 1)
                elif st.kind == "mlp":
                    mlp_chunk(st, 0, 0, True)
                    with pe.Fori(1, CHUNKS - 2) as j:
                        mlp_chunk(st, j, 1, False)
                    mlp_chunk(st, CHUNKS - 2, CHUNKS - 2, False, last=True)
                elif st.kind == "index_scores":
                    pe.wait_ge(t_evac, st.use + 1)
                    for b, (s, freed) in enumerate(st.banks):
                        wait(freed)
                        for i in range(st.per):
                            h = b * st.per + i
                            ins = pe.matmul(Sb[s % 2][:, i * st.n:(i + 1) * st.n], qk[:, INDEX_BLOCK[h], tok(st.t)],
                                            qk[:, Q_IK, 0:st.n], start=True, stop=True)
                        ins.then_inc(s_full, 1)
                elif st.kind == "shared_kv":
                    pe.wait_ge(t_evac, st.use + 1)
                    s, freed = st.s
                    wait(freed)
                    for t in range(NT):
                        ins = pe.matmul(Sb[s % 2][:, tok(t)], qk[:, Q_C, tok(t)],
                                        wukv[:, :, :].rearrange("p a b -> p (a b)"), start=True, stop=True)
                    ins.then_inc(s_full, 1)
                elif st.kind == "retention_scores":
                    pe.wait_ge(t_evac, st.use + 1)
                    for a, (s, freed) in enumerate(st.banks):
                        wait(freed)
                        n = TOK - a * P
                        for c in range(2):
                            ins = pe.matmul(Sb[s % 2][:, c * n:(c + 1) * n], headq[:, 4 + st.p, c, tok(a)],
                                            qk[:, Q_QB + st.p, a * P:TOK], start=True, stop=True)
                        ins.then_inc(s_full, 1)
                elif st.kind == "retention_out":
                    pe.wait_ge(*st.need)
                    pe.wait_ge(decayed, 2 * st.p + 2)
                    for t in range(NT):
                        o, freed = st.ro[t]
                        if st.p == 0:
                            wait(freed)
                        for c in range(2):
                            h = 2 * st.p + c
                            for a in range(t + 1):
                                n = TOK - a * P
                                wt = e[:, a, c * n + (t - a) * P:c * n + (t - a + 1) * P]
                                ins = pe.matmul(Ob[o % 2][:, h * DH:(h + 1) * DH], wt, v[:, a, h * DH:(h + 1) * DH],
                                                start=a == 0, stop=a == t)
                        if st.p == 3:
                            ins.then_inc(o_full, 1)
                    if st.p < 3:
                        ins.then_inc(decayed_used, 1)
                elif st.kind == "ffn":
                    ffn_chunk(st, 0, 0, True)
                    with pe.Fori(1, FCHUNKS - 2) as j:
                        ffn_chunk(st, j, 1, False)
                    ffn_chunk(st, FCHUNKS - 2, FCHUNKS - 2, False, lambda: ffn_turns(st, FCHUNKS - 1))
                    pe.wait_ge(t_evac, st.t0 + 2 * FCHUNKS)
                    u = st.base + 3 * FCHUNKS - 1
                    pe.wait_ge(lo_done, u + 1)
                    ffn_down(st, u, 2, False, True)

        @block.vector
        def _(dve):
            chain = [0]

            def behind(ins):
                chain[0] += 1
                ins.then_inc(dve_chain, 1)
                dve.wait_ge(dve_chain, chain[0])

            def split_lo(u, hi=None):
                if u >= N_UNITS:
                    return
                dve.wait_ge(hi_done, u + 1 if hi is None else hi)
                dve.tensor_tensor(shaped(wlo, u), shaped(raw, u), shaped(whi, u), ALU.subtract).then_inc(lo_done, 1)

            inverses = [0]

            def wait_inverse():
                inverses[0] += 1
                dve.wait_ge(inverse_done, inverses[0])

            def relu2(st, j, bank=Pb):
                for t in range(NT):
                    dve.wait_ge(relu_done, j * 2 + (st.relu0 + t + 1))
                    dve.tensor_tensor(hidden[:, t, :], hidden[:, t, :], bank[t][:], ALU.mult).then_inc(relu2_done, 1)

            def gated(st, j, bank=Pb):
                for t in range(NT):
                    dve.wait_ge(silu_done, j * 2 + (t + 1))
                    dve.tensor_tensor(hidden[:, t, 0:FCHUNK], zq[:, 1, t, 0:FCHUNK], bank[t][:, FCHUNK:2 * FCHUNK],
                                      ALU.mult).then_inc(relu2_done, 1)

            def hidden_lo(st, j, k0, per):
                for b in range(2):
                    dve.wait_ge(t_hi, j * 2 + (st.hi0 + b + 1))
                    ks = slice(k0 + per * b, k0 + per * b + per)
                    dve.tensor_tensor(set_lo[st.uset][:, ks, :], Tb[(st.t0 + b) % 2][:, 0:per * TOK]
                                      .rearrange("p (k n) -> p k n", k=per), set_hi[st.uset][:, ks, :],
                                      ALU.subtract).then_inc(t_evac, 1)

            def mlp_chunk(st, j, peel, last=False):
                u0 = st.base + 2 + AHEAD + 4 * peel
                hi = lambda u: j * 4 + (u + 1 - 4 * peel)
                split_lo(u0, hi(u0))
                hidden_lo(st, j, UK, 2)
                split_lo(u0 + 1, hi(u0 + 1))
                relu2(st, j + 1)
                split_lo(u0 + 2, hi(u0 + 2))
                if last:
                    hidden_lo(st, j + 1, 0, 2)
                split_lo(u0 + 3, hi(u0 + 3))

            def ffn_chunk(st, j, peel):
                u0 = st.base + 2 + AHEAD + 3 * peel
                hi = lambda u: j * 3 + (u + 1 - 3 * peel)
                split_lo(u0, hi(u0))
                hidden_lo(st, j, 0, 1)
                split_lo(u0 + 1, hi(u0 + 1))
                gated(st, j + 1)
                split_lo(u0 + 2, hi(u0 + 2))

            bank_of = {"P": Pb, "S": Sb, "O": Ob}
            heads_view = lambda ap, n=8: ap.rearrange("p (h d) -> p h d", h=n)
            spread = lambda ap, n: ap.unsqueeze(2).broadcast_to([P, ap.shape[1], n])

            for st in STEPS:
                if st.kind == "setup":
                    dve.wait_ge(s_full, 1)
                    dve.tensor_copy(gcol[:, 0:FIRST * KT], Sb[gain_s[0] % 2][:, 0:FIRST * KT]).then_inc(gain_cols, 1)
                    dve.wait_ge(gain_cols, 1)
                elif st.kind == "constants":
                    dve.wait_ge(s_full, 2)
                    n = (len(GAINS) - FIRST) * KT
                    dve.tensor_copy(gcol[:, FIRST * KT:], Sb[gain_s[1] % 2][:, 0:n]).then_inc(gain_cols, 1)
                    dve.wait_ge(gain_cols, 2)
                    a, b = g_at("norm1_w_2"), g_at("final_norm")
                    dve.tensor_tensor(gcol[:, a:a + KT], gcol[:, a:a + KT], gcol[:, b:b + KT], ALU.mult)\
                       .then_inc(gain_cols, 1)
                    dve.wait_ge(gain_cols, 3)
                    lam = st.lam
                    dve.wait_ge(consts_landed, CONSTS)
                    behind(dve.tensor_tensor(lamprod, lamrow[:, :, 0, :], lamrow[:, :, 1, :], ALU.mult))
                    dve.tensor_reduce(lam[:, 0:2], lamprod, AX_X, ALU.add).then_inc(lam_sum, 1)
                    dve.tensor_scalar(subln[:], subln[:], 1.0 - LAM_INIT, None, ALU.mult)
                    behind(dve.tensor_tensor(qkn[:, 0, :], qkn[:, 0, :], qkn[:, 1, :], ALU.mult))
                    dve.wait_ge(s_full, bias_s[0] + 1)
                    dve.tensor_copy(biasvec, Sb[bias_s[0] % 2][0:8, :]).then_inc(bias_vec, 1)
                    dve.wait_ge(lam_exp, 1)
                    dve.scalar_tensor_tensor(out=lam[:, 4:5], in0=lam[:, 2:3], scalar=LAM_INIT, in1=lam[:, 3:4],
                                             op0=ALU.add, op1=ALU.subtract).then_inc(lam_done, 1)
                    dve.wait_ge(lam_done, 1)
                    dve.wait_ge(heads_zeroed, 1)
                elif st.kind == "split":
                    split_lo(st.u)
                elif st.kind == "turn_operand":
                    for b in range(2):
                        n = st.use[b]
                        dve.wait_ge(t_hi, st.hi + b + 1)
                        for g, s, k0 in st.gains:
                            k = k0 + 2 * b
                            T = Tb[n % 2][:].rearrange("p (k n) -> p k n", k=2)
                            if g is None:
                                ins = dve.tensor_tensor(set_lo[s][:, k:k + 2, :], T, set_hi[s][:, k:k + 2, :],
                                                        ALU.subtract)
                            else:
                                for i in range(2):
                                    gi = g + UK * st.half + 2 * b + i
                                    ins = dve.scalar_tensor_tensor(
                                        out=set_lo[s][:, k + i, :], in0=T[:, i, :], scalar=gcol[:, gi:gi + 1],
                                        in1=set_hi[s][:, k + i, :], op0=ALU.mult, op1=ALU.subtract)
                        ins.then_inc(t_evac, 1)
                elif st.kind == "turn_heads":
                    for t in range(NT):
                        n = st.use[t]
                        dve.wait_ge(t_full, n + 1)
                        T = Tb[n % 2][:].rearrange("p (b n) -> p b n", b=4)
                        for ps, bs, dst in st.pieces:
                            ins = dve.tensor_copy(dst(t), T[ps, bs, :])
                        ins.then_inc(t_evac, 1)
                elif st.kind == "statistics":
                    if st.what == "final":
                        dve.wait_ge(late_landed, 32)
                        dve.wait_ge(t_full, st.factor)
                        dve.wait_ge(rstd_done, st.n + 1)
                        for t in range(NT):
                            ins = dve.scalar_tensor_tensor(out=x[:, t, :], in0=x[:, t, :], scalar=st.rs[:, t:t + 1],
                                                           in1=fgb, op0=ALU.mult, op1=ALU.mult)
                        ins.then_inc(x_normed, 1)
                elif st.kind == "scores":
                    it = st.it
                    dve.wait_ge(s_full, it.s + 1)
                    S = Sb[it.s % 2][:, 0:2 * it.n].rearrange("p (c n) -> p c n", c=2)
                    behind(dve.tensor_reduce(it.nm, S, AX_X, ALU.max))
                    dve.tensor_scalar(it.nm, it.nm, -SCALE, None, ALU.mult)\
                       .then_inc(nmax_done, 1)
                elif st.kind == "mix":
                    it = st.it
                    dve.wait_ge(exp_done, it.exp + 1)
                    ins = dve.reciprocal(it.rs, it.rs)
                    if it.kind == "diff":
                        behind(ins)
                        behind(dve.tensor_tensor(it.rs[:, 1:2], it.rs[:, 1:2], lam[:, 4:5], ALU.mult))
                        e0, e1 = e[:, it.buf, 0:it.n], e[:, it.buf, it.n:2 * it.n]
                        behind(dve.tensor_scalar(e1, e1, it.rs[:, 1:2], None, ALU.mult))
                        ins = dve.scalar_tensor_tensor(out=e0, in0=e0, scalar=it.rs[:, 0:1], in1=e1,
                                                       op0=ALU.mult, op1=ALU.subtract)
                    ins.then_inc(w_done, 1)
                elif st.kind == "turn_weights":
                    it = st.it
                    dve.wait_ge(t_full, it.use + 1)
                    if it.before:
                        dve.wait_ge(o_full, it.before.o + 1)
                    m = it.n * (1 if it.kind == "diff" else 2)
                    dve.tensor_copy(wT[:, it.buf, 0:m], Tb[it.use % 2][:, 0:m]).then_inc(t_evac, 1)
                elif st.kind == "attend":
                    it = st.it
                    O = Ob[it.o % 2][:, 0:P]
                    at = it.pair * P + (SELF if it.kind == "mem" else 0)
                    dst = o_nat[:, it.t, at:at + P]
                    if it.kind != "diff":
                        dve.wait_ge(o_full, it.o + 1)
                        dve.wait_ge(w_done, it.w)
                        dve.tensor_tensor(heads_view(dst, 2), heads_view(O, 2), spread(it.rs, DH), ALU.mult)\
                           .then_inc(o_evac, 1)
                elif st.kind == "diff_norm":
                    wait_inverse()
                    for it in st.items:
                        dve.scalar_tensor_tensor(out=o_nat[:, it.t, it.pair * P:(it.pair + 1) * P],
                                                 in0=Ob[it.o % 2][:, 0:P], scalar=it.ors, in1=subln[:],
                                                 op0=ALU.mult, op1=ALU.mult).then_inc(o_evac, 1)
                elif st.kind == "residual":
                    if st.scale is not None:
                        dve.wait_ge(rstd_done, st.scale.n_done)
                    for t in range(NT):
                        dve.wait_ge(mul_done, 2 * st.u + t + 1)
                        xs = x[:, t, st.half * COLS:(st.half + 1) * COLS]
                        if st.scale is None:
                            ins = dve.tensor_tensor(xs, xs, bank_of[st.bank][t][:], ALU.add)
                        else:
                            ins = dve.scalar_tensor_tensor(out=xs, in0=bank_of[st.bank][t][:],
                                                           scalar=st.scale.rs[:, t:t + 1], in1=xs,
                                                           op0=ALU.mult, op1=ALU.add)
                        ins.then_inc(resid_done, 1)
                elif st.kind == "mlp":
                    relu2(st, 0, Ob)
                    mlp_chunk(st, 0, 0)
                    with dve.Fori(1, CHUNKS - 2) as j:
                        mlp_chunk(st, j, 1)
                    mlp_chunk(st, CHUNKS - 2, CHUNKS - 2, last=True)
                elif st.kind == "query_norm":
                    for t in range(NT):
                        dve.wait_ge(qsq_done, t + 1)
                        ins = dve.tensor_reduce(st.ss[:, 8 * t:8 * t + 8], heads_view(rt[:, t, :]), AX_X, ALU.add)
                    ins.then_inc(sum_done, 1)
                elif st.kind == "query_scale":
                    wait_inverse()
                    for t in range(NT):
                        z = heads_view(zq[:, 0, t, :])
                        dve.tensor_tensor(z, z, spread(st.st.rs[:, 8 * t:8 * t + 8], DH), ALU.mult).then_inc(qn_done, 1)
                elif st.kind == "small_norm":
                    dve.wait_ge(heads_zeroed, 2)
                    for t in range(NT):
                        dve.wait_ge(chunk_evac, 2 * st.chunk + t + 1)
                        c = zs[:, t, 0:P]
                        ins = dve.tensor_tensor_reduce(sn[:, t, 2, :], c, c, 1.0, 0.0, ALU.mult, ALU.add,
                                                       st.ss[:, t:t + 1])
                    ins.then_inc(sum_done, 1)
                    for t in range(NT):
                        z = zs[:, t, :]
                        dve.tensor_copy(sn[:, t, 0, :], z[:, P:2 * P])
                        dve.tensor_copy(sn[:, t, 1, :].rearrange("p (r d) -> p r d", r=4),
                                        z[:, 2 * P:2 * P + 32].unsqueeze(1).broadcast_to([P, 4, 32]))
                    wait_inverse()
                    for t in range(NT):
                        dve.scalar_tensor_tensor(out=sn[:, t, 2, :], in0=zs[:, t, 0:P], scalar=st.rs[:, t:t + 1],
                                                 in1=kvn[:], op0=ALU.mult, op1=ALU.mult).then_inc(sn_done, 1)
                elif st.kind == "shared_key_norm":
                    kv = st.st
                    dve.wait_ge(kava_done, 1)
                    for t in range(NT):
                        ka = sn[:, t, 1, 0:DH]
                        ins = dve.tensor_tensor_reduce(sn[:, t, 2, 0:DH], ka, ka, 1.0, 0.0, ALU.mult, ALU.add,
                                                       kv.ss[:, t:t + 1])
                    ins.then_inc(sum_done, 1)
                    wait_inverse()
                    for t in range(NT):
                        for c in range(2):
                            ins = dve.scalar_tensor_tensor(out=sn[:, t, 0, c * DH:(c + 1) * DH], in0=sn[:, t, 1, 0:DH],
                                                           scalar=kv.rs[:, t:t + 1], in1=qkn[:, 0, :],
                                                           op0=ALU.mult, op1=ALU.mult)
                        ins.then_inc(ka_done, 1)
                elif st.kind == "index_sum":
                    ix = st.st
                    t, n = ix.t, ix.n
                    behind(dve.tensor_scalar(ix.ind, zs[:, t, 2 * P + 32:SMALL], IDX_W_SCALE, None, ALU.mult))
                    dve.wait_ge(dots_done, ix.dots + len(ix.banks))
                    sc = score[t]
                    behind(dve.tensor_scalar(sc, relu_dots[:, 0, 0:n], ix.ind[:, 0:1], None, ALU.mult))
                    for h in range(1, 4):
                        ins = dve.scalar_tensor_tensor(out=sc, in0=relu_dots[:, h, 0:n], scalar=ix.ind[:, h:h + 1],
                                                       in1=sc, op0=ALU.mult, op1=ALU.add)
                        if h < 3:
                            behind(ins)
                    ins.then_inc(dots_used, 1)
                    dve.wait_ge(dots_used, t + 1)
                    behind(dve.memset(sc[0:DH, n - DH:n], BELOW))
                elif st.kind == "select":
                    ix = st.st
                    t, n = ix.t, ix.n
                    bufs = [score[t], work[:, 0:n]]
                    for r in range(*st.rounds):
                        behind(dve.max(ix.m8, bufs[r % 2]))
                        behind(dve.match_replace(bufs[1 - r % 2], ix.m8, bufs[r % 2], TAKEN))
                    if st.rounds[1] == TOPK // MAX8:
                        dve.tensor_scalar(selmask[:, t, 0:n], bufs[0], TAKEN, NEG, ALU.not_equal, ALU.mult)\
                           .then_inc(sel_done, 1)
                elif st.kind == "retention_scores":
                    for a, (s, _) in enumerate(st.banks):
                        dve.wait_ge(s_full, s + 1)
                        n = TOK - a * P
                        if st.p == 0:
                            dve.wait_ge(t_full, st.before + 1)
                        else:
                            dve.wait_ge(decayed_used, st.p)
                        for c in range(2):
                            h = 2 * st.p + c
                            o = c * n
                            dst, src = e[:, a, o:o + n], Sb[s % 2][:, o:o + n]
                            ins = dve.scalar_tensor_tensor(out=dst[:, 0:P], in0=src[:, 0:P],
                                                           scalar=dec[:, a, 8 + h:9 + h], in1=tri[:], op0=ALU.mult,
                                                           op1=ALU.mult)
                            if n > P:
                                ins = dve.tensor_scalar(dst[:, P:n], src[:, P:n], dec[:, a, 8 + h:9 + h], None,
                                                        ALU.mult)
                        ins.then_inc(decayed, 1)
                elif st.kind == "group_center":
                    dve.wait_ge(sel_done, 2)
                    for t in range(NT):
                        dve.wait_ge(o_full, st.ro[t][0] + 1)
                        y = heads_view(o_nat[:, t, 512:1024])
                        o, mu = st.ro[t][0], st.mu[:, 8 * t:8 * t + 8]
                        dve.tensor_tensor(y, heads_view(Ob[o % 2][:]), spread(dec[:, t, 0:8], DH), ALU.mult)\
                           .then_inc(o_evac, 1)
                        dve.wait_ge(o_evac, o + 1)
                        behind(dve.tensor_reduce(mu, y, AX_X, ALU.add))
                        behind(dve.tensor_scalar(mu, mu, 1.0 / DH, None, ALU.mult))
                        dve.tensor_tensor(y, y, spread(mu, DH), ALU.subtract).then_inc(yc_done, 1)
                elif st.kind == "group_scale":
                    group = st.st
                    for t in range(NT):
                        dve.wait_ge(ysq_done, t + 1)
                        ins = dve.tensor_reduce(group.va[:, 8 * t:8 * t + 8], heads_view(rt[:, t, :]), AX_X, ALU.add)
                    ins.then_inc(sum_done, 1)
                    wait_inverse()
                    for t in range(NT):
                        y = heads_view(o_nat[:, t, 512:1024])
                        dve.tensor_tensor(y, y, spread(group.rs[:, 8 * t:8 * t + 8], DH), ALU.mult).then_inc(yn_done, 1)
                elif st.kind == "group_gate":
                    y = o_nat[:, 1, 512:1024]
                    dve.wait_ge(yn_done, 2)
                    dve.wait_ge(*st.st.gate)
                    dve.wait_ge(gn_landed, 32)
                    behind(dve.tensor_tensor(y, y, gn[:, 0, :], ALU.mult))
                    behind(dve.tensor_tensor(y, y, gn[:, 1, :], ALU.add))
                    dve.tensor_tensor(y, y, zq[:, 1, 1, :], ALU.mult).then_inc(ob_done, 1)
                elif st.kind == "ffn":
                    gated(st, 0, Ob)
                    ffn_chunk(st, 0, 0)
                    with dve.Fori(1, FCHUNKS - 2) as j:
                        ffn_chunk(st, j, 1)
                    ffn_chunk(st, FCHUNKS - 2, FCHUNKS - 2)
                    hidden_lo(st, FCHUNKS - 1, 2, 1)
                elif st.kind == "store":
                    dve.wait_ge(rstd_done, st.rs.n_done)
                    for i, (c, t) in enumerate((c, t) for c in range(2) for t in range(NT)):
                        dve.wait_ge(mul_done, 2 * st.u + i + 1)
                        xs = x[:, t, c * COLS:(c + 1) * COLS]
                        dve.scalar_tensor_tensor(out=xs, in0=bank_of["SO"[c]][t][:], scalar=st.rs.rs[:, t:t + 1],
                                                 in1=xs, op0=ALU.mult, op1=ALU.add).then_inc(resid_done, 1)


def kernel(**inputs):
    import concourse.bacc as bacc
    from concourse.bass_utils import run_bass_kernel_spmd

    nc = bacc.Bacc("TRN2", target_bir_lowering=False, num_devices=1)
    arrays, aps = {}, {}
    for name, a in [*inputs.items(), *shape_tables().items()]:
        a = np.ascontiguousarray(a)
        arrays[f"in_{name}"] = a
        aps[name] = nc.dram_tensor(f"in_{name}", a.shape, mybir.dt.from_np(a.dtype), kind="ExternalInput").ap()
    out = nc.dram_tensor("out_0", (1, TOK, D), F32, kind="ExternalOutput").ap()
    build(nc, aps, out)
    return run_bass_kernel_spmd(nc, [arrays], core_ids=[0]).results[0]["out_0"]
```

```python
from contextlib import ExitStack
import math

import numpy as np
import concourse.bass as bass
from concourse import mybir

F32 = mybir.dt.float32
F32R = mybir.dt.float32r
BF16 = mybir.dt.bfloat16
ACT = mybir.ActivationFunctionType
ALU = mybir.AluOpType
AX_X = mybir.AxisListType.X

P = 128
TOK = 256
NT = TOK // P
D = 1024
KT = D // P
DH = 64
COLS = 512
UK = 4
RING = 4
FRING = 3
AHEAD = 3
SELF = 768
DFF = 4096
CHUNKS = DFF // COLS
FFN = 2816
FCHUNK = 256
FCHUNKS = FFN // FCHUNK
EPS = 1e-6
GN_EPS = 1e-5
NEG = -1e30
BELOW = -3.0e38
TAKEN = -3.4e38
TOPK = 64
CONSTS = 16 * 12
STATS = 340
Q_QB, Q_KA, Q_IK, Q_C = 16, 20, 21, 22
MAX8 = 8
LAM_INIT = 0.8 - 0.6 * math.exp(-0.3 * 0)
SCALE = DH ** -0.5
IDX_SCALE = 32 ** -0.5
IDX_W_SCALE = 4 ** -0.5
SMALL = 292

GAINS = ["a_mem_norm", "b_mem_norm", "a_norm_attn", "a_norm_mlp", "kv_norm", "b_norm_attn",
         "b_norm_mlp", "norm1_w_2", "final_norm", "norm2_w_2"]
FIRST = 3


def shape_tables():
    half = DH // 2
    pos = np.arange(TOK, dtype=np.float32)[:, None]
    a = np.arange(half, dtype=np.float32)
    ten = np.float32(10000.0)
    out = {}
    for name, inv in (("rope1", np.float32(1) / ten ** (a / np.float32(half))),
                      ("rope2", ten ** (-a / np.float32(half)))):
        ang = (pos * inv[None, :].astype(np.float32)).astype(np.float32)
        c, s = np.cos(ang), np.sin(ang)
        out[name] = np.concatenate([c, c, -s, s], axis=1).astype(np.float32)
    rel = np.arange(512) - 255
    n = np.abs(rel)
    nf = np.maximum(n, 1).astype(np.float32)
    large = 8 + (np.log(nf / np.float32(8)) / np.float32(math.log(16)) * np.float32(8)).astype(np.int32)
    bucket = np.where(rel > 0, 16, 0) + np.where(n < 8, n, np.minimum(large, 15))
    out["bucket_onehot"] = (np.arange(32)[:, None] == bucket[None, :]).astype(np.float32)
    log_g = np.log1p(-(2.0 ** (-5.0 - np.arange(8.0))))
    t = np.arange(TOK, dtype=np.float64)[:, None]
    out["decays"] = np.concatenate([np.exp(t * log_g), np.exp(-t * log_g) * SCALE], axis=1).astype(np.float32)
    return out


class Step:
    pass


def build(nc, A, out):
    UNITS = []

    def unit(w, rows, cols, nk=UK):
        n = sum(c for _, c in cols)
        view = lambda r, k, c0, c: w[r:r + P * k, c0:c0 + c].rearrange("(k p) n -> p k n", p=P)
        if len(cols) == 1:
            h = nk // 2
            parts = [(view(rows + P * h * i, h, cols[0][0], n), slice(h * i, h * i + h), slice(0, n))
                     for i in range(2)]
        else:
            at, parts = 0, []
            for c0, c in cols:
                parts.append((view(rows, nk, c0, c), slice(0, nk), slice(at, at + c)))
                at += c
        un = Step()
        un.n, un.nk, un.parts = n, nk, parts
        UNITS.append(un)
        return len(UNITS) - 1

    def chunk_units(w, cols):
        return [unit(w, h * UK * P, cols) for h in range(2)]

    STEPS = []
    count = Step()
    count.t, count.hi, count.chunk, count.s, count.o, count.resid = 0, 0, 0, 0, 0, 0
    count.rstd, count.rope, count.exp, count.relu2, count.osq, count.ss = 0, 0, 0, 0, 0, 0
    count.decayed, count.w, count.dots = 0, 0, 0
    free = {}

    def add(kind):
        st = Step()
        st.kind = kind
        STEPS.append(st)
        return st

    ctx = ExitStack()
    with ctx:
        def sb(name, shape, dt=F32):
            return ctx.enter_context(nc.sbuf_tensor(name, shape, dt))

        def sem(name):
            return ctx.enter_context(nc.semaphore(name))

        raw = sb("raw", [P, RING, UK * COLS])
        whi = sb("whi", [P, RING, UK * COLS], F32R)
        wlo = sb("wlo", [P, RING, UK * COLS], F32R)
        x = sb("x", [P, NT, D])
        set_hi = [sb(f"set{i}_hi", [P, KT, TOK], F32R) for i in range(2)]
        set_lo = [sb(f"set{i}_lo", [P, KT, TOK], F32R) for i in range(2)]
        o_nat = sb("o_nat", [P, NT, D])
        zq = sb("zq", [P, 2, NT, COLS])
        rt = sb("rope_tmp", [P, 2, COLS])
        qk = sb("qk", [P, 24, TOK])
        v = sb("v", [P, NT, SELF])
        e = sb("e", [P, 2, COLS])
        wT = sb("wT", [P, 2, COLS])
        memkv = sb("memkv", [P, 2, COLS])
        rope1 = sb("rope1_sb", [P, NT, 4 * 32])
        rope2 = sb("rope2_sb", [P, NT, 4 * 32])
        ident = sb("ident", [P, P])
        identb = sb("identb", [P, P], BF16)
        cmask = sb("cmask", [P, P], BF16)
        flip = sb("flip", [P, P])
        tri = sb("tri", [P, P])
        gcol = sb("gcol", [P, len(GAINS) * KT])
        subln = sb("subln", [P, P])
        kvn = sb("kvn", [P, P])
        qkn = sb("qkn", [P, 2, DH])
        wukv = sb("wukv", [P, 2, DH])
        dec = sb("dec", [P, NT, 16])
        selmask = sb("selmask", [P, NT, TOK], BF16)
        stat = sb("stat", [P, STATS])
        newton = sb("newton", [P, 2, 16])
        minus_half = sb("minus_half", [P, 16])
        junk1 = sb("junk1", [P, P], BF16)
        rel8 = sb("rel8", [32, 8])
        mem_nat = o_nat
        hidden = zq[:, 0, :, :]
        zs = o_nat[:, 0, 0:2 * SMALL].rearrange("p (t n) -> p t n", t=2)
        sn = o_nat[:, 1, 0:768].rearrange("p (t b n) -> p t b n", t=2, b=3)
        relu_dots = wT[:, :, :].rearrange("p a b -> p (a b)").rearrange("p (h n) -> p h n", h=4)
        score = [o_nat[:, 0, SMALL + 4:SMALL + 4 + P], e[:, 1, COLS - TOK:COLS]]
        work = wT[:, 1, COLS - TOK:COLS]
        btoep = [memkv[:, :, :].rearrange("p a b -> p (a b)").rearrange("p (h n) -> p h n", h=4),
                 set_lo[1][:, 0:4, :].bitcast(F32)]
        fgb = qk[:, 16:20, :].rearrange("p a b -> p (a b)")
        gn = zq[:, 0, :, :]
        query_sq = zq[:, 1, :, :]
        junk = wT[:, :, :].rearrange("p a b -> p (a b)").bitcast(BF16).rearrange("p (t n) -> p t n", t=NT)
        lamrow = rt[:, 0, 0:256].rearrange("p (a b d) -> p a b d", a=2, b=2)
        lamprod = rt[:, 0, 256:384].rearrange("p (a d) -> p a d", a=2)
        onehot = e[0:32, 0, :]
        biasvec = e[0:8, 1, :]
        grow = [qk[0:len(group) * KT, 23 - i, 0:P] for i, group in enumerate((GAINS[:FIRST], GAINS[FIRST:]))]
        headq = qk[:, 0:16, :].rearrange("p (b c) n -> p b c n", c=2)

        ncol = [0]

        def col(n):
            ncol[0] += n
            assert ncol[0] <= STATS, ncol
            return stat[:, ncol[0] - n:ncol[0]]

        pb = lambda n: ctx.enter_context(nc.psum_tensor(n, [P, COLS], F32))
        Pb = [pb(f"proj{i}") for i in range(2)]
        Tb = [pb(f"turn{i}") for i in range(2)]
        Sb = [pb(f"score{i}") for i in range(2)]
        Ob = [pb(f"outp{i}") for i in range(2)]
        for i in range(2):
            for b in "PTSO":
                free[b, i] = None

        landed = [sem(f"unit_landed{i}") for i in range(RING)]
        hi_done = sem("hi_done")
        lo_done = sem("lo_done")
        mul_done = sem("mul_done")
        t_full = sem("t_full")
        t_hi = sem("t_hi")
        t_evac = [sem(f"t_evac{i}") for i in range(2)]
        chunk_evac = sem("chunk_evac")
        rope_done = sem("rope_done")
        s_full = sem("s_full")
        nmax_done = sem("nmax_done")
        exp_done = sem("exp_done")
        w_done = sem("w_done")
        o_full = sem("o_full")
        osq_done = sem("osq_done")
        o_evac = sem("o_evac")
        resid_done = sem("resid_done")
        ss_done = sem("ss_done")
        rstd_done = sem("rstd_done")
        relu_done = sem("relu_done")
        relu2_done = sem("relu2_done")
        silu_done = sem("silu_done")
        dots_done = sem("dots_done")
        dots_used = sem("dots_used")
        sel_done = sem("sel_done")
        kava_done = sem("kava_done")
        ka_done = sem("ka_done")
        sn_done = sem("sn_done")
        qn_done = sem("qn_done")
        qsq_done = sem("qsq_done")
        decayed = sem("decayed")
        yc_done = sem("yc_done")
        ysq_done = sem("ysq_done")
        yn_done = sem("yn_done")
        ob_done = sem("ob_done")
        sum_done = sem("sum_done")
        inverse_done = sem("inverse_done")
        x_normed = sem("x_normed")
        dve_chain = sem("dve_chain")
        pool_chain = sem("pool_chain")
        heads_zeroed = sem("heads_zeroed")
        consts_made = sem("consts_made")
        mem_landed = [sem(f"mem_landed{i}") for i in range(2)]
        x_landed, consts_landed = sem("x_landed"), sem("consts_landed")
        gain_cols = sem("gain_cols")
        lam_sum, lam_exp, lam_done = sem("lam_sum"), sem("lam_exp"), sem("lam_done")
        gains_landed, gn_landed = [sem(f"gains_landed{i}") for i in range(2)], sem("gn_landed")
        bias_vec, bias_stored = sem("bias_vec"), sem("bias_stored")
        late_landed = sem("late_landed")
        bias_landed = sem("bias_landed")
        stored = sem("stored")

        bias_dram = nc.dram_tensor("bias_by_distance", (8, 512), F32, kind="Internal").ap()

        def turned(n):
            return t_evac[n % 2], n // 2 + 1

        def t_use():
            n = count.t
            count.t += 1
            return n

        def turn_operand(src, half, gains, ready, set_free, cols=None):
            st = add("turn_operand")
            st.src, st.half, st.gains, st.ready, st.set_free = src, half, gains, ready, set_free
            st.use, st.hi = [t_use(), t_use()], count.hi
            count.hi += 2
            return st.use

        split_next = [0]

        def split(u):
            while split_next[0] <= u:
                st = add("split")
                st.u = split_next[0]
                split_next[0] += 1

        def multiply(u, lhs, k0, use, bank, start, stop, hold=False, tiles=range(NT)):
            st = add("multiply")
            st.u, st.lhs, st.k0, st.use, st.bank, st.start = u, lhs, k0, use, bank, start
            st.stop, st.freed, st.tiles = stop, [free[bank, t] for t in range(NT)] if start else None, tiles
            if not hold:
                split(u + AHEAD)

        def multiply_around(action, *a):
            multiply(*a, hold=True, tiles=[0])
            done = action()
            multiply(*a, hold=True, tiles=[1])
            return done

        def half_around(action, us, h, lhs, use, bank="P"):
            done = multiply_around(action, us[h], lhs, UK * h, use, bank, h == 0, h == 1)
            split(us[h] + AHEAD)
            return done

        def evacuate(u, pieces, scale, slot_free=None, silu=False, bank="P"):
            st = add("evacuate")
            st.u, st.pieces, st.scale, st.chunk = u, pieces, scale, count.chunk
            st.slot_free, st.silu, st.bank = slot_free, silu, bank
            for t in range(NT):
                free[bank, t] = (chunk_evac, 2 * count.chunk + t + 1)
            count.chunk += 1
            return st

        def rope(slot, n, table):
            st = add("rope")
            st.slot, st.n, st.table, st.chunk, st.rope = slot, n, table, count.chunk, count.rope
            count.rope += 1
            return st

        def turn_heads(src, blocks, pieces, ready):
            st = add("turn_heads")
            st.src, st.blocks, st.pieces, st.ready = src, blocks, pieces, ready
            st.use = [t_use(), t_use()]
            return st.use

        LOW, HIGH, ALL = slice(0, DH), slice(DH, P), slice(0, P)
        tok = lambda t: slice(t * P, (t + 1) * P)

        def pairs(a, first, n):
            return [(ALL, slice(a, a + n), lambda t: qk[:, first:first + n, tok(t)])]

        def heads(a, first, n):
            return [(LOW, slice(a, a + n), lambda t: headq[LOW, first:first + n, 0, tok(t)]),
                    (HIGH, slice(a, a + n), lambda t: headq[HIGH, first:first + n, 1, tok(t)])]

        def s_use(release):
            n = count.s
            count.s += 1
            f = free["S", n % 2]
            free["S", n % 2] = release
            return n, f

        def o_use():
            n = count.o
            count.o += 1
            f = free["O", n % 2]
            free["O", n % 2] = (o_evac, n + 1)
            return n, f

        ITEMS = []

        def scores(kind, pair, t, q, k, need):
            it = Step()
            it.kind, it.pair, it.t, it.q, it.k, it.need = kind, pair, t, q, k, need
            it.n, it.buf, it.i, it.nm = P * (t + 1), len(ITEMS) % 2, len(ITEMS), col(2)
            it.rs, it.before = col(2), ITEMS[-2] if len(ITEMS) > 1 else None
            if kind == "mem":
                it.n = TOK
            if kind == "diff":
                both = (col(2), col(2)) if t == 0 else ITEMS[-1].both
                it.both, it.oss, it.ors = both, both[0][:, t:t + 1], both[1][:, t:t + 1]
            it.exp = count.exp
            count.exp += 1
            it.s, it.s_free = s_use((exp_done, it.exp + 1))
            ITEMS.append(it)
            st = add("scores")
            st.it = it
            return it

        def mix(it):
            count.w += 1
            it.w = count.w
            st = add("mix")
            st.it = it

        def turn_weights(it):
            it.use = t_use()
            st = add("turn_weights")
            st.it = it

        def attend(it, vneed):
            it.o, it.o_free = o_use()
            it.vneed = vneed
            if it.kind == "diff":
                count.osq += 1
                it.osq = count.osq
            st = add("attend")
            st.it = it
            return it.o + 1

        def norm(pair):
            st = add("diff_norm")
            st.items, (st.oss, st.ors) = pair, pair[0].both

        def residual(half, bank, u, scale):
            st = add("residual")
            st.half, st.bank, st.u, st.scale, st.r = half, bank, u, scale, count.resid
            count.resid += 2
            for t in range(NT):
                free[bank, t] = (resid_done, st.r + t + 1)
            return st

        def statistics(src, ready, factor=None, kind="plain"):
            st = add("statistics")
            st.src, st.ready, st.n, st.ss, st.rs = src, ready, count.rstd, col(2), col(2)
            st.what, st.factor = kind, factor
            if kind == "final":
                st.ss2, st.r2 = col(2), col(2)
            st.sums = count.ss
            count.ss += 2 if kind == "final" else 1
            count.rstd += 2 if kind == "final" else 1
            st.n_done = count.rstd
            return st

        g_at = lambda name: GAINS.index(name) * KT

        zfree = [None, None]
        gain_s = [s_use((gain_cols, 1))[0]]
        add("setup")
        memA = chunk_units(A["a_w_mem_kv"][0], [(0, 512)])
        w = A["a_w_in"][0]
        qk0 = chunk_units(w, [(0, 256), (SELF, 256)])
        vm = chunk_units(w, [(2 * SELF + 512, 512)])
        v0 = chunk_units(w, [(2 * SELF, 512)])
        qk1 = chunk_units(w, [(256, 256), (SELF + 256, 256)])
        qk2 = chunk_units(w, [(512, 256), (SELF + 512, 256)])

        def out_units(w, rows=(0, 512)):
            return [unit(w, r, [(c, COLS)]) for r in rows for c in (0, COLS)]

        def mul_chunk_half(us, h, lhs, uses, bank="P", mixed=()):
            multiply(us[h], lhs, UK * h, uses[h], bank, h == 0, h == 1, hold=True)
            for it in mixed:
                mix(it)
            split(us[h] + AHEAD)

        def turn_mem(name, h, free):
            return turn_operand(mem_nat, h, [(g_at(name), 1, UK * h)], (mem_landed[h], 16), free)[-1]

        def turn_x(h, name, s):
            return turn_operand(x, h, [(g_at(name), s, UK * h)], (x_landed, 16), None)[-1]

        m1 = [turn_mem("a_mem_norm", 0, None)]
        split(1)
        m1.append(multiply_around(lambda: turn_mem("a_mem_norm", 1, None), memA[0], 1, 0, m1[0], "P", True, False))
        split(2)
        rs_mem = statistics(mem_nat, (mem_landed[1], 16))
        x1 = [half_around(lambda: turn_x(0, "a_norm_attn", 0), memA, 1, 1, m1[1])]
        def mem_pieces(slot):
            return [((0, 256), lambda t: zq[:, slot, t, 0:256]),
                    ((256, 512), lambda t: memkv[:, 1, t * 256:t * 256 + 256])]

        mk = memkv[:, 0, :].rearrange("p (b n) -> p b n", b=2)
        mem_keys = [(ALL, slice(0, 2), lambda t: mk[:, :, tok(t)])]

        def chunk_ready(ch):
            return lambda t: (chunk_evac, 2 * ch + t + 1)

        def rope_ready(r):
            return lambda t: (rope_done, 2 * r + t + 1)

        ev = evacuate(memA[1], mem_pieces(0), rs_mem)
        memV = (chunk_evac, 2)
        x1.append(half_around(lambda: turn_x(1, "a_norm_attn", 0), qk0, 0, 0, x1[0], "O"))
        rs_x = statistics(x, (x_landed, 16))
        mB = [half_around(lambda: turn_mem("b_mem_norm", 0, 2 * memA[1] + 2), qk0, 1, 0, x1[1], "O")]
        gain_s.append(s_use((gain_cols, 2))[0])
        bias_s = s_use((bias_vec, 1))
        constants = add("constants")
        constants.lam = col(5)
        mkA = turn_heads(zq[:, 0], [0, 1], mem_keys, chunk_ready(ev.chunk))[-1]
        zfree[0] = mkA + 1
        evacuate(qk0[1], [((0, 512), lambda t: zq[:, 1, t, :])], rs_x, bank="O")
        add("lambda").lam = constants.lam
        r0 = rope(1, 512, rope1)
        mB.append(half_around(lambda: turn_mem("b_mem_norm", 1, 2 * memA[1] + 2), vm, 0, 0, x1[0]))
        qk_pieces = lambda a: heads(0, a, 2) + pairs(2, 16 + a, 2)
        mul_chunk_half(vm, 1, 0, x1)
        ev = evacuate(vm[1], [((0, 256), lambda t: v[:, t, 512:768]), ((256, 512), lambda t: zq[:, 0, t, 0:256])],
                      rs_x, slot_free=zfree[0])

        def mem_item(p, t, qneed, kneed):
            return scores("mem", p, t, 6 + p, mk[:, p, :], max(qneed, kneed))

        def diff_item(h, t):
            return scores("diff", h, t, h, qk[:, 16 + h, :], h_use[h // 2])

        h_use = [turn_heads(zq[:, 1], [0, 1, 2, 3], qk_pieces(0), rope_ready(r0.rope))[-1]]
        zfree[1] = h_use[0] + 1
        multiply(v0[0], 0, 0, x1[0], "P", True, False, hold=True, tiles=[0])
        d = [diff_item(0, 0), diff_item(0, 1)]
        qm_use = turn_heads(zq[:, 0], [0, 1], heads(0, 6, 2), chunk_ready(ev.chunk))[-1]
        zfree[0] = qm_use + 1
        multiply(v0[0], 0, 0, x1[0], "P", True, False, hold=True, tiles=[1])
        mix(d[0]); mix(d[1])
        split(v0[0] + AHEAD)
        turn_weights(d[0]); turn_weights(d[1])
        d += [diff_item(1, 0), diff_item(1, 1)]
        multiply(v0[1], 0, UK, x1[1], "P", False, True, hold=True)
        mix(d[2]); mix(d[3])
        ev = evacuate(v0[1], [((0, 512), lambda t: v[:, t, 0:512])], rs_x)
        split(v0[1] + AHEAD)
        vneed = (chunk_evac, 2 * ev.chunk + 2)
        mul_chunk_half(qk1, 0, 0, x1)
        attend(d[0], vneed); attend(d[1], vneed); turn_weights(d[2]); turn_weights(d[3])
        m = [mem_item(0, 0, qm_use, mkA), mem_item(0, 1, qm_use, mkA)]
        norm(d[0:2])
        mul_chunk_half(qk1, 1, 0, x1, mixed=m[0:2])
        evacuate(qk1[1], [((0, 512), lambda t: zq[:, 1, t, :])], rs_x, slot_free=zfree[1])
        attend(d[2], vneed); attend(d[3], vneed); turn_weights(m[0]); turn_weights(m[1])
        m += [mem_item(1, 0, qm_use, mkA), mem_item(1, 1, qm_use, mkA)]
        norm(d[2:4])
        r1 = rope(1, 512, rope1)
        mul_chunk_half(qk2, 0, 0, x1, mixed=m[2:4])
        attend(m[0], memV); attend(m[1], memV); turn_weights(m[2]); turn_weights(m[3])
        mul_chunk_half(qk2, 1, 0, x1)
        evacuate(qk2[1], [((0, 512), lambda t: zq[:, 0, t, :])], rs_x, slot_free=zfree[0])
        r2 = rope(0, 512, rope1)
        h_use.append(turn_heads(zq[:, 1], [0, 1, 2, 3], qk_pieces(2), rope_ready(r1.rope))[-1])
        zfree[1] = h_use[1] + 1
        attend(m[2], memV); attend(m[3], memV)
        d += [diff_item(2, 0), diff_item(2, 1)]
        memB = chunk_units(A["b_w_mem_kv"][0], [(0, 512)])

        def mul_mem(h, t):
            multiply(memB[h], 1, UK * h, mB[h], "P", h == 0, h == 1, hold=True, tiles=[t])

        mul_mem(0, 0)
        mix(d[4]); mix(d[5])
        h_use.append(turn_heads(zq[:, 0], [0, 1, 2, 3], qk_pieces(4), rope_ready(r2.rope))[-1])
        zfree[0] = h_use[2] + 1
        turn_weights(d[4]); turn_weights(d[5])
        d += [diff_item(3, 0), diff_item(3, 1)]
        mul_mem(0, 1)
        mix(d[6]); mix(d[7])
        split(memB[0] + AHEAD)
        attend(d[4], vneed); attend(d[5], vneed); turn_weights(d[6]); turn_weights(d[7])
        d += [diff_item(4, 0), diff_item(4, 1)]
        norm(d[4:6])
        mul_mem(1, 0)
        mix(d[8]); mix(d[9])
        split(memB[1] + AHEAD)
        attend(d[6], vneed); o8 = attend(d[7], vneed); turn_weights(d[8]); turn_weights(d[9])
        d += [diff_item(5, 0), diff_item(5, 1)]
        norm(d[6:8])
        mul_mem(1, 1)
        mix(d[10]); mix(d[11])
        ev = evacuate(memB[1], mem_pieces(1), rs_mem, slot_free=zfree[1])
        memB_chunk = ev.chunk

        def finish_attention(w, items, o_half, last_qset_unit, oset, gain, vneed, around):
            ua, ub, uc, ud = out_units(w)
            o1 = turn_operand(o_nat, 0, [(None, oset, 0)], (o_evac, o_half), 2 * last_qset_unit + 2)[-1]
            attend(items[0], vneed); attend(items[1], vneed)
            turn_weights(items[2]); turn_weights(items[3])
            if items[0].kind == "diff":
                norm(items[0:2])

            def last_items():
                done = around()
                attend(items[2], vneed)
                o_all = attend(items[3], vneed)
                if items[0].kind == "diff":
                    norm(items[2:4])
                return o_all, done

            o_all, done = multiply_around(last_items, ua, oset, 0, o1, "P", True, False)
            split(ua + AHEAD)
            o2 = multiply_around(lambda: turn_operand(o_nat, 1, [(None, oset, UK)], (o_evac, o_all), 0)[-1],
                                 ub, oset, 0, o1, "S", True, False)
            return out_tail(ub, (uc, oset, UK, o2), (ud, oset, UK, o2), 1 - oset, gain), done

        def out_tail(u, third, fourth, xset, gain):
            multiply(*third, "P", False, True, hold=True)
            r = residual(0, "P", third[0], None)
            split(u + AHEAD)
            a = multiply_around(lambda: turn_operand(x, 0, [(gain, xset, 0)], (resid_done, r.r + 2), 0)[-1],
                                *fourth, "S", False, True)
            r = residual(1, "S", fourth[0], None)
            split(third[0] + AHEAD)
            return a, r

        def memory_keys():
            return turn_heads(zq[:, 1], [0, 1], mem_keys, chunk_ready(memB_chunk))[-1]

        (uses_a, r), mkB = finish_attention(A["a_w_out"][0], d[8:12], o8, qk2[1], 0, g_at("a_norm_mlp"), vneed,
                                            memory_keys)
        zfree[1] = mkB + 1

        def mlp_units(w_up, w_down):
            base = len(UNITS)
            up = lambda j: [unit(w_up, h * UK * P, [(j * COLS, COLS)]) for h in range(2)]
            down = lambda j: [unit(w_down, j * COLS, [(c * COLS, COLS)]) for c in range(2)]
            up(0)
            for j in range(CHUNKS - 1):
                up(j + 1)
                down(j)
            down(CHUNKS - 1)
            return base

        def mlp(w_up, w_down, hset, use0, r1, gain):
            base = mlp_units(w_up, w_down)
            use1 = multiply_around(lambda: turn_operand(x, 1, [(gain, hset, UK)], (resid_done, r1.r + 2), 0)[-1],
                                   base, hset, 0, use0, "O", True, False)
            split(base + AHEAD)
            stt = statistics(x, (resid_done, r1.r + 2), kind="square")
            multiply(base + 1, hset, UK, use1, "O", False, True)
            for t in range(NT):
                free["O", t] = (relu2_done, count.relu2 + t + 1)
            st = add("mlp")
            st.base, st.hset, st.uset, st.t0, st.hi0 = base, hset, 1 - hset, count.t, count.hi
            st.relu0, st.freed = count.relu2, {b: [free[b, t] for t in range(NT)] for b in "PSO"}
            st.w = (w_up, w_down)
            split_next[0] += 4 * (CHUNKS - 1)
            count.t += 2 * CHUNKS
            count.hi += 2 * CHUNKS
            count.relu2 += 2 * CHUNKS
            for t in range(NT):
                free["P", t] = (relu2_done, count.relu2 - 1 + t)
            return stt, base

        def mlp_end(base, gain, scale):
            ul = base + 4 * CHUNKS - 2
            mlp_step = STEPS[-1]
            uset, xset = mlp_step.uset, mlp_step.hset
            multiply(ul, uset, 0, count.t - 1, "S", False, True, hold=True)
            r0 = residual(0, "S", ul, scale)
            split(ul + AHEAD)
            hidden_use = count.t - 1
            a = multiply_around(lambda: turn_operand(x, 0, [(gain, xset, 0)], (resid_done, r0.r + 2), 0)[-1],
                                ul + 1, uset, 0, hidden_use, "O", False, True)
            return a, residual(1, "O", ul + 1, scale), ul + 1

        sc, base = mlp(A["a_w_up"][0], A["a_w_down"][0], 1, uses_a, r, g_at("a_norm_mlp"))
        a0, r1, last = mlp_end(base, g_at("b_norm_attn"), sc)
        w, wkv = A["b_w_in"][0], A["w_kv"]
        q1 = chunk_units(w, [(512, 512)])
        q0 = chunk_units(w, [(0, 512)])
        k0 = chunk_units(wkv, [(0, 512)])
        kv1 = chunk_units(wkv, [(512, 512)])
        v1 = chunk_units(wkv, [(1024, 512)])
        a1 = multiply_around(lambda: turn_operand(x, 1, [(g_at("b_norm_attn"), 1, UK)], (resid_done, r1.r + 2), 0)[-1],
                             q1[0], 1, 0, a0, "P", True, False)
        split(q1[0] + AHEAD)
        xb = [a0, a1]
        rs_b = statistics(x, (resid_done, r1.r + 2))
        mul_chunk_half(q1, 1, 1, xb)
        evacuate(q1[1], [((0, 512), lambda t: zq[:, 1, t, :])], rs_b, slot_free=zfree[1])
        r1_ = rope(1, 256, rope1)
        turn_kv = lambda h: turn_operand(x, h, [(g_at("kv_norm"), 0, UK * h)], (resid_done, r1.r + 2), 2 * last + 2)[-1]
        xk = [half_around(lambda: turn_kv(h), q0, h, 1, xb[h], "O") for h in range(2)]
        evacuate(q0[1], [((0, 512), lambda t: zq[:, 0, t, :])], rs_b, slot_free=zfree[0], bank="O")
        r0_ = rope(0, 512, rope1)
        qm_use = half_around(lambda: turn_heads(zq[:, 1], [0, 1, 2, 3], heads(0, 4, 4), rope_ready(r1_.rope))[-1],
                             k0, 0, 0, xk[0])
        zfree[1] = qm_use + 1
        m = [mem_item(0, 0, qm_use, mkB), mem_item(0, 1, qm_use, mkB)]
        mul_chunk_half(k0, 1, 0, xk, mixed=(m[0], m[1]))
        evacuate(k0[1], [((0, 512), lambda t: zq[:, 1, t, :])], rs_b, slot_free=zfree[1])
        r2_ = rope(1, 512, rope1)
        turn_weights(m[0]); turn_weights(m[1])
        m += [mem_item(1, 0, qm_use, mkB), mem_item(1, 1, qm_use, mkB)]
        q_use = turn_heads(zq[:, 0], [0, 1, 2, 3], heads(0, 0, 4), rope_ready(r0_.rope))[-1]
        zfree[0] = q_use + 1
        memV = (chunk_evac, 2 * memB_chunk + 2)
        mul_chunk_half(kv1, 0, 0, xk, mixed=(m[2], m[3]))
        attend(m[0], memV); attend(m[1], memV); turn_weights(m[2]); turn_weights(m[3])
        k_use = turn_heads(zq[:, 1], [0, 1, 2, 3], pairs(0, 16, 4), rope_ready(r2_.rope))[-1]
        zfree[1] = k_use + 1
        attend(m[2], memV); attend(m[3], memV)

        def causal_item(p, t):
            return scores("causal", p, t, p, qk[:, 16 + p, :], k_use if p < 4 else k2_use)

        c = [causal_item(0, 0), causal_item(0, 1)]
        mul_chunk_half(kv1, 1, 0, xk, mixed=(c[0], c[1]))
        ev = evacuate(kv1[1], [((0, 256), lambda t: zq[:, 0, t, 0:256]), ((256, 512), lambda t: v[:, t, 0:256])],
                      rs_b, slot_free=zfree[0])
        v_first = (chunk_evac, 2 * ev.chunk + 2)
        r3_ = rope(0, 256, rope1)
        turn_weights(c[0]); turn_weights(c[1])
        c += [causal_item(1, 0), causal_item(1, 1)]
        mul_chunk_half(v1, 0, 0, xk, mixed=(c[2], c[3]))
        k2_use = turn_heads(zq[:, 0], [0, 1], pairs(0, 20, 2), rope_ready(r3_.rope))[-1]
        zfree[0] = k2_use + 1
        attend(c[0], v_first); attend(c[1], v_first); turn_weights(c[2]); turn_weights(c[3])
        c += [causal_item(2, 0), causal_item(2, 1)]
        mul_chunk_half(v1, 1, 0, xk, mixed=(c[4], c[5]))
        ev = evacuate(v1[1], [((0, 512), lambda t: v[:, t, 256:768])], rs_b)
        v_all = (chunk_evac, 2 * ev.chunk + 2)
        attend(c[2], v_first); attend(c[3], v_first); turn_weights(c[4]); turn_weights(c[5])
        c += [causal_item(3, 0), causal_item(3, 1)]
        attend(c[4], v_all); attend(c[5], v_all)
        mix(c[6]); mix(c[7]); turn_weights(c[6]); turn_weights(c[7])
        c += [causal_item(4, 0), causal_item(4, 1)]
        attend(c[6], v_all); o8 = attend(c[7], v_all)
        mix(c[8]); mix(c[9]); turn_weights(c[8]); turn_weights(c[9])
        c += [causal_item(5, 0), causal_item(5, 1)]
        mix(c[10]); mix(c[11])
        (uses_a, r), _ = finish_attention(A["b_w_out"][0], c[8:12], o8, q0[1], 1, g_at("b_norm_mlp"), v_all,
                                          lambda: None)
        st = add("late_loads")
        st.o = count.o
        sc, base = mlp(A["b_w_up"][0], A["b_w_down"][0], 0, uses_a, r, g_at("b_norm_mlp"))

        a0, r1, last = mlp_end(base, g_at("norm1_w_2"), sc)
        w = A["w_in_2"][0]
        at = 512 + SMALL
        kb = [unit(w, 0, [(at + COLS, COLS)])]
        sm = chunk_units(w, [(512, SMALL)])
        kb.append(unit(w, UK * P, [(at + COLS, COLS)]))
        qb, vb, qa, gb = (chunk_units(w, [(c, COLS)]) for c in (at, at + 2 * COLS, 0, at + 3 * COLS))
        a1 = multiply_around(lambda: turn_operand(x, 1, [(g_at("norm1_w_2"), 0, UK)], (resid_done, r1.r + 2), 0)[-1],
                             kb[0], 0, 0, a0, "S", True, False)
        split(kb[0] + AHEAD)
        xb = [a0, a1]
        add("bias_load").u = last
        rs_2 = statistics(x, (resid_done, r1.r + 2), kind="final", factor=a1 + 1)
        mul_chunk_half(sm, 0, 0, xb)
        add("normed_statistics").st = rs_2
        mul_chunk_half(sm, 1, 0, xb)
        ev = evacuate(sm[1], [((0, SMALL), lambda t: zs[:, t, :])], rs_2)
        small = add("small_norm")
        small.chunk, small.ss, small.rs = ev.chunk, col(2), col(2)
        mul_chunk_half(kb, 1, 0, xb, "S")
        evacuate(kb[1], [((0, 512), lambda t: zq[:, 1, t, :])], rs_2, slot_free=zfree[1], bank="S")
        rk = rope(1, 512, rope2)
        mul_chunk_half(qb, 0, 0, xb, "O")
        INDEX_BLOCK = [8, 10, 9, 11]
        index_q = lambda h: (lambda t: qk[32 * h:32 * h + 32, INDEX_BLOCK[h]:INDEX_BLOCK[h] + 1, tok(t)])

        def turn_small():
            return turn_heads(sn[:, :, :, :].rearrange("p t b n -> p t (b n)"), [0, 1, 2],
                              [(slice(32 * h, 32 * h + 32), slice(0, 1), index_q(h)) for h in range(4)] +
                              pairs(1, Q_IK, 2), lambda t: (sn_done, t + 1))[-1]

        sn_use = half_around(turn_small, qb, 1, 0, xb[1], "O")
        evacuate(qb[1], [((0, 512), lambda t: zq[:, 0, t, :])], rs_2, slot_free=zfree[0], bank="O")
        rq = rope(0, 512, rope2)

        def index_scores(t):
            n = P * (t + 1)
            per = COLS // n
            st = add("index_scores")
            st.t, st.n, st.per, st.use, st.banks, st.dots = t, n, per, sn_use, [], count.dots
            st.m8, st.ind = col(8), col(4)
            for b in range(4 // per):
                count.dots += 1
                st.banks.append(s_use((dots_done, count.dots)))
            return st

        def retention_scores(p, after):
            st = add("retention_scores")
            st.p, st.use, st.banks, st.after = p, max(kb_use, qb_use), [], after
            for a in range(2):
                count.decayed += 1
                st.banks.append(s_use((decayed, count.decayed)))

        def retention_out(p):
            st = add("retention_out")
            st.p, st.need = p, vr_need
            st.o, st.o_free = o_use()
            return o_full, st.o + 1

        def idx_item(p, t):
            return scores("idx", p, t, p, qk[:, Q_KA, :], max(ka_use, qa_use))

        def select(ix, first, last):
            st = add("select")
            st.st, st.rounds = ix, (first, last)

        def step(kind, of):
            add(kind).st = of

        def tile(us, h, t, use):
            multiply(us[h], 0, UK * h, use[h], "P", h == 0, h == 1, hold=True, tiles=[t])

        tile(vb, 0, 0, xb)
        i0 = index_scores(0)
        kava = add("shared_kv")
        kava.use, kava.s, kava.ss, kava.rs = sn_use, s_use((kava_done, 1)), col(2), col(2)
        va_need = (kava_done, 1)
        step("index_sum", i0)
        step("shared_key_sum", kava)
        tile(vb, 0, 1, xb)
        split(vb[0] + AHEAD)
        i1 = index_scores(1)
        kb_use = turn_heads(zq[:, 1], [0, 1, 2, 3], heads(0, 4, 4), rope_ready(rk.rope))[-1]
        zfree[1] = kb_use + 1
        step("index_sum", i1)
        tile(vb, 1, 0, xb)
        select(i0, 0, 4)
        step("shared_key_norm", kava)
        qb_use = turn_heads(zq[:, 0], [0, 1, 2, 3], pairs(0, Q_QB, 4), rope_ready(rq.rope))[-1]
        zfree[0] = qb_use + 1
        tile(vb, 1, 1, xb)
        split(vb[1] + AHEAD)
        ev = evacuate(vb[1], [((0, 512), lambda t: v[:, t, 0:512])], rs_2)
        vr_need = (chunk_evac, 2 * ev.chunk + 2)
        retention_scores(0, rope_ready(rq.rope)(1))
        tile(qa, 0, 0, xb)
        r = retention_out(0)
        retention_scores(1, r)
        select(i0, 4, 8)
        tile(qa, 0, 1, xb)
        split(qa[0] + AHEAD)
        r = retention_out(1)
        retention_scores(2, r)
        ka_use = turn_heads(sn[:, :, 0, :].rearrange("p t n -> p t n"), [0], pairs(0, Q_KA, 1),
                            lambda t: (ka_done, t + 1))[-1]
        tile(qa, 1, 0, xb)
        r = retention_out(2)
        retention_scores(3, r)
        select(i1, 0, 4)
        tile(qa, 1, 1, xb)
        ev = evacuate(qa[1], [((0, 512), lambda t: zq[:, 0, t, :])], rs_2, slot_free=zfree[0])
        qn = add("query_norm")
        qn.chunk, qn.ss, qn.rs = ev.chunk, col(16), col(16)
        split(qa[1] + AHEAD)
        last = retention_out(3)
        group = add("group_center")
        group.o, group.mu, group.va, group.rs = last[1], col(16), col(16), col(16)
        step("query_scale", qn)
        tile(gb, 0, 0, xb)
        step("group_sum", group)
        tile(gb, 0, 1, xb)
        split(gb[0] + AHEAD)
        tile(gb, 1, 0, xb)
        qa_use = turn_heads(zq[:, 0], [0, 1, 2, 3], heads(0, 0, 4), lambda t: (qn_done, t + 1))[-1]
        zfree[0] = qa_use + 1
        st = add("gain_load")
        st.free = zfree[0]
        tile(gb, 1, 1, xb)
        d = [idx_item(0, 0), idx_item(1, 0)]
        step("group_scale", group)
        step("group_gain", group)
        mix(d[0]); mix(d[1])
        evacuate(gb[1], [((0, 512), lambda t: zq[:, 1, t, :])], rs_2, slot_free=zfree[1], silu=True)
        group.gate = (chunk_evac, 2 * count.chunk)
        turn_weights(d[0]); turn_weights(d[1])
        d += [idx_item(2, 0), idx_item(3, 0)]
        step("group_gate", group)
        attend(d[0], va_need); attend(d[1], va_need)
        mix(d[2]); mix(d[3])
        ua, ub, uc, ud = out_units(A["w_out_2"][0], (512, 0))
        o2 = turn_operand(o_nat, 1, [(None, 1, UK)], (ob_done, 2), 0)[-1]
        select(i1, 4, 8)
        split(gb[1] + AHEAD)
        multiply(ua, 1, UK, o2, "P", True, False, hold=True, tiles=[0])
        turn_weights(d[2]); turn_weights(d[3])
        d += [idx_item(0, 1), idx_item(1, 1)]
        attend(d[2], va_need); attend(d[3], va_need)
        multiply(ua, 1, UK, o2, "P", True, False, hold=True, tiles=[1])
        mix(d[4]); mix(d[5]); turn_weights(d[4]); turn_weights(d[5])
        d += [idx_item(2, 1), idx_item(3, 1)]
        attend(d[4], va_need); attend(d[5], va_need)
        multiply(ub, 1, UK, o2, "S", True, False, hold=True, tiles=[0])
        mix(d[6]); mix(d[7]); turn_weights(d[6]); turn_weights(d[7])
        attend(d[6], va_need)
        o_a = attend(d[7], va_need)
        o1 = turn_operand(o_nat, 0, [(None, 1, 0)], (o_evac, o_a), 0)[-1]
        multiply(ub, 1, UK, o2, "S", True, False, hold=True, tiles=[1])
        split(ua + AHEAD)
        uses_a, r = out_tail(ub, (uc, 1, 0, o1), (ud, 1, 0, o1), 0, g_at("norm2_w_2"))

        fbase = len(UNITS)
        gate_up = lambda j: [unit_gate(j, h) for h in range(2)]

        def unit_gate(j, h):
            n = 2 * FCHUNK
            parts = [(A[nm][0][h * UK * P:(h + 1) * UK * P, j * FCHUNK:(j + 1) * FCHUNK]
                      .rearrange("(k p) n -> p k n", p=P), slice(0, UK), slice(i * FCHUNK, (i + 1) * FCHUNK))
                     for i, nm in enumerate(("w_gate_2", "w_up_2"))]
            un = Step()
            un.n, un.nk, un.parts = n, UK, parts
            UNITS.append(un)
            return len(UNITS) - 1

        def unit_fdown(j):
            return unit(A["w_down_2"][0], j * FCHUNK, [(0, D)], nk=2)

        gate_up(0)
        for j in range(FCHUNKS - 1):
            gate_up(j + 1)
            unit_fdown(j)
        unit_fdown(FCHUNKS - 1)
        use1 = multiply_around(lambda: turn_operand(x, 1, [(g_at("norm2_w_2"), 0, UK)], (resid_done, r.r + 2), 0)[-1],
                               fbase, 0, 0, uses_a, "O", True, False)
        split(fbase + AHEAD)
        rs_f = statistics(x, (resid_done, r.r + 2))
        multiply(fbase + 1, 0, UK, use1, "O", False, True)
        for t in range(NT):
            free["O", t] = (relu2_done, count.relu2 + t + 1)
        st = add("ffn")
        st.base, st.uset, st.hset, st.t0, st.hi0 = fbase, 1, 0, count.t, count.hi
        st.relu0, st.rs = count.relu2, rs_f
        st.freed = {b: [free[b, t] for t in range(NT)] for b in "PSO"}
        st = add("store")
        st.u, st.rs, st.r = len(UNITS) - 1, rs_f, count.resid

        N_UNITS = len(UNITS)
        slot, prev, fills = [], [], []
        owner, filled = [None] * RING, [0] * RING
        for u in range(N_UNITS):
            s = u % RING if u < fbase else (fbase + (u - fbase) % FRING) % RING
            slot.append(s)
            prev.append(owner[s])
            owner[s] = u
            filled[s] += 1
            fills.append(filled[s])
        assert fbase % RING == 0

        def shaped(buf, u):
            un = UNITS[u]
            return buf[:, slot[u], 0:un.nk * un.n].rearrange("p (k n) -> p k n", k=un.nk)

        out_rows = out[0].rearrange("(t p) n -> p t n", p=P)

        block = ctx.enter_context(nc.Block())

        @block.sync
        def _(sp):
            def load(u):
                if prev[u] is not None:
                    sp.wait_ge(hi_done, prev[u] + 1)
                    sp.wait_ge(lo_done, prev[u] + 1)
                dst = shaped(raw, u)
                for src, ks, cs in UNITS[u].parts:
                    sp.dma_start(dst[:, ks, cs], src).then_inc(landed[slot[u]], 16)

            def load_mlp(base, w_up, w_down):
                with sp.Fori(0, CHUNKS - 1) as j:
                    for c in range(4):
                        u = base + 2 + c
                        sp.wait_ge(hi_done, j * 4 + (prev[u] + 1))
                        sp.wait_ge(lo_done, j * 4 + (prev[u] + 1))
                        dst = shaped(raw, u)
                        for i in range(2):
                            if c < 2:
                                rows = (c * UK + 2 * i) * P
                                src = w_up[rows:rows + 2 * P, bass.ds(j * COLS + COLS, COLS)]
                            else:
                                src = w_down[bass.ds(j * COLS + 2 * i * P, 2 * P), (c - 2) * COLS:(c - 1) * COLS]
                            sp.dma_start(dst[:, 2 * i:2 * i + 2, :], src.rearrange("(k p) n -> p k n", p=P))\
                              .then_inc(landed[slot[u]], 16)

            def load_ffn(base):
                with sp.Fori(1, FCHUNKS - 2) as j:
                    for c in range(3):
                        u = base + 2 + 3 + c
                        sp.wait_ge(hi_done, j * 3 + (prev[u] + 1 - 3))
                        sp.wait_ge(lo_done, j * 3 + (prev[u] + 1 - 3))
                        dst = shaped(raw, u)
                        for i in range(2):
                            if c < 2:
                                wsrc = A[("w_gate_2", "w_up_2")[i]][0]
                                src = wsrc[c * UK * P:(c + 1) * UK * P, bass.ds(j * FCHUNK + FCHUNK, FCHUNK)]
                                d_ = dst[:, :, i * FCHUNK:(i + 1) * FCHUNK]
                            else:
                                src = A["w_down_2"][0][bass.ds(j * FCHUNK + i * P, P), :]
                                d_ = dst[:, i:i + 1, :]
                            sp.dma_start(d_, src.rearrange("(k p) n -> p k n", p=P)).then_inc(landed[slot[u]], 16)

            def load_gains(group):
                names = (GAINS[:FIRST], GAINS[FIRST:])[group]
                for i, g in enumerate(names):
                    g_ap = A[g] if len(A[g].shape) == 1 else A[g][0]
                    sp.dma_start(grow[group][i * KT:(i + 1) * KT, :], g_ap.rearrange("(k p) -> k p", p=P))\
                      .then_inc(gains_landed[group], 16)

            def load_constants():
                load_gains(1)
                def spread(dst, src):
                    sp.dma_start(dst, src.partition_broadcast(P)).then_inc(consts_landed, 16)
                spread(subln[:], A["a_subln"][0])
                sp.dma_start(rt[:, 0, 0:256], A["a_lambda"][0].rearrange("a d -> (a d)").partition_broadcast(P))\
                   .then_inc(consts_landed, 16)
                spread(kvn[:], A["kv_norm_w_2"][0])
                spread(qkn[:, 0, :], A["q_norm_w_2"][0])
                spread(qkn[:, 1, :], A["k_norm_w_2"][0])
                for dst, name in ((rope1, "rope1"), (rope2, "rope2"), (dec, "decays")):
                    sp.dma_start(dst[:], A[name].rearrange("(t p) n -> p t n", p=P)).then_inc(consts_landed, 16)
                sp.dma_start(onehot, A["bucket_onehot"]).then_inc(consts_landed, 16)
                sp.dma_start(rel8[:], A["rel_bias_2"]).then_inc(consts_landed, 16)
                sp.dma_start(wukv[:, 0, :], A["w_uk_2"][0]).then_inc(consts_landed, 16)
                sp.dma_start(wukv[:, 1, :], A["w_uv_2"][0]).then_inc(consts_landed, 16)

            mlps = {st.base: st.w for st in STEPS if st.kind == "mlp"}

            def load_memory(h):
                cols = slice(h * COLS, (h + 1) * COLS)
                sp.dma_start(mem_nat[:, :, cols], A["mem"][0][:, cols].rearrange("(t p) n -> p t n", p=P))\
                  .then_inc(mem_landed[h], 16)

            load_memory(0)
            load_gains(0)
            u = 0
            while u < N_UNITS:
                if u == 1:
                    load_memory(1)
                if u == 2:
                    sp.dma_start(x[:], A["x"][0].rearrange("(t p) n -> p t n", p=P)).then_inc(x_landed, 16)
                if u == RING:
                    load_constants()
                if u - 2 in mlps:
                    load_mlp(u - 2, *mlps[u - 2])
                    u += 4 * (CHUNKS - 1)
                elif u == fbase + 5:
                    load_ffn(fbase)
                    u += 3 * (FCHUNKS - 3)
                else:
                    load(u)
                    u += 1
            last = STEPS[-1]
            for i, (half, t) in enumerate((c, t) for c in range(2) for t in range(NT)):
                sp.wait_ge(resid_done, last.r + i + 1)
                sp.dma_start(out_rows[:, t, half * COLS:(half + 1) * COLS], x[:, t, half * COLS:(half + 1) * COLS])\
                  .then_inc(stored, 16)
            sp.wait_ge(stored, 16 * 4)

        @block.gpsimd
        def _(pool):
            chain = [0]

            def behind(ins):
                chain[0] += 1
                ins.then_inc(pool_chain, 1)
                pool.wait_ge(pool_chain, chain[0])

            def inverse_rms(dst, ss, n, eps=EPS):
                width = dst.shape[1]
                var, r2 = newton[:, 0, 0:width], newton[:, 1, 0:width]
                behind(pool.tensor_scalar(var, ss, 1.0 / n, eps, ALU.mult, ALU.add))
                behind(pool.tensor_tensor(dst, var, minus_half[:, 0:width], ALU.pow))
                behind(pool.tensor_tensor(r2, dst, dst, ALU.mult))
                behind(pool.tensor_tensor(r2, r2, var, ALU.mult))
                behind(pool.tensor_scalar(r2, r2, -0.5, 1.5, ALU.mult, ALU.add))
                return pool.tensor_tensor(dst, dst, r2, ALU.mult)

            sums = [0]

            def inverse_of_sums(dst, ss, n, eps=EPS):
                sums[0] += 1
                pool.wait_ge(sum_done, sums[0])
                inverse_rms(dst, ss, n, eps).then_inc(inverse_done, 1)

            def do_rope(st):
                nh = st.n // DH
                for t in range(NT):
                    pool.wait_ge(chunk_evac, 2 * (st.chunk - 1) + t + 1)
                    if st.rope or t:
                        pool.wait_ge(rope_done, 2 * st.rope + t)
                    z = zq[:, st.slot, t, 0:st.n].rearrange("p (h d) -> p h d", d=DH)
                    zh = zq[:, st.slot, t, 0:st.n].rearrange("p (h x d) -> p h x d", x=2, d=DH // 2)
                    t1 = rt[:, 0, 0:st.n].rearrange("p (h d) -> p h d", d=DH)
                    t2 = rt[:, 1, 0:st.n].rearrange("p (h x d) -> p h x d", x=2, d=DH // 2)
                    cos = st.table[:, t, 0:64].unsqueeze(1).broadcast_to([P, nh, DH])
                    pool.tensor_tensor(t1, z, cos, ALU.mult)
                    for i in range(2):
                        sin = st.table[:, t, 64 + 32 * i:96 + 32 * i].unsqueeze(1).broadcast_to([P, nh, DH // 2])
                        last = pool.tensor_tensor(t2[:, :, i, :], zh[:, :, 1 - i, :], sin, ALU.mult)
                    behind(last)
                    pool.tensor_tensor(zq[:, st.slot, t, 0:st.n], rt[:, 0, 0:st.n], rt[:, 1, 0:st.n], ALU.add)\
                        .then_inc(rope_done, 1)

            for st in STEPS:
                if st.kind == "setup":
                    behind(pool.memset(ident[:], 0.0))
                    pool.affine_select(out=ident[:], in_=ident[:], compare_op=ALU.not_equal, fill=1.0, base=0,
                                       pattern=[[-1, P]], channel_multiplier=1).then_inc(consts_made, 1)
                    pool.memset(minus_half[:], -0.5)
                    pool.memset(tri[:], 1.0)
                    pool.memset(flip[:], 0.0)
                    pool.memset(identb[:], 0.0)
                    behind(pool.memset(cmask[:], 0.0))
                    pool.affine_select(out=identb[:], in_=identb[:], compare_op=ALU.not_equal, fill=1.0, base=0,
                                       pattern=[[-1, P]], channel_multiplier=1).then_inc(consts_made, 1)
                    pool.affine_select(out=flip[:], in_=flip[:], compare_op=ALU.not_equal, fill=1.0 / SCALE,
                                       base=1 - P, pattern=[[1, P]], channel_multiplier=1).then_inc(consts_made, 1)
                    pool.affine_select(out=cmask[:], in_=cmask[:], compare_op=ALU.is_ge, fill=NEG, base=0,
                                       pattern=[[-1, P]], channel_multiplier=1).then_inc(consts_made, 1)
                    pool.affine_select(out=tri[:], in_=tri[:], compare_op=ALU.is_ge, fill=0.0, base=0,
                                       pattern=[[1, P]], channel_multiplier=-1).then_inc(consts_made, 1)
                    pool.memset(qk[:, 0:16, :], 0.0).then_inc(heads_zeroed, 1)
                elif st.kind == "constants":
                    pool.wait_ge(bias_vec, 1)
                    pool.dma_start(bias_dram, biasvec).then_inc(bias_stored, 16)
                elif st.kind == "lambda":
                    pool.wait_ge(lam_done, 1)
                elif st.kind == "rope":
                    do_rope(st)
                elif st.kind == "statistics":
                    pool.wait_ge(ss_done, st.sums + 1)
                    ins = inverse_rms(st.rs, st.ss, D)
                    if st.what == "square":
                        behind(ins)
                        ins = pool.tensor_tensor(st.rs, st.rs, st.rs, ALU.mult)
                    ins.then_inc(rstd_done, 1)
                    if st.what == "final":
                        pool.wait_ge(ss_done, st.sums + 2)
                        behind(inverse_rms(st.r2, st.ss2, D))
                        pool.tensor_tensor(st.rs, st.rs, st.r2, ALU.mult).then_inc(rstd_done, 1)
                elif st.kind == "diff_norm":
                    pool.wait_ge(osq_done, st.items[1].osq)
                    inverse_rms(st.ors, st.oss, P).then_inc(inverse_done, 1)
                elif st.kind == "late_loads":
                    pool.wait_ge(o_evac, st.o)
                    pool.memset(qk[:, 0:16, :], 0.0).then_inc(heads_zeroed, 1)
                elif st.kind == "query_norm":
                    inverse_of_sums(st.rs, st.ss, DH)
                elif st.kind == "small_norm":
                    inverse_of_sums(st.rs, st.ss, P)
                elif st.kind == "shared_key_sum":
                    inverse_of_sums(st.st.rs, st.st.ss, DH)
                elif st.kind == "group_sum":
                    inverse_of_sums(st.st.rs, st.st.va, DH, GN_EPS)
                elif st.kind == "group_gate":
                    y = o_nat[:, 0, 512:1024]
                    pool.wait_ge(yn_done, 1)
                    pool.wait_ge(gn_landed, 32)
                    behind(pool.tensor_tensor(y, y, gn[:, 0, :], ALU.mult))
                    behind(pool.tensor_tensor(y, y, gn[:, 1, :], ALU.add))
                    pool.wait_ge(*st.st.gate)
                    pool.tensor_tensor(y, y, zq[:, 1, 0, :], ALU.mult).then_inc(ob_done, 1)

        @block.scalar
        def _(act):
            def split_hi(u):
                if u >= N_UNITS:
                    return
                act.wait_ge(landed[slot[u]], 32 * fills[u])
                if prev[u] is not None:
                    act.wait_ge(mul_done, 2 * prev[u] + 2)
                act.activation(shaped(whi, u), shaped(raw, u), ACT.Copy).then_inc(hi_done, 1)

            def split_hi_loop(u, j, j0, per):
                act.wait_ge(landed[slot[u]], j * 32 + (32 * fills[u] - 32 * j0))
                act.wait_ge(mul_done, j * (2 * per) + (2 * prev[u] + 2 - 2 * per * j0))
                act.activation(shaped(whi, u), shaped(raw, u), ACT.Copy).then_inc(hi_done, 1)

            def mlp_chunk(st, j, peel, last=False):
                u0 = st.base + 2 + AHEAD + (4 * peel)
                one = (lambda u: split_hi(u)) if isinstance(j, int) else (lambda u: split_hi_loop(u, j, peel, 4))
                one(u0)
                hidden_hi(st, j, UK, 2)
                one(u0 + 1)
                relu(j * 8 + (2 * st.base + 6))
                one(u0 + 2)
                if last:
                    hidden_hi(st, j + 1, 0, 2)
                one(u0 + 3)

            def relu(multiplied, bank=Pb):
                for t in range(NT):
                    act.wait_ge(mul_done, multiplied + (t + 1))
                    act.activation(hidden[:, t, :], bank[t][:], ACT.Relu).then_inc(relu_done, 1)

            def ffn_chunk(st, j, peel):
                u0 = st.base + 2 + AHEAD + 3 * peel
                one = (lambda u: split_hi(u)) if isinstance(j, int) else (lambda u: split_hi_loop(u, j, peel, 3))
                one(u0)
                hidden_hi(st, j, 0, 1)
                one(u0 + 1)
                silu(st, j * 6 + (2 * st.base + 6))
                one(u0 + 2)

            def hidden_hi(st, j, k0, per):
                for b in range(2):
                    act.wait_ge(t_full, j * 2 + (st.t0 + b + 1))
                    k = k0 + per * b
                    act.activation(set_hi[st.uset][:, k:k + per, :], Tb[(st.t0 + b) % 2][:, 0:per * TOK], ACT.Copy)\
                       .then_inc(t_hi, 1)

            def silu(st, multiplied, bank=Pb):
                for t in range(NT):
                    act.wait_ge(mul_done, multiplied + (t + 1))
                    act.activation(zq[:, 1, t, 0:FCHUNK], bank[t][:, 0:FCHUNK], ACT.Silu, scale=st.rs.rs[:, t:t + 1])\
                       .then_inc(silu_done, 1)

            def biases(h):
                return bass.AP(bias_dram.tensor, h * 512, [[1, P], [512, 4], [1, TOK]])

            banks = {"P": Pb, "S": Sb, "O": Ob}

            for st in STEPS:
                if st.kind == "lambda":
                    act.wait_ge(heads_zeroed, 1)
                    act.wait_ge(lam_sum, 1)
                    act.activation(st.lam[:, 2:4], st.lam[:, 0:2], ACT.Exp).then_inc(lam_exp, 1)
                elif st.kind == "split":
                    split_hi(st.u)
                elif st.kind == "statistics":
                    act.wait_ge(*st.ready)
                    if st.src is mem_nat:
                        act.wait_ge(mem_landed[0], 16)
                    for t in range(NT):
                        ins = act.activation(junk[:, t, :], st.src[:, t, :], ACT.Square, accum_out=st.ss[:, t:t + 1])
                    ins.then_inc(ss_done, 1)
                elif st.kind == "normed_statistics":
                    act.wait_ge(x_normed, 1)
                    act.wait_ge(ss_done, st.st.sums + 1)
                    for t in range(NT):
                        ins = act.activation(junk[:, t, :], x[:, t, :], ACT.Square, accum_out=st.st.ss2[:, t:t + 1])
                    ins.then_inc(ss_done, 1)
                elif st.kind == "turn_operand":
                    for b in range(2):
                        n = st.use[b]
                        act.wait_ge(t_full, n + 1)
                        if st.set_free and b == 0:
                            act.wait_ge(mul_done, st.set_free)
                        for g, s, k0 in st.gains:
                            k = k0 + 2 * b
                            if g is None:
                                ins = act.activation(set_hi[s][:, k:k + 2, :], Tb[n % 2][:], ACT.Copy)
                            else:
                                kk = 4 * st.half + 2 * b
                                act.wait_ge(gain_cols, 1 if g < FIRST * KT else 3)
                                for i in range(2):
                                    ins = act.activation(set_hi[s][:, k + i, :], Tb[n % 2][:, i * TOK:(i + 1) * TOK],
                                                         ACT.Copy, scale=gcol[:, g + kk + i:g + kk + i + 1])
                        ins.then_inc(t_hi, 1)
                elif st.kind == "evacuate":
                    act.wait_ge(rstd_done, st.scale.n_done)
                    for t in range(NT):
                        act.wait_ge(mul_done, 2 * st.u + t + 1)
                        if st.slot_free and t == 0:
                            act.wait_ge(t_full, st.slot_free)
                        for i, ((a, b), dst) in enumerate(st.pieces):
                            ins = act.activation(dst(t), banks[st.bank][t][:, a:b], ACT.Silu if st.silu else ACT.Copy,
                                                 scale=st.scale.rs[:, t:t + 1])
                        ins.then_inc(chunk_evac, 1)
                elif st.kind == "turn_heads":
                    for t in range(NT):
                        n = st.use[t]
                        act.wait_ge(t_full, n + 1)
                        T = Tb[n % 2][:].rearrange("p (b n) -> p b n", b=4)
                        for ps, bs, dst in st.pieces:
                            ins = act.activation(dst(t), T[ps, bs, :], ACT.Copy)
                        ins.then_inc(t_evac[n % 2], 1)
                elif st.kind == "turn_weights":
                    it = st.it
                    act.wait_ge(t_full, it.use + 1)
                    if it.before:
                        act.wait_ge(o_full, it.before.o + 1)
                    m = it.n * (1 if it.kind == "diff" else 2)
                    act.activation(wT[:, it.buf, 0:m], Tb[it.use % 2][:, 0:m], ACT.Copy)\
                       .then_inc(t_evac[it.use % 2], 1)
                elif st.kind == "small_norm":
                    act.wait_ge(heads_zeroed, 2)
                elif st.kind == "scores":
                    it = st.it
                    act.wait_ge(nmax_done, it.i + 1)
                    if it.i == 0:
                        act.wait_ge(bias_stored, 16)
                    if it.before:
                        act.wait_ge(t_full, it.before.use + 1)
                    for c in range(2):
                        dst = e[:, it.buf, c * it.n:(c + 1) * it.n]
                        src = Sb[it.s % 2][:, c * it.n:(c + 1) * it.n]
                        ins = act.activation(dst, src, ACT.Exp, bias=it.nm[:, c:c + 1], scale=SCALE,
                                             accum_out=it.rs[:, c:c + 1])
                    ins.then_inc(exp_done, 1)
                elif st.kind == "attend":
                    it = st.it
                    if it.kind == "diff":
                        act.wait_ge(o_full, it.o + 1)
                        if it.osq > 1:
                            act.wait_ge(osq_done, it.osq - 1)
                        act.activation(junk1[:], Ob[it.o % 2][:, 0:P], ACT.Square, accum_out=it.oss).then_inc(osq_done, 1)
                elif st.kind == "late_loads":
                    act.wait_ge(o_evac, st.o)
                    act.dma_start(fgb, A["final_norm"].partition_broadcast(P)).then_inc(late_landed, 16)
                elif st.kind == "bias_load":
                    act.wait_ge(mul_done, 2 * st.u + 2)
                    for i in range(2):
                        act.dma_start(btoep[i], biases(4 * i)).then_inc(bias_landed, 16)
                elif st.kind == "gain_load":
                    act.wait_ge(t_full, st.free)
                    for i, g in enumerate(("ret_gn_w_2", "ret_gn_b_2")):
                        act.dma_start(gn[:, i, :], A[g][0].partition_broadcast(P)).then_inc(gn_landed, 16)
                elif st.kind == "index_scores":
                    for b in range(4 // st.per):
                        s = st.banks[b][0]
                        act.wait_ge(s_full, s + 1)
                        if st.t == 1 and b == 0:
                            act.wait_ge(dots_used, 1)
                        act.activation(relu_dots[:, b * st.per:(b + 1) * st.per, 0:st.n],
                                       Sb[s % 2][:, 0:st.per * st.n].rearrange("p (h n) -> p h n", h=st.per),
                                       ACT.Relu, scale=IDX_SCALE).then_inc(dots_done, 1)
                elif st.kind == "query_norm":
                    for t in range(NT):
                        act.wait_ge(chunk_evac, 2 * st.chunk + t + 1)
                        act.activation(query_sq[:, t, :], zq[:, 0, t, :], ACT.Square).then_inc(qsq_done, 1)
                elif st.kind == "group_center":
                    for t in range(NT):
                        act.wait_ge(yc_done, t + 1)
                        act.activation(rt[:, t, :], o_nat[:, t, 512:1024], ACT.Square).then_inc(ysq_done, 1)
                elif st.kind == "shared_kv":
                    s = st.s[0]
                    act.wait_ge(s_full, s + 1)
                    for t in range(NT):
                        act.activation(sn[:, t, 1, 0:DH], Sb[s % 2][:, t * P:t * P + DH], ACT.Copy)
                        ins = act.activation(v[:, t, 512:512 + DH], Sb[s % 2][:, t * P + DH:t * P + P], ACT.Copy)
                    ins.then_inc(kava_done, 1)
                elif st.kind == "mlp":
                    relu(2 * (st.base + 1), Ob)
                    mlp_chunk(st, 0, 0)
                    with act.Fori(1, CHUNKS - 2) as j:
                        mlp_chunk(st, j, 1)
                    mlp_chunk(st, CHUNKS - 2, CHUNKS - 2, last=True)
                elif st.kind == "ffn":
                    act.wait_ge(rstd_done, st.rs.n_done)
                    silu(st, 2 * (st.base + 1), Ob)
                    ffn_chunk(st, 0, 0)
                    with act.Fori(1, FCHUNKS - 2) as j:
                        ffn_chunk(st, j, 1)
                    ffn_chunk(st, FCHUNKS - 2, FCHUNKS - 2)
                    hidden_hi(st, FCHUNKS - 1, 2, 1)

        @block.tensor
        def _(pe):
            def wait(pair):
                if pair is not None:
                    pe.wait_ge(*pair)

            def wait_turned(n):
                wait(turned(n - 1))
                wait(turned(n))

            def products(out_, hi, lo, wh, wl, start, stop):
                pe.matmul(out_, hi, wh, start=start, stop=False)
                pe.matmul(out_, hi, wl, start=False, stop=False)
                return pe.matmul(out_, lo, wh, start=False, stop=stop)

            def half_unit(u, t, lhs, k0, out_, start, stop):
                n = UNITS[u].n
                wh, wl = shaped(whi, u), shaped(wlo, u)
                for k in range(UK):
                    ins = products(out_[:, 0:n], set_hi[lhs][:, k0 + k, tok(t)], set_lo[lhs][:, k0 + k, tok(t)],
                                   wh[:, k, :], wl[:, k, :], start and k == 0, stop and k == UK - 1)
                ins.then_inc(mul_done, 1)

            banks = {"P": Pb, "S": Sb, "O": Ob}

            def turn_gains(group):
                n = (FIRST, len(GAINS) - FIRST)[group] * KT
                pe.wait_ge(gains_landed[group], 16 * (n // KT))
                if group:
                    pe.wait_ge(gain_cols, 1)
                pe.transpose(Sb[gain_s[group] % 2][:, 0:n], grow[group], ident[0:n, 0:n]).then_inc(s_full, 1)

            def turn_bank(n, src, tiles):
                for i, k in enumerate(tiles):
                    for t in range(NT):
                        at = (i * NT + t) * P
                        ins = pe.transpose(Tb[n % 2][:, at:at + P], src(t, k), ident[:])
                ins.then_inc(t_full, 1)

            def hidden_block(t, k):
                return hidden[:, t, k * P:(k + 1) * P]

            def mlp_chunk(st, j, peel, first, last=False):
                u0 = st.base + 2 + 4 * peel
                at = lambda base, per: j * per + (base - per * peel)
                for h in range(2):
                    u = u0 + h
                    pe.wait_ge(lo_done, at(u + 1, 4))
                    for t in range(NT):
                        if h == 0 and first:
                            wait(st.freed["P"][t])
                        elif h == 0:
                            pe.wait_ge(relu2_done, at(st.relu0 + 2 * peel + t + 1, 2))
                        half_unit(u, t, st.hset, UK * h, Pb[t], h == 0, h == 1)
                    if h == 0:
                        hidden_turns(st, j)
                hidden_operand(st, j)
                for c, b in enumerate("SO"):
                    u = u0 + 2 + c
                    pe.wait_ge(lo_done, at(u + 1, 4))
                    for t in range(NT):
                        if first:
                            wait(st.freed[b][t])
                        half_unit(u, t, st.uset, UK, banks[b][t], first, False)
                    if last and c == 0:
                        hidden_turns(st, j + 1)

            def hidden_operand(st, j):
                for n in range(st.t0, st.t0 + 2):
                    pe.wait_ge(t_evac[n % 2], j + (n // 2 + 1))

            def hidden_turns(st, j):
                pe.wait_ge(relu2_done, j * 2 + (st.relu0 + 2))
                for b in range(2):
                    n = st.t0 + b
                    pe.wait_ge(t_evac[n % 2], j + n // 2)
                    turn_bank(st.t0 + b, hidden_block, [2 * b, 2 * b + 1])

            def ffn_down(st, u, k0, first, last, between=None):
                wh, wl = shaped(whi, u), shaped(wlo, u)
                for c, b in enumerate("SO"):
                    for t in range(NT):
                        if first:
                            wait(st.freed[b][t])
                        for k in range(2):
                            cs = slice(c * COLS, (c + 1) * COLS)
                            ins = products(banks[b][t][:], set_hi[st.uset][:, k0 + k, tok(t)],
                                           set_lo[st.uset][:, k0 + k, tok(t)],
                                           wh[:, k, cs], wl[:, k, cs], first and k == 0, last and k == 1)
                        if last or c == 1:
                            ins.then_inc(mul_done, 1)
                    if between and c == 0:
                        between()

            def ffn_turns(st, j):
                pe.wait_ge(relu2_done, j * 2 + (st.relu0 + 2))
                for b in range(2):
                    n = st.t0 + b
                    pe.wait_ge(t_evac[n % 2], j + n // 2)
                    turn_bank(st.t0 + b, hidden_block, [b])

            def ffn_chunk(st, j, peel, first, between=None):
                u0 = st.base + 2 + 3 * peel
                at = lambda base, per: j * per + (base - per * peel)
                for h in range(2):
                    u = u0 + h
                    pe.wait_ge(lo_done, at(u + 1, 3))
                    for t in range(NT):
                        if h == 0 and first:
                            wait(st.freed["P"][t])
                        elif h == 0:
                            pe.wait_ge(relu2_done, at(st.relu0 + 2 * peel + t + 1, 2))
                        half_unit(u, t, st.hset, UK * h, Pb[t], h == 0, h == 1)
                    if h == 0:
                        ffn_turns(st, j)
                hidden_operand(st, j)
                pe.wait_ge(lo_done, at(u0 + 3, 3))
                ffn_down(st, u0 + 2, 0, first, False, between)

            for st in STEPS:
                if st.kind == "setup":
                    pe.wait_ge(consts_made, 1)
                    turn_gains(0)
                elif st.kind == "constants":
                    pe.wait_ge(consts_made, 5)
                    turn_gains(1)
                    pe.wait_ge(consts_landed, CONSTS)
                    pe.matmul(Sb[bias_s[0] % 2][0:8, :], rel8[:], onehot, start=True, stop=True).then_inc(s_full, 1)
                elif st.kind == "turn_operand":
                    wait(st.ready)
                    for b in range(2):
                        n = st.use[b]
                        if n >= 2:
                            wait(turned(n - 2))
                        k0 = UK * st.half + 2 * b
                        turn_bank(n, lambda t, k: st.src[:, t, k * P:(k + 1) * P], [k0, k0 + 1])
                elif st.kind == "multiply":
                    wait_turned(st.use)
                    pe.wait_ge(lo_done, st.u + 1)
                    for t in st.tiles:
                        if st.start:
                            wait(st.freed[t])
                        half_unit(st.u, t, st.lhs, st.k0, banks[st.bank][t], st.start, st.stop)
                elif st.kind == "turn_heads":
                    for t in range(NT):
                        n = st.use[t]
                        pe.wait_ge(*st.ready(t))
                        wait(turned(n - 2))
                        for i, b in enumerate(st.blocks):
                            ins = pe.transpose(Tb[n % 2][:, i * P:(i + 1) * P], st.src[:, t, b * P:(b + 1) * P],
                                               ident[:])
                        ins.then_inc(t_full, 1)
                elif st.kind == "scores":
                    it = st.it
                    wait_turned(it.need)
                    wait(it.s_free)
                    if it.kind == "idx":
                        pe.wait_ge(sel_done, it.t + 1)
                        pe.wait_ge(bias_landed, 32)
                    S = Sb[it.s % 2]
                    for c in range(2):
                        o = c * it.n
                        ins = pe.matmul(S[:, o:o + it.n], headq[:, it.q, c, tok(it.t)], it.k[:, 0:it.n],
                                        start=True, stop=it.kind == "mem")
                        if it.kind == "idx":
                            c0 = P - P * it.t
                            pe.matmul(S[:, o:o + it.n], flip[:], btoep[it.pair // 2][:, 2 * it.pair % 4 + c, c0:c0 + it.n],
                                      start=False, stop=False)
                            ins = pe.matmul(S[:, o:o + it.n], identb[:], selmask[:, it.t, 0:it.n],
                                            start=False, stop=True)
                        elif it.kind != "mem":
                            ins = pe.matmul(S[:, o + it.n - P:o + it.n], identb[:], cmask[:], start=False, stop=True)
                    ins.then_inc(s_full, 1)
                elif st.kind == "turn_weights":
                    it = st.it
                    if it.kind == "diff":
                        pe.wait_ge(w_done, it.w)
                    else:
                        pe.wait_ge(exp_done, it.exp + 1)
                    wait(turned(it.use - 2))
                    nb = it.n // P * (1 if it.kind == "diff" else 2)
                    for b in range(nb):
                        ins = pe.transpose(Tb[it.use % 2][:, b * P:(b + 1) * P], e[:, it.buf, b * P:(b + 1) * P],
                                           ident[:])
                    ins.then_inc(t_full, 1)
                elif st.kind == "attend":
                    it = st.it
                    wait(turned(it.use))
                    wait(it.o_free)
                    pe.wait_ge(*it.vneed)
                    nk = it.n // P
                    O = Ob[it.o % 2]
                    for c in range(1 if it.kind == "diff" else 2):
                        for k in range(nk):
                            b = c * nk + k
                            wt = wT[:, it.buf, b * P:(b + 1) * P]
                            h = 2 * it.pair + c
                            dst = O[:, c * DH:(c + 1) * DH]
                            if it.kind == "diff":
                                val, dst = v[:, k, it.pair * P:(it.pair + 1) * P], O[:, 0:P]
                            elif it.kind == "mem":
                                val = memkv[:, 1, k * 256 + h * DH:k * 256 + (h + 1) * DH]
                            elif it.kind == "causal":
                                val = v[:, k, h * DH:(h + 1) * DH]
                            else:
                                val = v[:, k, 512:512 + DH]
                            ins = pe.matmul(dst, wt, val, start=k == 0, stop=k == nk - 1)
                    ins.then_inc(o_full, 1)
                elif st.kind == "mlp":
                    mlp_chunk(st, 0, 0, True)
                    with pe.Fori(1, CHUNKS - 2) as j:
                        mlp_chunk(st, j, 1, False)
                    mlp_chunk(st, CHUNKS - 2, CHUNKS - 2, False, last=True)
                elif st.kind == "index_scores":
                    wait_turned(st.use)
                    for b, (s, freed) in enumerate(st.banks):
                        wait(freed)
                        for i in range(st.per):
                            h = b * st.per + i
                            ins = pe.matmul(Sb[s % 2][:, i * st.n:(i + 1) * st.n], qk[:, INDEX_BLOCK[h], tok(st.t)],
                                            qk[:, Q_IK, 0:st.n], start=True, stop=True)
                        ins.then_inc(s_full, 1)
                elif st.kind == "shared_kv":
                    wait_turned(st.use)
                    s, freed = st.s
                    wait(freed)
                    for t in range(NT):
                        ins = pe.matmul(Sb[s % 2][:, tok(t)], qk[:, Q_C, tok(t)],
                                        wukv[:, :, :].rearrange("p a b -> p (a b)"), start=True, stop=True)
                    ins.then_inc(s_full, 1)
                elif st.kind == "retention_scores":
                    wait_turned(st.use)
                    for a, (s, freed) in enumerate(st.banks):
                        wait(freed)
                        n = TOK - a * P
                        for c in range(2):
                            ins = pe.matmul(Sb[s % 2][:, c * n:(c + 1) * n], headq[:, 4 + st.p, c, tok(a)],
                                            qk[:, Q_QB + st.p, a * P:TOK], start=True, stop=True)
                        ins.then_inc(s_full, 1)
                elif st.kind == "retention_out":
                    pe.wait_ge(*st.need)
                    pe.wait_ge(decayed, 2 * st.p + 2)
                    wait(st.o_free)
                    for t in range(NT):
                        for c in range(2):
                            h = 2 * st.p + c
                            for a in range(t + 1):
                                n = TOK - a * P
                                wt = rt[:, a, c * n + (t - a) * P:c * n + (t - a + 1) * P]
                                dst = Ob[st.o % 2][:, t * P + c * DH:t * P + (c + 1) * DH]
                                ins = pe.matmul(dst, wt, v[:, a, h * DH:(h + 1) * DH], start=a == 0, stop=a == t)
                    ins.then_inc(o_full, 1)
                elif st.kind == "ffn":
                    ffn_chunk(st, 0, 0, True)
                    with pe.Fori(1, FCHUNKS - 2) as j:
                        ffn_chunk(st, j, 1, False)
                    ffn_chunk(st, FCHUNKS - 2, FCHUNKS - 2, False, lambda: ffn_turns(st, FCHUNKS - 1))
                    wait_turned(st.t0 + 2 * FCHUNKS - 1)
                    u = st.base + 3 * FCHUNKS - 1
                    pe.wait_ge(lo_done, u + 1)
                    ffn_down(st, u, 2, False, True)

        @block.vector
        def _(dve):
            chain = [0]

            def behind(ins):
                chain[0] += 1
                ins.then_inc(dve_chain, 1)
                dve.wait_ge(dve_chain, chain[0])

            def split_lo(u, hi=None):
                if u >= N_UNITS:
                    return
                dve.wait_ge(hi_done, u + 1 if hi is None else hi)
                dve.tensor_tensor(shaped(wlo, u), shaped(raw, u), shaped(whi, u), ALU.subtract).then_inc(lo_done, 1)

            inverses = [0]

            def wait_inverse():
                inverses[0] += 1
                dve.wait_ge(inverse_done, inverses[0])

            def relu2(st, j, bank=Pb):
                for t in range(NT):
                    dve.wait_ge(relu_done, j * 2 + (st.relu0 + t + 1))
                    dve.tensor_tensor(hidden[:, t, :], hidden[:, t, :], bank[t][:], ALU.mult).then_inc(relu2_done, 1)

            def gated(st, j, bank=Pb):
                for t in range(NT):
                    dve.wait_ge(silu_done, j * 2 + (t + 1))
                    dve.tensor_tensor(hidden[:, t, 0:FCHUNK], zq[:, 1, t, 0:FCHUNK], bank[t][:, FCHUNK:2 * FCHUNK],
                                      ALU.mult).then_inc(relu2_done, 1)

            def hidden_lo(st, j, k0, per):
                for b in range(2):
                    dve.wait_ge(t_hi, j * 2 + (st.hi0 + b + 1))
                    ks = slice(k0 + per * b, k0 + per * b + per)
                    dve.tensor_tensor(set_lo[st.uset][:, ks, :], Tb[(st.t0 + b) % 2][:, 0:per * TOK]
                                      .rearrange("p (k n) -> p k n", k=per), set_hi[st.uset][:, ks, :],
                                      ALU.subtract).then_inc(t_evac[(st.t0 + b) % 2], 1)

            def mlp_chunk(st, j, peel, last=False):
                u0 = st.base + 2 + AHEAD + 4 * peel
                hi = lambda u: j * 4 + (u + 1 - 4 * peel)
                split_lo(u0, hi(u0))
                hidden_lo(st, j, UK, 2)
                split_lo(u0 + 1, hi(u0 + 1))
                relu2(st, j + 1)
                split_lo(u0 + 2, hi(u0 + 2))
                if last:
                    hidden_lo(st, j + 1, 0, 2)
                split_lo(u0 + 3, hi(u0 + 3))

            def ffn_chunk(st, j, peel):
                u0 = st.base + 2 + AHEAD + 3 * peel
                hi = lambda u: j * 3 + (u + 1 - 3 * peel)
                split_lo(u0, hi(u0))
                hidden_lo(st, j, 0, 1)
                split_lo(u0 + 1, hi(u0 + 1))
                gated(st, j + 1)
                split_lo(u0 + 2, hi(u0 + 2))

            bank_of = {"P": Pb, "S": Sb, "O": Ob}
            heads_view = lambda ap, n=8: ap.rearrange("p (h d) -> p h d", h=n)
            spread = lambda ap, n: ap.unsqueeze(2).broadcast_to([P, ap.shape[1], n])

            for st in STEPS:
                if st.kind == "setup":
                    dve.wait_ge(s_full, 1)
                    dve.tensor_copy(gcol[:, 0:FIRST * KT], Sb[gain_s[0] % 2][:, 0:FIRST * KT]).then_inc(gain_cols, 1)
                    dve.wait_ge(gain_cols, 1)
                elif st.kind == "constants":
                    dve.wait_ge(s_full, 2)
                    n = (len(GAINS) - FIRST) * KT
                    dve.tensor_copy(gcol[:, FIRST * KT:], Sb[gain_s[1] % 2][:, 0:n]).then_inc(gain_cols, 1)
                    dve.wait_ge(gain_cols, 2)
                    a, b = g_at("norm1_w_2"), g_at("final_norm")
                    dve.tensor_tensor(gcol[:, a:a + KT], gcol[:, a:a + KT], gcol[:, b:b + KT], ALU.mult)\
                       .then_inc(gain_cols, 1)
                    dve.wait_ge(gain_cols, 3)
                    lam = st.lam
                    dve.wait_ge(consts_landed, CONSTS)
                    behind(dve.tensor_tensor(lamprod, lamrow[:, :, 0, :], lamrow[:, :, 1, :], ALU.mult))
                    dve.tensor_reduce(lam[:, 0:2], lamprod, AX_X, ALU.add).then_inc(lam_sum, 1)
                    dve.tensor_scalar(subln[:], subln[:], 1.0 - LAM_INIT, None, ALU.mult)
                    behind(dve.tensor_tensor(qkn[:, 0, :], qkn[:, 0, :], qkn[:, 1, :], ALU.mult))
                    dve.wait_ge(s_full, bias_s[0] + 1)
                    dve.tensor_copy(biasvec, Sb[bias_s[0] % 2][0:8, :]).then_inc(bias_vec, 1)
                elif st.kind == "lambda":
                    dve.wait_ge(lam_exp, 1)
                    dve.scalar_tensor_tensor(out=lam[:, 4:5], in0=lam[:, 2:3], scalar=LAM_INIT, in1=lam[:, 3:4],
                                             op0=ALU.add, op1=ALU.subtract).then_inc(lam_done, 1)
                    dve.wait_ge(lam_done, 1)
                elif st.kind == "split":
                    split_lo(st.u)
                elif st.kind == "turn_operand":
                    for b in range(2):
                        n = st.use[b]
                        dve.wait_ge(t_hi, st.hi + b + 1)
                        for g, s, k0 in st.gains:
                            k = k0 + 2 * b
                            T = Tb[n % 2][:].rearrange("p (k n) -> p k n", k=2)
                            if g is None:
                                ins = dve.tensor_tensor(set_lo[s][:, k:k + 2, :], T, set_hi[s][:, k:k + 2, :],
                                                        ALU.subtract)
                            else:
                                for i in range(2):
                                    gi = g + UK * st.half + 2 * b + i
                                    ins = dve.scalar_tensor_tensor(
                                        out=set_lo[s][:, k + i, :], in0=T[:, i, :], scalar=gcol[:, gi:gi + 1],
                                        in1=set_hi[s][:, k + i, :], op0=ALU.mult, op1=ALU.subtract)
                        ins.then_inc(t_evac[n % 2], 1)
                elif st.kind == "statistics":
                    if st.what == "final":
                        dve.wait_ge(late_landed, 16)
                        dve.wait_ge(t_full, st.factor)
                        dve.wait_ge(rstd_done, st.n + 1)
                        for t in range(NT):
                            ins = dve.scalar_tensor_tensor(out=x[:, t, :], in0=x[:, t, :], scalar=st.rs[:, t:t + 1],
                                                           in1=fgb, op0=ALU.mult, op1=ALU.mult)
                        ins.then_inc(x_normed, 1)
                elif st.kind == "scores":
                    it = st.it
                    dve.wait_ge(s_full, it.s + 1)
                    S = Sb[it.s % 2][:, 0:2 * it.n].rearrange("p (c n) -> p c n", c=2)
                    behind(dve.tensor_reduce(it.nm, S, AX_X, ALU.max))
                    dve.tensor_scalar(it.nm, it.nm, -SCALE, None, ALU.mult)\
                       .then_inc(nmax_done, 1)
                elif st.kind == "mix":
                    it = st.it
                    dve.wait_ge(exp_done, it.exp + 1)
                    ins = dve.reciprocal(it.rs, it.rs)
                    if it.kind == "diff":
                        behind(ins)
                        behind(dve.tensor_tensor(it.rs[:, 1:2], it.rs[:, 1:2], lam[:, 4:5], ALU.mult))
                        e0, e1 = e[:, it.buf, 0:it.n], e[:, it.buf, it.n:2 * it.n]
                        behind(dve.tensor_scalar(e1, e1, it.rs[:, 1:2], None, ALU.mult))
                        ins = dve.scalar_tensor_tensor(out=e0, in0=e0, scalar=it.rs[:, 0:1], in1=e1,
                                                       op0=ALU.mult, op1=ALU.subtract)
                    ins.then_inc(w_done, 1)
                elif st.kind == "attend":
                    it = st.it
                    O = Ob[it.o % 2][:, 0:P]
                    at = it.pair * P + (SELF if it.kind == "mem" else 0)
                    dst = o_nat[:, it.t, at:at + P]
                    if it.kind != "diff":
                        dve.wait_ge(o_full, it.o + 1)
                        dve.wait_ge(w_done, it.w)
                        dve.tensor_tensor(heads_view(dst, 2), heads_view(O, 2), spread(it.rs, DH), ALU.mult)\
                           .then_inc(o_evac, 1)
                elif st.kind == "diff_norm":
                    wait_inverse()
                    for it in st.items:
                        dve.scalar_tensor_tensor(out=o_nat[:, it.t, it.pair * P:(it.pair + 1) * P],
                                                 in0=Ob[it.o % 2][:, 0:P], scalar=it.ors, in1=subln[:],
                                                 op0=ALU.mult, op1=ALU.mult).then_inc(o_evac, 1)
                elif st.kind == "residual":
                    if st.scale is not None:
                        dve.wait_ge(rstd_done, st.scale.n_done)
                    for t in range(NT):
                        dve.wait_ge(mul_done, 2 * st.u + t + 1)
                        xs = x[:, t, st.half * COLS:(st.half + 1) * COLS]
                        if st.scale is None:
                            ins = dve.tensor_tensor(xs, xs, bank_of[st.bank][t][:], ALU.add)
                        else:
                            ins = dve.scalar_tensor_tensor(out=xs, in0=bank_of[st.bank][t][:],
                                                           scalar=st.scale.rs[:, t:t + 1], in1=xs,
                                                           op0=ALU.mult, op1=ALU.add)
                        ins.then_inc(resid_done, 1)
                elif st.kind == "mlp":
                    relu2(st, 0, Ob)
                    mlp_chunk(st, 0, 0)
                    with dve.Fori(1, CHUNKS - 2) as j:
                        mlp_chunk(st, j, 1)
                    mlp_chunk(st, CHUNKS - 2, CHUNKS - 2, last=True)
                elif st.kind == "query_norm":
                    for t in range(NT):
                        dve.wait_ge(qsq_done, t + 1)
                        ins = dve.tensor_reduce(st.ss[:, 8 * t:8 * t + 8], heads_view(query_sq[:, t, :]), AX_X, ALU.add)
                    ins.then_inc(sum_done, 1)
                elif st.kind == "query_scale":
                    wait_inverse()
                    for t in range(NT):
                        z = heads_view(zq[:, 0, t, :])
                        dve.tensor_tensor(z, z, spread(st.st.rs[:, 8 * t:8 * t + 8], DH), ALU.mult).then_inc(qn_done, 1)
                elif st.kind == "small_norm":
                    for t in range(NT):
                        dve.wait_ge(chunk_evac, 2 * st.chunk + t + 1)
                        c = zs[:, t, 0:P]
                        ins = dve.tensor_tensor_reduce(sn[:, t, 2, :], c, c, 1.0, 0.0, ALU.mult, ALU.add,
                                                       st.ss[:, t:t + 1])
                    ins.then_inc(sum_done, 1)
                    for t in range(NT):
                        z = zs[:, t, :]
                        dve.tensor_copy(sn[:, t, 0, :], z[:, P:2 * P])
                        dve.tensor_copy(sn[:, t, 1, :].rearrange("p (r d) -> p r d", r=4),
                                        z[:, 2 * P:2 * P + 32].unsqueeze(1).broadcast_to([P, 4, 32]))
                    wait_inverse()
                    for t in range(NT):
                        dve.scalar_tensor_tensor(out=sn[:, t, 2, :], in0=zs[:, t, 0:P], scalar=st.rs[:, t:t + 1],
                                                 in1=kvn[:], op0=ALU.mult, op1=ALU.mult).then_inc(sn_done, 1)
                elif st.kind == "shared_key_sum":
                    dve.wait_ge(kava_done, 1)
                    for t in range(NT):
                        ka = sn[:, t, 1, 0:DH]
                        ins = dve.tensor_tensor_reduce(sn[:, t, 2, 0:DH], ka, ka, 1.0, 0.0, ALU.mult, ALU.add,
                                                       st.st.ss[:, t:t + 1])
                    ins.then_inc(sum_done, 1)
                elif st.kind == "shared_key_norm":
                    kv = st.st
                    wait_inverse()
                    for t in range(NT):
                        for c in range(2):
                            ins = dve.scalar_tensor_tensor(out=sn[:, t, 0, c * DH:(c + 1) * DH], in0=sn[:, t, 1, 0:DH],
                                                           scalar=kv.rs[:, t:t + 1], in1=qkn[:, 0, :],
                                                           op0=ALU.mult, op1=ALU.mult)
                        ins.then_inc(ka_done, 1)
                elif st.kind == "index_sum":
                    ix = st.st
                    t, n = ix.t, ix.n
                    behind(dve.tensor_scalar(ix.ind, zs[:, t, 2 * P + 32:SMALL], IDX_W_SCALE, None, ALU.mult))
                    dve.wait_ge(dots_done, ix.dots + len(ix.banks))
                    sc = score[t]
                    behind(dve.tensor_scalar(sc, relu_dots[:, 0, 0:n], ix.ind[:, 0:1], None, ALU.mult))
                    for h in range(1, 4):
                        ins = dve.scalar_tensor_tensor(out=sc, in0=relu_dots[:, h, 0:n], scalar=ix.ind[:, h:h + 1],
                                                       in1=sc, op0=ALU.mult, op1=ALU.add)
                        if h < 3:
                            behind(ins)
                    ins.then_inc(dots_used, 1)
                    dve.wait_ge(dots_used, t + 1)
                    behind(dve.memset(sc[0:DH, n - DH:n], BELOW))
                elif st.kind == "select":
                    ix = st.st
                    t, n = ix.t, ix.n
                    bufs = [score[t], work[:, 0:n]]
                    for r in range(*st.rounds):
                        behind(dve.max(ix.m8, bufs[r % 2]))
                        behind(dve.match_replace(bufs[1 - r % 2], ix.m8, bufs[r % 2], TAKEN))
                    if st.rounds[1] == TOPK // MAX8:
                        dve.tensor_scalar(selmask[:, t, 0:n], bufs[0], TAKEN, NEG, ALU.not_equal, ALU.mult)\
                           .then_inc(sel_done, 1)
                elif st.kind == "retention_scores":
                    for a, (s, _) in enumerate(st.banks):
                        dve.wait_ge(s_full, s + 1)
                        n = TOK - a * P
                        dve.wait_ge(*st.after)
                        for c in range(2):
                            h = 2 * st.p + c
                            o = c * n
                            dst, src = rt[:, a, o:o + n], Sb[s % 2][:, o:o + n]
                            ins = dve.scalar_tensor_tensor(out=dst[:, 0:P], in0=src[:, 0:P],
                                                           scalar=dec[:, a, 8 + h:9 + h], in1=tri[:], op0=ALU.mult,
                                                           op1=ALU.mult)
                            if n > P:
                                ins = dve.tensor_scalar(dst[:, P:n], src[:, P:n], dec[:, a, 8 + h:9 + h], None,
                                                        ALU.mult)
                        ins.then_inc(decayed, 1)
                elif st.kind == "retention_out":
                    dve.wait_ge(o_full, st.o + 1)
                    for t in range(NT):
                        at = 512 + st.p * P
                        ins = dve.tensor_tensor(heads_view(o_nat[:, t, at:at + P], 2),
                                                heads_view(Ob[st.o % 2][:, tok(t)], 2),
                                                spread(dec[:, t, 2 * st.p:2 * st.p + 2], DH), ALU.mult)
                    ins.then_inc(o_evac, 1)
                elif st.kind == "group_center":
                    dve.wait_ge(o_evac, st.o)
                    for t in range(NT):
                        y, mu = heads_view(o_nat[:, t, 512:1024]), st.mu[:, 8 * t:8 * t + 8]
                        behind(dve.tensor_reduce(mu, y, AX_X, ALU.add))
                        behind(dve.tensor_scalar(mu, mu, 1.0 / DH, None, ALU.mult))
                        dve.tensor_tensor(y, y, spread(mu, DH), ALU.subtract).then_inc(yc_done, 1)
                elif st.kind == "group_sum":
                    group = st.st
                    for t in range(NT):
                        dve.wait_ge(ysq_done, t + 1)
                        ins = dve.tensor_reduce(group.va[:, 8 * t:8 * t + 8], heads_view(rt[:, t, :]), AX_X, ALU.add)
                    ins.then_inc(sum_done, 1)
                elif st.kind == "group_scale":
                    group = st.st
                    wait_inverse()
                    for t in range(NT):
                        y = heads_view(o_nat[:, t, 512:1024])
                        dve.tensor_tensor(y, y, spread(group.rs[:, 8 * t:8 * t + 8], DH), ALU.mult).then_inc(yn_done, 1)
                elif st.kind == "group_gain":
                    y = o_nat[:, 1, 512:1024]
                    dve.wait_ge(yn_done, 2)
                    dve.wait_ge(gn_landed, 32)
                    behind(dve.tensor_tensor(y, y, gn[:, 0, :], ALU.mult))
                    behind(dve.tensor_tensor(y, y, gn[:, 1, :], ALU.add))
                elif st.kind == "group_gate":
                    y = o_nat[:, 1, 512:1024]
                    dve.wait_ge(*st.st.gate)
                    dve.tensor_tensor(y, y, zq[:, 1, 1, :], ALU.mult).then_inc(ob_done, 1)
                elif st.kind == "ffn":
                    gated(st, 0, Ob)
                    ffn_chunk(st, 0, 0)
                    with dve.Fori(1, FCHUNKS - 2) as j:
                        ffn_chunk(st, j, 1)
                    ffn_chunk(st, FCHUNKS - 2, FCHUNKS - 2)
                    hidden_lo(st, FCHUNKS - 1, 2, 1)
                elif st.kind == "store":
                    dve.wait_ge(rstd_done, st.rs.n_done)
                    for i, (c, t) in enumerate((c, t) for c in range(2) for t in range(NT)):
                        dve.wait_ge(mul_done, 2 * st.u + i + 1)
                        xs = x[:, t, c * COLS:(c + 1) * COLS]
                        dve.scalar_tensor_tensor(out=xs, in0=bank_of["SO"[c]][t][:], scalar=st.rs.rs[:, t:t + 1],
                                                 in1=xs, op0=ALU.mult, op1=ALU.add).then_inc(resid_done, 1)


def kernel(**inputs):
    import concourse.bacc as bacc
    from concourse.bass_utils import run_bass_kernel_spmd

    nc = bacc.Bacc("TRN2", target_bir_lowering=False, num_devices=1)
    arrays, aps = {}, {}
    for name, a in [*inputs.items(), *shape_tables().items()]:
        a = np.ascontiguousarray(a)
        arrays[f"in_{name}"] = a
        aps[name] = nc.dram_tensor(f"in_{name}", a.shape, mybir.dt.from_np(a.dtype), kind="ExternalInput").ap()
    out = nc.dram_tensor("out_0", (1, TOK, D), F32, kind="ExternalOutput").ap()
    build(nc, aps, out)
    return run_bass_kernel_spmd(nc, [arrays], core_ids=[0]).results[0]["out_0"]
```
